# Optimizing a Trainium2 kernel written in Bass

```python
import math
import jax, jax.numpy as jnp
from jax import lax
import numpy as np

D_MODEL = 2048
BATCH = 1
SEQ = 256
DEPTH = 1
DEC_BATCH = 8
DEC_SEQ = 1
PAST_LEN = 2048
PAGE_SIZE = 128

POOL_WINDOWS = (2, 4, 8, 16)
POOL_GROUPS = 4
POOL_DIM = D_MODEL
POOL_GC = POOL_DIM // POOL_GROUPS
POOL_BUF = 15
D_INNER = 2 * D_MODEL
SSD_HEAD_DIM = 64
SSD_HEADS = D_INNER // SSD_HEAD_DIM
SSD_GROUPS = 8
SSD_HPG = SSD_HEADS // SSD_GROUPS
D_STATE = 128
CONV_WIDTH = 4
CONV_DIM = D_INNER + 2 * SSD_GROUPS * D_STATE
SSD_CHUNK = 128
N_MEM = 256
MEM_HEADS = 4
MEM_HEAD_DIM = 128
MEM_DIM = MEM_HEADS * MEM_HEAD_DIM
D_FF = -(-8 * D_MODEL // (3 * 256)) * 256
IN_DIM = POOL_DIM + D_INNER + CONV_DIM + SSD_HEADS + 2 * D_MODEL
SPLIT_1 = POOL_DIM
SPLIT_2 = SPLIT_1 + D_INNER
SPLIT_3 = SPLIT_2 + CONV_DIM
SPLIT_4 = SPLIT_3 + SSD_HEADS
SPLIT_5 = SPLIT_4 + D_MODEL
ALPHA = (2 * DEPTH) ** 0.25
BETA = (8 * DEPTH) ** -0.25
LN_EPS = 1e-5
RMS_EPS = 1e-5

kernel_name = 'hybrid_pool_ssd_memory_decoder_step'

def layer_norm(x, g, b):
    xf = x.astype(jnp.float32)
    mu = jnp.mean(xf, axis=-1, keepdims=True)
    var = jnp.mean(jnp.square(xf - mu), axis=-1, keepdims=True)
    return ((xf - mu) * lax.rsqrt(var + LN_EPS) * g + b).astype(x.dtype)

def multiscale_pool(u, buf, start_pos):
    L = u.shape[1]
    cat = jnp.concatenate([buf.astype(u.dtype), u], axis=1)
    cs = jnp.cumsum(cat.astype(jnp.float32), axis=1)
    cs0 = jnp.pad(cs, ((0, 0), (1, 0), (0, 0)))
    pos = start_pos + jnp.arange(L)
    outs = []
    for g, w in enumerate(POOL_WINDOWS):
        sl = slice(g * POOL_GC, (g + 1) * POOL_GC)
        hi = cs0[:, POOL_BUF + 1:POOL_BUF + 1 + L, sl]
        lo = cs0[:, POOL_BUF + 1 - w:POOL_BUF + 1 - w + L, sl]
        cnt = jnp.minimum(w, pos + 1).astype(jnp.float32)
        outs.append((hi - lo) / cnt[None, :, None])
    pooled = jnp.concatenate(outs, axis=-1) - u.astype(jnp.float32)
    return pooled, cat[:, -POOL_BUF:]

def causal_conv(xbc, buf, w, bias):
    L = xbc.shape[1]
    cat = jnp.concatenate([buf.astype(xbc.dtype), xbc], axis=1)
    out = bias.astype(jnp.float32)
    for k in range(CONV_WIDTH):
        out = out + cat[:, k:k + L].astype(jnp.float32) * w[k].astype(jnp.float32)
    return jax.nn.silu(out), cat[:, -(CONV_WIDTH - 1):]

def ssd_chunked(xh, dt, a, bm, cm, state0):
    b, L = xh.shape[0], xh.shape[1]
    c = min(SSD_CHUNK, L)
    nc = -(-L // c)
    pad = nc * c - L
    if pad:
        xh = jnp.pad(xh, ((0, 0), (0, pad), (0, 0), (0, 0)))
        dt = jnp.pad(dt, ((0, 0), (0, pad), (0, 0)))
        bm = jnp.pad(bm, ((0, 0), (0, pad), (0, 0), (0, 0)))
        cm = jnp.pad(cm, ((0, 0), (0, pad), (0, 0), (0, 0)))
    Lp = nc * c
    dA = (dt * a).reshape(b, Lp, SSD_GROUPS, SSD_HPG)
    xdt = (xh * dt[..., None]).reshape(b, Lp, SSD_GROUPS, SSD_HPG, SSD_HEAD_DIM)

    def to_chunks(t):
        return jnp.moveaxis(t.reshape((b, nc, c) + t.shape[2:]), 1, 0)

    causal = jnp.tril(jnp.ones((c, c), dtype=bool))[None, :, :, None, None]

    def step(state, inp):
        xdt_k, dA_k, b_k, c_k = inp
        cum = jnp.cumsum(dA_k, axis=1)
        seg = cum[:, :, None] - cum[:, None, :]
        decay = jnp.where(causal, jnp.exp(jnp.where(causal, seg, 0.0)), 0.0)
        cb = jnp.einsum('blgn,bsgn->blsg', c_k, b_k)
        y_diag = jnp.einsum('blsg,blsgh,bsghp->blghp', cb, decay, xdt_k)
        y_off = jnp.einsum('blgn,bghpn->blghp', c_k, state) * jnp.exp(cum)[..., None]
        last = cum[:, -1]
        w_s = jnp.exp(last[:, None] - cum)
        new_state = state * jnp.exp(last)[..., None, None] + jnp.einsum('bsgn,bsgh,bsghp->bghpn', b_k, w_s, xdt_k)
        return new_state, y_diag + y_off

    state_g = state0.reshape(b, SSD_GROUPS, SSD_HPG, SSD_HEAD_DIM, D_STATE)
    state_g, y = lax.scan(step, state_g, (to_chunks(xdt), to_chunks(dA), to_chunks(bm), to_chunks(cm)))
    y = jnp.moveaxis(y, 0, 1).reshape(b, Lp, SSD_HEADS, SSD_HEAD_DIM)[:, :L]
    return y, state_g.reshape(b, SSD_HEADS, SSD_HEAD_DIM, D_STATE)

def token_mixer(h, lp, pool_buf, conv_buf, ssd_state, start_pos):
    b, L, _ = h.shape
    proj = jnp.einsum('bld,dk->blk', h, lp['w_in'])
    u, z, xbc, dt_raw, g_pool, g_ssd = jnp.split(proj, [SPLIT_1, SPLIT_2, SPLIT_3, SPLIT_4, SPLIT_5], axis=-1)
    pooled, new_pool_buf = multiscale_pool(u, pool_buf, start_pos)
    pooled = jnp.einsum('blgc,gcd->blgd', pooled.reshape(b, L, POOL_GROUPS, POOL_GC).astype(h.dtype), lp['w_pool'])
    pooled = pooled.reshape(b, L, POOL_DIM) * lp['pool_scale']
    branch_a = jnp.einsum('blc,cd->bld', pooled.astype(h.dtype), lp['w_pool_br'])
    xbc, new_conv_buf = causal_conv(xbc, conv_buf, lp['conv_w'], lp['conv_b'])
    xs, bm, cm = jnp.split(xbc, [D_INNER, D_INNER + SSD_GROUPS * D_STATE], axis=-1)
    xh = xs.reshape(b, L, SSD_HEADS, SSD_HEAD_DIM)
    dt = jax.nn.softplus(dt_raw.astype(jnp.float32) + lp['dt_bias'].astype(jnp.float32))
    a = -jnp.exp(lp['a_log'].astype(jnp.float32))
    y, new_state = ssd_chunked(xh, dt, a,
                               bm.reshape(b, L, SSD_GROUPS, D_STATE), cm.reshape(b, L, SSD_GROUPS, D_STATE),
                               ssd_state.astype(jnp.float32))
    y = y + lp['d_skip'].astype(jnp.float32)[:, None] * xh
    y = y.reshape(b, L, D_INNER) * jax.nn.silu(z.astype(jnp.float32))
    yg = y.reshape(b, L, SSD_GROUPS, D_INNER // SSD_GROUPS)
    yg = yg * lax.rsqrt(jnp.mean(jnp.square(yg), axis=-1, keepdims=True) + RMS_EPS)
    y = yg.reshape(b, L, D_INNER) * lp['ssd_norm_w']
    branch_b = jnp.einsum('blc,cd->bld', y.astype(h.dtype), lp['w_ssd_br'])
    merged = jax.nn.sigmoid(g_pool) * branch_a + jax.nn.sigmoid(g_ssd) * branch_b
    out = jnp.einsum('bld,de->ble', merged.astype(h.dtype), lp['w_out'])
    return out, new_pool_buf, new_conv_buf, new_state

def memory_attention(h, mk, mv, w_mq, w_mo):
    b, L, _ = h.shape
    q = jnp.einsum('bld,dk->blk', h, w_mq).reshape(b, L, MEM_HEADS, MEM_HEAD_DIM)
    s = jnp.einsum('blhd,bmhd->bhlm', q.astype(jnp.float32), mk.astype(jnp.float32)) / math.sqrt(MEM_HEAD_DIM)
    p = jax.nn.softmax(s, axis=-1)
    o = jnp.einsum('bhlm,bmhd->blhd', p, mv.astype(jnp.float32)).reshape(b, L, MEM_DIM)
    return jnp.einsum('blk,kd->bld', o.astype(h.dtype), w_mo)

def swiglu(h, w_gate, w_up, w_down):
    g = jnp.einsum('bld,df->blf', h, w_gate)
    u = jnp.einsum('bld,df->blf', h, w_up)
    return jnp.einsum('blf,fd->bld', jax.nn.silu(g) * u, w_down)

def decoder_layer(x, mk, mv, pool_buf, conv_buf, ssd_state, start_pos, lp):
    mix, new_pool_buf, new_conv_buf, new_state = token_mixer(x, lp, pool_buf, conv_buf, ssd_state, start_pos)
    x = layer_norm(ALPHA * x + mix, lp['ln_mix_g'], lp['ln_mix_b'])
    ca = memory_attention(x, mk, mv, lp['w_mq'], lp['w_mo'])
    x = layer_norm(ALPHA * x + ca, lp['ln_mem_g'], lp['ln_mem_b'])
    f = swiglu(x, lp['w_ffn_gate'], lp['w_ffn_up'], lp['w_ffn_down'])
    x = layer_norm(ALPHA * x + f, lp['ln_ffn_g'], lp['ln_ffn_b'])
    return x, new_pool_buf, new_conv_buf, new_state

def setup_inputs(seed: int = 0) -> dict:
    key = jax.random.key(seed)
    k = jax.random.split(key, 40)
    f32 = jnp.float32

    def nrm(kk, shape, scale):
        return scale * jax.random.normal(kk, shape, f32)

    dt0 = jnp.exp(jax.random.uniform(k[10], (DEPTH, SSD_HEADS), f32, math.log(1e-3), math.log(1e-1)))
    return {
        'x_prompt': nrm(k[0], (BATCH, SEQ, D_MODEL), 1.0),
        'x_sample': nrm(k[1], (DEC_BATCH, DEC_SEQ, D_MODEL), 1.0),
        'mem_prompt': nrm(k[2], (BATCH, N_MEM, D_MODEL), 1.0),
        'state_ssd': nrm(k[3], (DEPTH, DEC_BATCH, SSD_HEADS, SSD_HEAD_DIM, D_STATE), 0.1),
        'state_conv': nrm(k[4], (DEPTH, DEC_BATCH, CONV_WIDTH - 1, CONV_DIM), 1.0),
        'state_pool': nrm(k[5], (DEPTH, DEC_BATCH, POOL_BUF, POOL_DIM), 1.0),
        'cache_mem_k': nrm(k[6], (DEPTH, DEC_BATCH, N_MEM, MEM_HEADS, MEM_HEAD_DIM), 1.0),
        'cache_mem_v': nrm(k[7], (DEPTH, DEC_BATCH, N_MEM, MEM_HEADS, MEM_HEAD_DIM), 1.0),
        'w_in': nrm(k[8], (DEPTH, D_MODEL, IN_DIM), D_MODEL ** -0.5),
        'w_pool': nrm(k[9], (DEPTH, POOL_GROUPS, POOL_GC, POOL_GC), POOL_GC ** -0.5),
        'pool_scale': 1.0 + nrm(k[11], (DEPTH, POOL_DIM), 0.1),
        'w_pool_br': nrm(k[12], (DEPTH, POOL_DIM, D_MODEL), BETA * POOL_DIM ** -0.5),
        'conv_w': nrm(k[13], (DEPTH, CONV_WIDTH, CONV_DIM), CONV_WIDTH ** -0.5),
        'conv_b': nrm(k[14], (DEPTH, CONV_DIM), 0.02),
        'dt_bias': dt0 + jnp.log(-jnp.expm1(-dt0)),
        'a_log': jnp.log(jax.random.uniform(k[15], (DEPTH, SSD_HEADS), f32, 1.0, 16.0)),
        'd_skip': 1.0 + nrm(k[16], (DEPTH, SSD_HEADS), 0.1),
        'ssd_norm_w': 1.0 + nrm(k[17], (DEPTH, D_INNER), 0.02),
        'w_ssd_br': nrm(k[18], (DEPTH, D_INNER, D_MODEL), BETA * D_INNER ** -0.5),
        'w_out': nrm(k[19], (DEPTH, D_MODEL, D_MODEL), BETA * D_MODEL ** -0.5),
        'ln_mix_g': 1.0 + nrm(k[20], (DEPTH, D_MODEL), 0.02),
        'ln_mix_b': nrm(k[21], (DEPTH, D_MODEL), 0.02),
        'w_mq': nrm(k[22], (DEPTH, D_MODEL, MEM_DIM), D_MODEL ** -0.5),
        'w_mk': nrm(k[23], (DEPTH, D_MODEL, MEM_DIM), D_MODEL ** -0.5),
        'w_mv': nrm(k[24], (DEPTH, D_MODEL, MEM_DIM), BETA * D_MODEL ** -0.5),
        'w_mo': nrm(k[25], (DEPTH, MEM_DIM, D_MODEL), BETA * MEM_DIM ** -0.5),
        'ln_mem_g': 1.0 + nrm(k[26], (DEPTH, D_MODEL), 0.02),
        'ln_mem_b': nrm(k[27], (DEPTH, D_MODEL), 0.02),
        'w_ffn_gate': nrm(k[28], (DEPTH, D_MODEL, D_FF), D_MODEL ** -0.5),
        'w_ffn_up': nrm(k[29], (DEPTH, D_MODEL, D_FF), BETA * D_MODEL ** -0.5),
        'w_ffn_down': nrm(k[30], (DEPTH, D_FF, D_MODEL), BETA * D_FF ** -0.5),
        'ln_ffn_g': 1.0 + nrm(k[31], (DEPTH, D_MODEL), 0.02),
        'ln_ffn_b': nrm(k[32], (DEPTH, D_MODEL), 0.02),
    }

def reference(x_prompt, x_sample, mem_prompt, state_ssd, state_conv, state_pool, cache_mem_k, cache_mem_v,
              w_in, w_pool, pool_scale, w_pool_br, conv_w, conv_b, dt_bias, a_log, d_skip, ssd_norm_w,
              w_ssd_br, w_out, ln_mix_g, ln_mix_b, w_mq, w_mk, w_mv, w_mo, ln_mem_g, ln_mem_b,
              w_ffn_gate, w_ffn_up, w_ffn_down, ln_ffn_g, ln_ffn_b):
    bp = x_prompt.shape[0]
    xp, xs = x_prompt, x_sample
    ssd_p, conv_p, pool_p, mk_list, mv_list = [], [], [], [], []
    ssd_s, conv_s, pool_s = [], [], []
    for l in range(DEPTH):
        lp = {
            'w_in': w_in[l], 'w_pool': w_pool[l], 'pool_scale': pool_scale[l], 'w_pool_br': w_pool_br[l],
            'conv_w': conv_w[l], 'conv_b': conv_b[l], 'dt_bias': dt_bias[l], 'a_log': a_log[l],
            'd_skip': d_skip[l], 'ssd_norm_w': ssd_norm_w[l], 'w_ssd_br': w_ssd_br[l], 'w_out': w_out[l],
            'ln_mix_g': ln_mix_g[l], 'ln_mix_b': ln_mix_b[l], 'w_mq': w_mq[l], 'w_mo': w_mo[l],
            'ln_mem_g': ln_mem_g[l], 'ln_mem_b': ln_mem_b[l], 'w_ffn_gate': w_ffn_gate[l],
            'w_ffn_up': w_ffn_up[l], 'w_ffn_down': w_ffn_down[l], 'ln_ffn_g': ln_ffn_g[l], 'ln_ffn_b': ln_ffn_b[l],
        }
        mk_p = jnp.einsum('bmd,dk->bmk', mem_prompt, w_mk[l]).reshape(bp, N_MEM, MEM_HEADS, MEM_HEAD_DIM)
        mv_p = jnp.einsum('bmd,dk->bmk', mem_prompt, w_mv[l]).reshape(bp, N_MEM, MEM_HEADS, MEM_HEAD_DIM)
        zero_pool = jnp.zeros((bp, POOL_BUF, POOL_DIM), x_prompt.dtype)
        zero_conv = jnp.zeros((bp, CONV_WIDTH - 1, CONV_DIM), x_prompt.dtype)
        zero_ssd = jnp.zeros((bp, SSD_HEADS, SSD_HEAD_DIM, D_STATE), jnp.float32)
        xp, pb, cb, st = decoder_layer(xp, mk_p, mv_p, zero_pool, zero_conv, zero_ssd, 0, lp)
        ssd_p.append(st.astype(x_prompt.dtype))
        conv_p.append(cb)
        pool_p.append(pb)
        mk_list.append(mk_p)
        mv_list.append(mv_p)
        xs, pb, cb, st = decoder_layer(xs, cache_mem_k[l], cache_mem_v[l], state_pool[l], state_conv[l],
                                       state_ssd[l], PAST_LEN, lp)
        ssd_s.append(st.astype(state_ssd.dtype))
        conv_s.append(cb)
        pool_s.append(pb)
    new_ssd_prompt = jnp.stack(ssd_p)
    new_conv_prompt = jnp.stack(conv_p)
    new_pool_prompt = jnp.stack(pool_p)
    new_mem_k_prompt = jnp.stack(mk_list)
    new_mem_v_prompt = jnp.stack(mv_list)
    new_ssd_sample = jnp.stack(ssd_s)
    new_conv_sample = jnp.stack(conv_s)
    new_pool_sample = jnp.stack(pool_s)
    return (xp, xs, new_ssd_prompt, new_conv_prompt, new_pool_prompt, new_mem_k_prompt, new_mem_v_prompt,
            new_ssd_sample, new_conv_sample, new_pool_sample)


_drawn_inputs = setup_inputs


def setup_inputs(seed=0):
    import zlib

    import numpy as np

    out = dict(_drawn_inputs(seed))
    spreads = {}
    factors = {'pool_scale': 4.079,
     'd_skip': 4.479,
     'ssd_norm_w': 8.0,
     'ln_mix_g': 2.818,
     'ln_mix_b': 2.727,
     'ln_mem_g': 2.799,
     'ln_mem_b': 2.788,
     'ln_ffn_g': 2.855,
     'ln_ffn_b': 2.748}
    for name, (base, spread) in spreads.items():
        noise = np.random.default_rng([zlib.crc32(name.encode()), seed]).standard_normal(out[name].shape)
        drawn = base * np.exp(spread * noise) if base else spread * noise
        out[name] = __import__('jax').numpy.asarray(drawn.astype(out[name].dtype))
    for name, factor in factors.items():
        out[name] = (out[name] * factor).astype(out[name].dtype)
    return out
```

```python
from contextlib import ExitStack, contextmanager
import math

import numpy as np

import concourse.bass as bass
from concourse import mybir

F32 = mybir.dt.float32
F32R = mybir.dt.float32r
ALU = mybir.AluOpType
ACT = mybir.ActivationFunctionType
AX_X = mybir.AxisListType.X

P = 128
D_MODEL = 2048
SEQ = 256
NSAMP = 8
T = SEQ + NSAMP
KT = D_MODEL // P
WINDOWS = (2, 4, 8, 16)
POOL_HIST = 15
GROUPS = 8
HPG = 8
HEADS = 64
D_INNER = 4096
D_STATE = 128
CONV_W = 4
CONV_DIM = D_INNER + 2 * GROUPS * D_STATE
CT = CONV_DIM // P
CPG = CT // GROUPS
XPG = 4
YT = D_INNER // P
N_MEM = 256
MH = 4
MHD = 128
MEM_DIM = MH * MHD
D_FF = -(-8 * D_MODEL // (3 * 256)) * 256
FT = D_FF // P
ALPHA = 2 ** 0.25
LN_EPS = 1e-5
RMS_EPS = 1e-5
RING = 4
UNIT = 1024
BLK = 256

VECS = [("conv_w", CT * CONV_W), ("conv_b", CT), ("norm_w", YT), ("d_skip", YT), ("pool_scale", KT),
        ("ln_mix_g", KT), ("ln_mix_b", KT), ("ln_mem_g", KT), ("ln_mem_b", KT),
        ("ln_ffn_g", KT), ("ln_ffn_b", KT)]
VEC_AT, _at = {}, 0
for _name, _n in VECS:
    VEC_AT[_name] = _at
    _at += _n
NVEC = _at

U_BCX = 3 * 4
U_Z = 2 * 4
U_UP = 8 * 4
U_POOL = 4 * 2
U_BRA = 8 * 8
U_BRB = 8 * 12
U_OUT = 8 * 4
U_MEM = 4 * 4
U_Q = 2 * 4
U_MO = 8
U_F1 = (FT // 2) * 8
U_F2 = 8 * (FT // 4)
N_MISC = 9
START = {"sgm": 1, "br_read": 1, "h_read": 1, "h_hi": 1, "seg_ready": 1, "res_ready": 3,
         "outer_free": 1}
STEPS = 28
N_UNITS = GROUPS * (U_BCX + U_Z) + U_UP + U_POOL + U_BRA + U_BRB + U_OUT + U_MEM + U_Q + U_MO + U_F1 + U_F2


class Tally:

    def __init__(self):
        self.base, self.k, self.per, self.reg = 0, 0, 0, None

    def add(self, n=1):
        self.k += n
        return self.now()

    def now(self, less=0):
        v = self.base + self.k - less
        return v if self.reg is None else self.reg * self.per + v


class Tallies(dict):
    def __missing__(self, name):
        self[name] = Tally()
        return self[name]


@contextmanager
def rounds(eng, n, tallies, per):
    with eng.Fori(0, n) as i:
        frozen = {}
        for name, p in per.items():
            t = tallies[name]
            t.base, t.k, t.per, t.reg = t.base + t.k, 0, p, i
        for name, t in tallies.items():
            if name not in per:
                frozen[name] = t.k
        yield i
        for name, p in per.items():
            assert tallies[name].k == p, (name, tallies[name].k, p)
        for name, t in tallies.items():
            assert name in per or t.k == frozen.get(name, 0), (name, t.k)
    for name, p in per.items():
        t = tallies[name]
        t.base, t.k, t.reg = t.base + n * p, 0, None


def flat(ap):
    return ap.rearrange("p a b -> p (a b)")


def build(nc, a, o):
    ctx = ExitStack()
    with ctx:
        def sem(name):
            return ctx.enter_context(nc.semaphore(name))

        def alloc(stack, name, shape, dt=F32):
            return stack.enter_context(nc.sbuf_tensor("sb_" + name, shape, dt))

        def overlay(skip, **tensors):
            out = []
            with ExitStack() as s:
                if skip:
                    alloc(s, f"skip_{next(iter(tensors))}", [P, skip // 4])
                for name, (shape, *dt) in tensors.items():
                    out.append(alloc(s, name, shape, *dt))
            return out

        raw = alloc(ctx, "raw", [P, RING, UNIT])
        whi = alloc(ctx, "whi", [P, RING, UNIT], F32R)
        wlo = alloc(ctx, "wlo", [P, RING, UNIT], F32R)
        xH = alloc(ctx, "xH", [P, KT, T], F32R)
        xL = alloc(ctx, "xL", [P, KT, T], F32R)
        resid = alloc(ctx, "resid", [P, KT, T])
        ident = alloc(ctx, "ident", [P, P])
        ones = alloc(ctx, "ones", [P, P])
        vec = alloc(ctx, "vec", [P, NVEC])
        rc = alloc(ctx, "rc", [P, 4, 16])
        phs = alloc(ctx, "phs", [P, KT, NSAMP])
        eps = alloc(ctx, "eps", [P, 2])

        def vcol(name, i, n=1):
            if isinstance(i, int):
                return vec[:, VEC_AT[name] + i:VEC_AT[name] + i + n]
            return vec[:, bass.ds(i + VEC_AT[name], n)]

        G = [[ctx.enter_context(nc.psum_tensor(f"G{s}{j}", [P, 512], F32)) for j in range(2)] for s in range(2)]
        M = [ctx.enter_context(nc.psum_tensor(f"M{j}", [P, 512], F32)) for j in range(4)]
        SETS = [G[0], G[1], [M[2], M[3]]]

        YB = 2 * YT * T * 4
        yH, yL = overlay(0, yH=([P, YT, T], F32R), yL=([P, YT, T], F32R))
        (zs, cumbc, bcb, xdt, BT, CTt, cbm, cmask, E, MM, Btok, bcs, outer, R, cacc, dttok, ncum, wtok,
         dts, dtx, ysamp, chist, tails) = overlay(
            YB, zs=([P, XPG, T],), cumbc=([P, HPG, SEQ],), bcb=([P, 2, 2, 2 * P],), xdt=([P, 2, HPG * 64],),
            BT=([P, T],), CTt=([P, T],), cbm=([P, 384],), cmask=([P, 384],), E=([P, 2, 384],),
            MM=([P, 3, 384],), Btok=([P, 2, P],), bcs=([NSAMP, 2 * P],), outer=([P, 4, P],),
            R=([P, 2, CONV_W - 1 + T],), cacc=([P, 2, T],), dttok=([P, 2, HEADS],), ncum=([P, 2, HEADS],),
            wtok=([P, 2, HEADS],), dts=([P, YT, 2 * NSAMP],), dtx=([P, XPG, NSAMP],),
            ysamp=([P, XPG, NSAMP],), chist=([P, CT, NSAMP],), tails=([P, CT, 11],))
        rstd = E[:, 0, 0:T]
        xs = resid[:, 0:XPG, :]
        yg = resid[:, XPG:2 * XPG, :]
        st = resid[:, 8:16, :].rearrange("p a b -> p (a b)")[:, 0:2048].rearrange(
            "p (s b i n) -> p s b i n", s=2, b=2, i=XPG)
        wdt, hist, hpool, S, dAtok, pcol, pxs, ctmp = overlay(
            0, wdt=([P, KT, HEADS],), hist=([P, CT, NSAMP * 3],), hpool=([P, KT, NSAMP, POOL_HIST],),
            S=([HEADS, 8, T],), dAtok=([P, 2, HEADS],), pcol=([HEADS, 4],), pxs=([HEADS, 2 * NSAMP],),
            ctmp=([P, CT, NSAMP],))
        mixH, mixL, U, V, tmp, utail, sgA = overlay(
            YB, mixH=([P, KT, T], F32R), mixL=([P, KT, T], F32R), U=([P, POOL_HIST + T],),
            V=([P, 2, POOL_HIST + T],), tmp=([P, 2, T],), utail=([P, KT, 23],), sgA=([P, 2, T],))
        sq, KTm, Vn, mean, lrstd, memH, memL, memraw = overlay(
            0, sq=([P, 2, 4 * T],), KTm=([P, MH, N_MEM],), Vn=([P, 2, MEM_DIM],), mean=([P, T],),
            lrstd=([P, T],), memH=([P, KT, N_MEM], F32R), memL=([P, KT, N_MEM], F32R),
            memraw=([P, 2, 4 * N_MEM],))
        ATT = (2 * 4 * T + 2 * MH * N_MEM + 2 * T) * 4
        (kc, vc, qT, Pe, PT, oT, ssT, sP, sPT, smx, snm, srs, sri, oH, oL) = overlay(
            ATT, kc=([P, NSAMP, MH, N_MEM],), vc=([P, NSAMP, 2, MEM_DIM],), qT=([P, MH, T],),
            Pe=([P, 2 * MH, N_MEM],), PT=([P, 2, 512],), oT=([P, MH, T],), ssT=([P, 2, 32],),
            sP=([32, N_MEM],), sPT=([P, 2, 32],), smx=([P, 9],), snm=([P, 9],), srs=([P, 9],),
            sri=([P, 9],), oH=([P, MH, T], F32R), oL=([P, MH, T], F32R))
        sq2, mean2, lrstd2, hH, hL, hf, sgF = overlay(
            0, sq2=([P, 2, 4 * T],), mean2=([P, T],), lrstd2=([P, T],), hH=([P, FT, T], F32R),
            hL=([P, FT, T], F32R), hf=([P, 2, T],), sgF=([P, 2, T],))

        scr_cum = nc.dram_tensor("scr_cum", (HEADS, SEQ), F32, kind="Internal").ap()
        scr_dts = nc.dram_tensor("scr_dts", (HEADS, 2 * NSAMP), F32, kind="Internal").ap()
        scr_bc = nc.dram_tensor("scr_bc", (NSAMP, 2 * P), F32, kind="Internal").ap()

        landed = [sem(f"landed{k}") for k in range(RING)]
        hi_ready, lo_ready, used = sem("hi_ready"), sem("lo_ready"), sem("used")
        in_x, in_misc = sem("in_x"), sem("in_misc")
        act_step, dve_step = sem("act_step"), sem("dve_step")
        s = {n: sem(n) for n in (
            "outer_free pool_past seg_ready w_sum y2_ready bc_used kv_out tails_out x_hi x_lo dt_psum dt_z dt_abs dt_exp dt_u dt_ln dt_ready dA_tok_ps dA_tok cum_ps cum_sb cumt_ps "
            "pre_exp pre_done scr_out dts_in ones_set "
            "raw_ready conv_done xbc_ready xtok_ps btok_ps btok_sb bc_rows cb_ps xdt_ready e_ready m_ready "
            "y_done xw_ready st_ps fst_ready z_ready dtx_ready out_ready st_done sq_ready rms_ps sd_ready "
            "y3_ready yh_ready yl_ready cum_in bc_out bc_in0 bc_in1 st_in0 st_in1 st_out0 st_out1 fst_out "
            "uraw pool_f mix_hi mix_lo wp_ready sgm br_read res_ready res_part "
            "ln_sum mean_ready cen_ready sqc_ready sqc_used  lsd_ready nrm_ready xn_ready "
            "mem_in0 mem_in1 mem_hi mem_lo kt_ready vn_ready kv_in q_ready sc_ps mx_ready p_ready pn_ready "
            "pt_ps pt_ready o_ps o_f o_hi o_lo ss_ps ss_sb sst_ps sp_exp sp_n spt_ps spt_sb so_ps "
            "h_read h_hi h_lo outs").split()}
        block = ctx.enter_context(nc.Block())

        @block.sync
        def _(sp):
            sp.dma_start(flat(resid[:, :, :]), a["xT"]).then_inc(in_x, 16)
            with sp.Fori(0, N_UNITS // RING) as i:
                for k in range(RING):
                    sp.wait_ge(lo_ready, i * RING + (k + 1))
                    sp.dma_start(raw[:, k, :], a["wstream"][bass.ds(i * RING + k, 1), :, :].rearrange(
                        "u p c -> (u p) c")).then_inc(landed[k], 16)

        @block.tensor
        def _(pe):
            t = Tallies()
            pe.sem_inc(used, RING)
            for name, value in START.items():
                pe.sem_inc(s[name], value)

            def mm3(slot, col, kH, kL, out, start, stop):
                w = whi[:, slot, col:col + P]
                pe.matmul(out, w, kH, start=start, stop=False)
                pe.matmul(out, w, kL, start=False, stop=False)
                return pe.matmul(out, wlo[:, slot, col:col + P], kH, start=False, stop=stop)

            def unit(plan):
                u = t["unit"]
                assert u.base % RING == 0 and (u.reg is None or u.per % RING == 0)
                slot = u.k % RING
                pe.wait_ge(lo_ready, u.add() + RING)
                for p in plan:
                    last = mm3(slot, *p)
                last.then_inc(used, 1)

            def block_units(H, L, kts, out, n=T, between=None, before=None):
                for q in range(0, kts, 4):
                    if before:
                        before(q // 4)
                    unit([(kk * BLK + j * P, H[:, q + kk, 0:n], L[:, q + kk, 0:n], out[j][:, 0:n],
                           q + kk == 0, q + kk == kts - 1) for kk in range(4) for j in range(2)])
                    if between:
                        between(q // 4)

            def bc_units(out):
                for j in range(2):
                    for q in (0, 8):
                        unit([(kk * P, xH[:, q + kk, :], xL[:, q + kk, :], out[j][:, 0:T],
                               q + kk == 0, q + kk == KT - 1) for kk in range(8)])

            pe.wait_ge(in_x, 16)
            pe.wait_ge(in_misc, N_MISC * 16)
            for k in range(KT):
                last = pe.matmul(M[0][0:HEADS, 0:T], wdt[:, k, :], resid[:, k, :], start=k == 0, stop=k == KT - 1)
            last.then_inc(s["dt_psum"], 1)

            def decay_setup():
                pe.wait_ge(s["dt_ready"], 1)
                for b in range(2):
                    pe.transpose(M[1][:, b * 64:b * 64 + 64], S[:, 0, b * P:b * P + P], ident[0:HEADS, 0:HEADS])
                for b in range(2):
                    last = pe.transpose(M[2][:, b * 64:b * 64 + 64], S[:, 7, b * P:b * P + P], ident[0:HEADS, 0:HEADS])
                last.then_inc(s["dA_tok_ps"], 1)
                pe.wait_ge(s["dA_tok"], 2)
                pe.wait_ge(s["ones_set"], 1)
                pe.matmul(M[3][0:HEADS, 0:SEQ], dAtok[:, 0, :], cmask[:, 0:SEQ], start=True, stop=False)
                pe.matmul(M[3][0:HEADS, P:SEQ], dAtok[:, 1, :], cmask[:, SEQ:384], start=False, stop=True)
                for b in range(2):
                    last = pe.matmul(M[0][:, 0:HEADS], ones[:, :], dAtok[:, b, :], start=b == 0, stop=b == 1)
                last.then_inc(s["cum_ps"], 1)
                pe.wait_ge(s["cum_sb"], 1)
                for b in range(2):
                    last = pe.transpose(M[1][:, b * 64:b * 64 + 64], S[:, 1, b * P:b * P + P], ident[0:HEADS, 0:HEADS])
                last.then_inc(s["cumt_ps"], 1)

            def token_major():
                pe.wait_ge(s["xbc_ready"], t["xbc"].add(CPG))
                for b in range(2):
                    for j in range(XPG):
                        last = pe.transpose(M[b][:, j * P:j * P + P], xs[:, j, b * P:b * P + P], ident[:, :])
                last.then_inc(s["xtok_ps"], 1)
                for b in range(2):
                    pe.transpose(M[2][:, b * P:b * P + P], BT[:, b * P:b * P + P], ident[:, :])
                pe.transpose(M[2][0:NSAMP, 256:384], BT[:, SEQ:T], ident[:, :])
                pe.transpose(M[2][0:NSAMP, 384:512], CTt[:, SEQ:T], ident[:, :]).then_inc(s["btok_ps"], 1)
                pe.matmul(M[3][:, 0:SEQ], BT[:, 0:P], CTt[:, 0:SEQ], start=True, stop=True)
                pe.matmul(M[3][:, SEQ:384], BT[:, P:SEQ], CTt[:, P:SEQ], start=True, stop=True).then_inc(s["cb_ps"], 1)

            def head(h):
                if h == 0:
                    pe.wait_ge(s["xdt_ready"], t["xdt"].add(2))
                pe.wait_ge(s["m_ready"], t["m"].add())
                out = M[h // 4][64 * (h % 2):64 * (h % 2) + 64, (h // 2 % 2) * SEQ:(h // 2 % 2) * SEQ + SEQ]
                pe.matmul(out, xdt[:, 0, h * 64:h * 64 + 64], MM[:, h % 3, 0:SEQ], start=True, stop=False)
                pe.matmul(out[:, P:SEQ], xdt[:, 1, h * 64:h * 64 + 64], MM[:, h % 3, SEQ:384],
                          start=False, stop=True).then_inc(s["y_done"], 1)

            def state():
                pe.wait_ge(s["btok_sb"], t["btok"].add())
                pe.wait_ge(s["xw_ready"], t["xw"].add())
                for j in range(XPG):
                    for b in range(2):
                        last = pe.matmul(M[2][:, j * P:j * P + P], xdt[:, b, j * P:j * P + P], Btok[:, b, :],
                                         start=b == 0, stop=b == 1)
                last.then_inc(s["st_ps"], 1)

            def rms():
                pe.wait_ge(s["sq_ready"], t["sq"].add(XPG))
                for j in range(XPG):
                    last = pe.matmul(M[3][:, 0:T], ones[:, :], zs[:, j, :], start=j == 0, stop=j == XPG - 1)
                last.then_inc(s["rms_ps"], 1)

            def z_blocks():
                pe.wait_ge(s["raw_ready"], t["raw"].add(2))
                block_units(xH, xL, KT, SETS[0], between=lambda q: token_major() if q == 1 else None)
                pe.wait_ge(s["raw_ready"], t["raw"].add(2))
                block_units(xH, xL, KT, SETS[1], between=lambda q: [head(2 * q), head(2 * q + 1)])

            def bcx_blocks(first=False):
                if not first:
                    pe.wait_ge(s["z_ready"], t["z"].add(2))
                bc_units(SETS[0])
                if not first:
                    state()
                    pe.wait_ge(s["z_ready"], t["z"].add(2))
                block_units(xH, xL, KT, SETS[1])
                if not first:
                    rms()
                    pe.wait_ge(s["fst_ready"], t["fst"].add())
                    pe.wait_ge(s["sd_ready"], t["sd"].add())
                block_units(xH, xL, KT, SETS[2])
                t["raw"].add(2)

            pe.wait_ge(s["x_lo"], 4)
            decay_setup()
            pe.wait_ge(s["pre_done"], 1)
            t["raw"].k = 0
            bcx_blocks(first=True)
            t["raw"].k = 0
            with rounds(pe, GROUPS - 1, t, dict(unit=U_BCX + U_Z, raw=6, xbc=6, xdt=2, m=8, btok=1, xw=1, sq=4,
                                                z=4, fst=1, sd=1)):
                z_blocks()
                bcx_blocks()
            z_blocks()

            evac = 0
            for b in range(8):
                if b < 2:
                    pe.wait_ge(s["z_ready"], t["z"].add(2))
                else:
                    pe.wait_ge(s["uraw"], 2 * (b - 1))
                block_units(xH, xL, KT, SETS[b % 2])
                if b == 0:
                    state()
                if b == 1:
                    rms()
            for g in range(4):
                pe.wait_ge(s["mix_lo"], 4 * (g + 1))
                if g == 0:
                    pe.wait_ge(s["uraw"], KT)
                else:
                    pe.wait_ge(s["wp_ready"], 4 * g)
                for b in range(2):
                    unit([(kk * BLK + j * P, mixH[:, 4 * g + kk, :], mixL[:, 4 * g + kk, :], SETS[b][j][:, 0:T],
                           kk == 0, kk == 3) for kk in range(4) for j in range(2)])
            pe.wait_ge(s["wp_ready"], KT)
            pe.wait_ge(s["mix_lo"], 2 * KT)

            for H, L, kts in ((mixH, mixL, KT), (yH, yL, YT)):
                if kts == YT:
                    pe.wait_ge(s["yl_ready"], YT)
                with rounds(pe, 8, t, dict(unit=4 + kts // 4, sgm=2, br_read=2)):
                    pe.wait_ge(s["sgm"], START["sgm"] + t["sgm"].now())
                    block_units(xH, xL, KT, SETS[0])
                    pe.wait_ge(s["br_read"], START["br_read"] + t["br_read"].now())
                    block_units(H, L, kts, SETS[1])
                    t["sgm"].add(2)
                    t["br_read"].add(2)
            pe.wait_ge(s["br_read"], START["br_read"] + t["br_read"].now())
            pe.wait_ge(s["mix_lo"], 3 * KT)

            def project(H, L, kts, pairs=4):
                with rounds(pe, pairs, t, dict(unit=2 * kts // 4 * (4 // pairs), res=16 // pairs)):
                    for b in range(8 // pairs):
                        pe.wait_ge(s["res_ready"], t["res"].now() + START["res_ready"] - 2)
                        block_units(H, L, kts, SETS[b % 2])
                        t["res"].add(2)

            def ln_sum():
                pe.wait_ge(s["res_ready"], t["res"].now() + START["res_ready"])
                for k in range(KT):
                    last = pe.matmul(M[0][:, 0:T], ones[:, :], resid[:, k, :], start=k == 0, stop=k == KT - 1)
                last.then_inc(s["ln_sum"], 1)

            def ln_var(sqb):
                for c in range(4):
                    pe.wait_ge(s["sqc_ready"], t["sqc"].add())
                    for k in range(4):
                        last = pe.matmul(M[1][:, 0:T], ones[:, :], sqb[:, c % 2, k * T:k * T + T],
                                         start=c == 0 and k == 0, stop=c == 3 and k == 3)
                    last.then_inc(s["sqc_used"], 1)

            project(mixH, mixL, KT)
            ln_sum()
            pe.wait_ge(s["mem_lo"], 4)
            block_units(memH, memL, KT, SETS[0], n=N_MEM)
            ln_var(sq)
            block_units(memH, memL, KT, SETS[1], n=N_MEM)
            for b in range(2):
                pe.wait_ge(s["kt_ready"], 2 * b + 2)
                for q in range(4):
                    slot = t["unit"].k % RING
                    pe.wait_ge(lo_ready, t["unit"].add() + RING)
                    for kk in range(4):
                        for m in range(2):
                            k = 4 * q + kk
                            wH, wL = whi[:, slot, kk * BLK:kk * BLK + BLK], wlo[:, slot, kk * BLK:kk * BLK + BLK]
                            mH, mL = memH[:, k, m * P:m * P + P], memL[:, k, m * P:m * P + P]
                            out = SETS[b][m][:, 0:BLK]
                            pe.matmul(out, mH, wH, start=k == 0, stop=False)
                            pe.matmul(out, mH, wL, start=False, stop=False)
                            last = pe.matmul(out, mL, wH, start=False, stop=k == KT - 1)
                    last.then_inc(used, 1)
            for b in range(2):
                pe.wait_ge(s["vn_ready"], 2 * b + 2)
                block_units(xH, xL, KT, SETS[b], before=lambda q: pe.wait_ge(s["x_lo"], 4 + q + 1))
            pe.wait_ge(s["q_ready"], MH)
            for h in range(MH):
                for b in range(2):
                    last = pe.matmul(M[h][:, b * N_MEM:b * N_MEM + N_MEM], qT[:, h, b * P:b * P + P], KTm[:, h, :],
                                     start=True, stop=True)
                last.then_inc(s["sc_ps"], 1)
            pe.wait_ge(s["kv_in"], 32)
            for m in range(2):
                for h in range(MH):
                    for b in range(NSAMP):
                        c = m * 32 + h * NSAMP + b
                        last = pe.matmul(G[0][0][:, c:c + 1], kc[:, b, h, m * P:m * P + P], qT[:, h, SEQ + b:SEQ + b + 1],
                                         start=True, stop=True)
            last.then_inc(s["ss_ps"], 1)
            pe.wait_ge(s["ss_sb"], 1)
            for m in range(2):
                last = pe.transpose(G[0][1][0:32, m * P:m * P + P], ssT[:, m, :], ident[:, :])
            last.then_inc(s["sst_ps"], 1)
            for h in range(MH):
                pe.wait_ge(s["pn_ready"], 2 * h + 2)
                if h >= 2:
                    pe.wait_ge(s["pt_ready"], h - 1)
                for m in range(2):
                    for b in range(2):
                        last = pe.transpose(G[1][h % 2][:, (m * 2 + b) * P:(m * 2 + b) * P + P],
                                            Pe[:, 2 * h + b, m * P:m * P + P], ident[:, :])
                last.then_inc(s["pt_ps"], 1)
                if h == MH - 1:
                    pe.wait_ge(s["sp_n"], 1)
                    for m in range(2):
                        last = pe.transpose(G[0][0][:, m * 32:m * 32 + 32], sP[:, m * P:m * P + P], ident[0:32, 0:32])
                    last.then_inc(s["spt_ps"], 1)
                pe.wait_ge(s["pt_ready"], h + 1)
                for m in range(2):
                    last = pe.matmul(M[h][:, 0:SEQ], Vn[:, m, h * MHD:h * MHD + MHD], PT[:, h % 2, m * SEQ:m * SEQ + SEQ],
                                     start=m == 0, stop=m == 1)
                last.then_inc(s["o_ps"], 1)
            pe.wait_ge(s["spt_sb"], 1)
            for h in range(MH):
                for b in range(NSAMP):
                    for m in range(2):
                        last = pe.matmul(G[0][1][:, h * NSAMP + b:h * NSAMP + b + 1], vc[:, b, m, h * MHD:h * MHD + MHD],
                                         sPT[:, m, h * NSAMP + b:h * NSAMP + b + 1], start=m == 0, stop=m == 1)
            last.then_inc(s["so_ps"], 1)
            pe.wait_ge(s["o_lo"], MH)
            for b in range(8):
                pe.wait_ge(s["res_ready"], t["res"].now() + START["res_ready"] - 2)
                unit([(kk * BLK + j * P, oH[:, kk, :], oL[:, kk, :], SETS[b % 2][j][:, 0:T],
                       kk == 0, kk == 3) for kk in range(4) for j in range(2)])
                t["res"].add(2)
            ln_sum()
            ln_var(sq2)
            pe.wait_ge(s["x_lo"], 12)
            with rounds(pe, FT // 2, t, dict(unit=8, sgm=2, h_read=2)):
                pe.wait_ge(s["sgm"], START["sgm"] + t["sgm"].now())
                block_units(xH, xL, KT, SETS[0])
                pe.wait_ge(s["h_read"], START["h_read"] + t["h_read"].now())
                block_units(xH, xL, KT, SETS[1])
                t["sgm"].add(2)
                t["h_read"].add(2)
            pe.wait_ge(s["h_lo"], FT)
            project(hH, hL, FT, pairs=2)
            ln_sum()
            ln_var(sq2)
            assert t["unit"].now() == N_UNITS, (t["unit"].now(), N_UNITS)

        @block.scalar
        def _(act):
            t = Tallies()

            def step(ins):
                ins.then_inc(act_step, 1)
                act.wait_ge(act_step, t["step"].add())

            def split(n):
                u = t["unit"]
                assert u.base % RING == 0 and (u.reg is None or u.per % RING == 0)
                for _ in range(n):
                    slot = u.k % RING
                    lap = u.base // RING + u.k // RING + 1
                    if u.reg is not None:
                        lap = u.reg * (u.per // RING) + lap
                    act.wait_ge(landed[slot], lap * 16)
                    act.wait_ge(used, u.add())
                    act.activation(whi[:, slot, :], raw[:, slot, :], ACT.Copy).then_inc(hi_ready, 1)

            def finished(units):
                act.wait_ge(used, t["done"].add(units) + RING)

            act.wait_ge(in_x, 16)
            for c in range(4):
                act.activation(flat(xH[:, 4 * c:4 * c + 4, :]), flat(resid[:, 4 * c:4 * c + 4, :]),
                               ACT.Copy).then_inc(s["x_hi"], 1)
            act.wait_ge(in_misc, N_MISC * 16)
            step(act.activation(pcol[:, 2:3], pcol[:, 1:2], ACT.Exp))
            act.wait_ge(s["dt_z"], 1)
            step(act.activation(S[:, 3, :], S[:, 2, :], ACT.Abs))
            act.activation(S[:, 4, :], S[:, 3, :], ACT.Exp, scale=-1.0).then_inc(s["dt_exp"], 1)
            act.wait_ge(s["dt_u"], 1)
            act.activation(S[:, 6, :], S[:, 5, :], ACT.Ln).then_inc(s["dt_ln"], 1)
            act.wait_ge(s["dt_ready"], 1)
            act.activation(pxs[:, NSAMP:2 * NSAMP], S[:, 0, SEQ:T], ACT.Exp).then_inc(s["pre_exp"], 1)
            act.wait_ge(s["w_sum"], 1)
            act.activation(flat(wtok[:, :, :]), flat(wtok[:, :, :]), ACT.Exp).then_inc(s["pre_done"], 1)

            def conv_block(dests, outs):
                for j in range(2):
                    n = t["raw"]
                    if n.reg is not None or n.k >= 2:
                        act.wait_ge(s["conv_done"], n.now(1))
                    act.activation(R[:, n.k % 2, CONV_W - 1:CONV_W - 1 + T], outs[j][:, 0:T], ACT.Copy)\
                       .then_inc(s["raw_ready"], 1)
                    n.add()
                for j in range(2):
                    c = t["conv"]
                    act.wait_ge(s["conv_done"], c.add())
                    act.activation(dests[j], cacc[:, (c.k - 1) % 2, :], ACT.Silu).then_inc(s["xbc_ready"], 1)

            def z_block(j):
                finished(4)
                for k in range(2):
                    act.activation(zs[:, 2 * j + k, :], SETS[j][k][:, 0:T], ACT.Silu).then_inc(s["z_ready"], 1)

            def heads(h0):
                for h in (h0, h0 + 1):
                    act.wait_ge(s["seg_ready"], START["seg_ready"] + t["e"].add())
                    act.activation(E[:, h % 2, :], E[:, h % 2, :], ACT.Exp).then_inc(s["e_ready"], 1)

            def group(epi):
                split(2)
                act.wait_ge(s["btok_ps"], t["btok"].add())
                act.activation(flat(Btok[:, :, :]), M[2][:, 0:256], ACT.Copy).then_inc(s["btok_sb"], 1)
                act.activation(bcs[:, :], M[2][0:NSAMP, 256:512], ACT.Copy).then_inc(s["bc_rows"], 1)
                split(1)
                heads(0)
                split(1)
                heads(2)
                z_block(0)
                split(1)
                heads(4)
                split(1)
                heads(6)
                split(2)
                z_block(1)
                act.wait_ge(s["dtx_ready"], t["dtx"].add())
                act.wait_ge(s["outer_free"], START["outer_free"] + t["fo"].now())
                t["fo"].add()
                for c in range(4):
                    split(1)
                    act.wait_ge(s[f"bc_in{c % 2}"], t[f"bc{c % 2}"].add() * 16)
                    for b in range(2):
                        if c + b:
                            act.wait_ge(s["st_done"], t["std"].now())
                        t["std"].add()
                        for i in range(XPG):
                            last = act.activation(outer[:, i, :], bcb[:, c % 2, b, 0:P], ACT.Copy,
                                                  scale=dtx[:, i, 2 * c + b:2 * c + b + 1])
                        last.then_inc(s["out_ready"], 1)
                act.wait_ge(s["st_done"], t["std"].now())
                act.wait_ge(s["st_ps"], t["st"].add())
                act.activation(flat(outer[:, :, :]), M[2][:, :], ACT.Copy).then_inc(s["fst_ready"], 1)
                for i in range(XPG):
                    act.wait_ge(s["y2_ready"], t["y2"].add())
                    act.activation(zs[:, i, :], yg[:, i, :], ACT.Square).then_inc(s["sq_ready"], 1)
                epi[0]()
                split(4)
                act.wait_ge(s["rms_ps"], t["rms"].add())
                act.activation(rstd, M[3][:, 0:T], ACT.Sqrt, scale=1.0 / (XPG * P), bias=eps[:, 0:1])\
                   .then_inc(s["sd_ready"], 1)
                for i in range(XPG):
                    act.wait_ge(s["y3_ready"], t["y3"].add())
                    yt = t["g"].now() * XPG + i
                    dst = yH[:, yt:yt + 1, :] if isinstance(yt, int) else yH[:, bass.ds(yt, 1), :]
                    act.activation(flat(dst), yg[:, i, :], ACT.Copy).then_inc(s["yh_ready"], 1)
                epi[1]()
                t["g"].add()

            def bcx_epilogue(i):
                finished(4)
                conv_block([[BT[:, :], CTt[:, :]], [xs[:, 0, :], xs[:, 1, :]], [xs[:, 2, :], xs[:, 3, :]]][i], SETS[i])

            split(4)
            for i in range(3):
                split(4)
                bcx_epilogue(i)
            with rounds(act, GROUPS - 1, t, dict(unit=20, done=20, raw=6, conv=6, e=8, g=1, btok=1, dtx=1,
                                                 fo=1, bc0=2, bc1=2, std=8, st=1, y2=4, rms=1, y3=4)):
                group([lambda: bcx_epilogue(0), lambda: (bcx_epilogue(1), split(4), bcx_epilogue(2))])
            group([lambda: None, lambda: None])

            act.wait_ge(s["tails_out"], 16)
            act.wait_ge(s["outer_free"], START["outer_free"] + GROUPS)
            n = 0
            for b in range(8):
                finished(4)
                for j in range(2):
                    if n >= 1:
                        act.wait_ge(s["pool_f"], n)
                        act.activation(mixH[:, n - 1, :], tmp[:, (n - 1) % 2, :], ACT.Copy).then_inc(s["mix_hi"], 1)
                    act.activation(U[:, POOL_HIST:POOL_HIST + T], SETS[b % 2][j][:, 0:T], ACT.Copy).then_inc(s["uraw"], 1)
                    n += 1
                if b < 6:
                    split(4)
            act.wait_ge(s["pool_f"], n)
            act.activation(mixH[:, n - 1, :], tmp[:, (n - 1) % 2, :], ACT.Copy).then_inc(s["mix_hi"], 1)
            for g in range(4):
                split(2)
                t["done"].add(2)
                for j in range(4):
                    act.wait_ge(s["wp_ready"], 4 * g + j + 1)
                    act.activation(mixH[:, 4 * g + j, :], tmp[:, j % 2, :], ACT.Copy).then_inc(s["mix_hi"], 1)
            for br in range(2):
                extra = 4 * br
                with rounds(act, 8, t, dict(unit=8 + extra, done=8 + extra, br=2, **({"mf": 2} if br else {}))):
                    split(4)
                    finished(4)
                    act.wait_ge(s["br_read"], START["br_read"] + t["br"].now())
                    for j in range(2):
                        act.activation(sgA[:, j, :], SETS[0][j][:, 0:T], ACT.Sigmoid).then_inc(s["sgm"], 1)
                    t["br"].add(2)
                    split(4 + extra)
                    t["done"].add(4 + extra)
                    if br:
                        i = t["mf"].now()
                        for j in range(2):
                            act.wait_ge(s["br_read"], START["br_read"] + t["br"].now(1 - j))
                            act.activation(flat(mixH[:, bass.ds(i + j, 1), :]), tmp[:, j, :], ACT.Copy)\
                               .then_inc(s["mix_hi"], 1)
                        t["mf"].add(2)
            for b in range(8):
                split(4)
                t["done"].add(4)
                if b % 2:
                    c = b // 2
                    act.wait_ge(s[f"mem_in{c % 2}"], 16 * (c // 2) + 16)
                    act.activation(flat(memH[:, 4 * c:4 * c + 4, :]), memraw[:, c % 2, :], ACT.Copy)\
                       .then_inc(s["mem_hi"], 1)

            def ln_stats(sqb, meanb):
                act.wait_ge(s["ln_sum"], t["ln"].add())
                act.activation(meanb[:, :], M[0][:, 0:T], ACT.Copy, scale=1.0 / D_MODEL).then_inc(s["mean_ready"], 1)
                for c in range(4):
                    act.wait_ge(s["cen_ready"], t["cen"].add())
                    if t["sqc"].k >= 2:
                        act.wait_ge(s["sqc_used"], t["sqc"].k - 1)
                    act.activation(sqb[:, c % 2, :], flat(resid[:, 4 * c:4 * c + 4, :]), ACT.Square)\
                       .then_inc(s["sqc_ready"], 1)
                    t["sqc"].add()

            def ln_sd(rb):
                act.wait_ge(s["sqc_used"], t["var"].add(4))
                act.activation(rb[:, :], M[1][:, 0:T], ACT.Sqrt, scale=1.0 / D_MODEL, bias=eps[:, 1:2])\
                   .then_inc(s["lsd_ready"], 1)

            def ln_high(c):
                act.wait_ge(s["xn_ready"], t["xn"].add())
                act.activation(flat(xH[:, 4 * c:4 * c + 4, :]), flat(resid[:, 4 * c:4 * c + 4, :]), ACT.Copy)\
                   .then_inc(s["x_hi"], 1)

            def keys(b):
                finished(4)
                for j in range(2):
                    act.activation(KTm[:, 2 * b + j, :], SETS[b][j][:, 0:N_MEM], ACT.Copy).then_inc(s["kt_ready"], 1)

            def values(b):
                finished(4)
                for m in range(2):
                    act.activation(Vn[:, m, b * BLK:b * BLK + BLK], SETS[b][m][:, 0:BLK], ACT.Copy)\
                       .then_inc(s["vn_ready"], 1)

            def queries(b):
                finished(4)
                for j in range(2):
                    act.activation(qT[:, 2 * b + j, :], SETS[b][j][:, 0:T], ACT.Copy).then_inc(s["q_ready"], 1)

            ln_stats(sq, mean)
            split(4)
            ln_sd(lrstd)
            ln_high(0)
            ln_high(1)
            keys(0)
            split(4)
            ln_high(2)
            ln_high(3)
            keys(1)
            split(4)
            split(4)
            values(0)
            split(4)
            values(1)
            queries(0)
            split(4)
            queries(1)
            for h in range(MH):
                act.wait_ge(s["mx_ready"], h + 1)
                for b in range(2):
                    n = 2 * h + b
                    act.activation(Pe[:, n, :], M[h][:, b * N_MEM:b * N_MEM + N_MEM], ACT.Exp, bias=snm[:, n:n + 1],
                                   scale=MHD ** -0.5, accum_out=srs[:, n:n + 1]).then_inc(s["p_ready"], 1)
            act.wait_ge(s["ss_ps"], 1)
            act.activation(flat(ssT[:, :, :]), G[0][0][:, 0:64], ACT.Copy).then_inc(s["ss_sb"], 1)
            act.wait_ge(s["mx_ready"], MH + 1)
            act.activation(sP[:, :], G[0][1][0:32, 0:N_MEM], ACT.Exp, bias=snm[0:32, 8:9],
                           scale=MHD ** -0.5, accum_out=srs[0:32, 8:9]).then_inc(s["sp_exp"], 1)
            for h in range(MH):
                act.wait_ge(s["pt_ps"], h + 1)
                if h >= 2:
                    act.wait_ge(s["o_ps"], h - 1)
                act.activation(PT[:, h % 2, :], G[1][h % 2][:, :], ACT.Copy).then_inc(s["pt_ready"], 1)
            act.wait_ge(s["spt_ps"], 1)
            act.activation(flat(sPT[:, :, :]), G[0][0][:, 0:64], ACT.Copy).then_inc(s["spt_sb"], 1)
            for h in range(MH):
                act.wait_ge(s["o_f"], h + 1)
                act.activation(oH[:, h, :], oT[:, h, :], ACT.Copy).then_inc(s["o_hi"], 1)
            split(8)
            t["done"].add(8)
            act.wait_ge(s["kv_out"], 32)
            ln_stats(sq2, mean2)
            ln_sd(lrstd2)
            for c in range(4):
                ln_high(c)
            with rounds(act, FT // 2, t, dict(unit=8, done=8, h=2)):
                split(4)
                finished(4)
                act.wait_ge(s["h_read"], START["h_read"] + t["h"].now())
                for j in range(2):
                    act.activation(sgF[:, j, :], SETS[0][j][:, 0:T], ACT.Silu).then_inc(s["sgm"], 1)
                split(4)
                t["done"].add(4)
                i = t["h"].now()
                for j in range(2):
                    act.wait_ge(s["h_read"], START["h_read"] + t["h"].add())
                    act.activation(flat(hH[:, bass.ds(i + j, 1), :]), hf[:, j, :], ACT.Copy).then_inc(s["h_hi"], 1)
            for b in range(8):
                split(11 if b < 7 else 7)
            ln_stats(sq2, mean2)
            ln_sd(lrstd2)

        @block.vector
        def _(dve):
            t = Tallies()

            def step(ins):
                ins.then_inc(dve_step, 1)
                dve.wait_ge(dve_step, t["step"].add())

            def split(n):
                u = t["unit"]
                for _ in range(n):
                    slot = u.k % RING
                    dve.wait_ge(hi_ready, u.add())
                    dve.tensor_tensor(wlo[:, slot, :], raw[:, slot, :], whi[:, slot, :].bitcast(F32), ALU.subtract)\
                       .then_inc(lo_ready, 1)

            def finished(units):
                dve.wait_ge(used, t["done"].add(units) + RING)

            dve.memset(eps[:, 0:1], RMS_EPS)
            dve.memset(eps[:, 1:2], LN_EPS)
            dve.memset(R[:, :, 0:CONV_W - 1], 0.0)
            dve.memset(ones[:, :], 1.0).then_inc(s["ones_set"], 1)
            dve.sem_inc(lo_ready, RING)
            for c in range(4):
                dve.wait_ge(s["x_hi"], c + 1)
                dve.tensor_tensor(flat(xL[:, 4 * c:4 * c + 4, :]), flat(resid[:, 4 * c:4 * c + 4, :]),
                                  flat(xH[:, 4 * c:4 * c + 4, :]).bitcast(F32), ALU.subtract).then_inc(s["x_lo"], 1)
            dve.wait_ge(in_misc, N_MISC * 16)
            dve.wait_ge(s["dt_psum"], 1)
            dve.tensor_scalar(S[:, 2, :], M[0][0:HEADS, 0:T], pcol[:, 0:1], None, ALU.add).then_inc(s["dt_z"], 1)
            dve.wait_ge(s["dt_exp"], 1)
            dve.tensor_scalar(S[:, 5, :], S[:, 4, :], 1.0, None, ALU.add).then_inc(s["dt_u"], 1)
            dve.wait_ge(s["dt_u"], 1)
            step(dve.tensor_scalar(S[:, 3, :], S[:, 5, :], -1.0, 1e-30, ALU.add, ALU.max))
            step(dve.reciprocal(S[:, 7, :], S[:, 3, :]))
            step(dve.tensor_tensor(S[:, 3, :], S[:, 7, :], S[:, 4, :], ALU.mult))
            dve.wait_ge(s["dt_ln"], 1)
            step(dve.tensor_tensor(S[:, 7, :], S[:, 3, :], S[:, 6, :], ALU.mult))
            step(dve.scalar_tensor_tensor(out=S[:, 3, :], in0=S[:, 5, :], scalar=1.0, in1=S[:, 4, :],
                                          op0=ALU.is_equal, op1=ALU.mult))
            step(dve.tensor_tensor(S[:, 6, :], S[:, 7, :], S[:, 3, :], ALU.add))
            step(dve.scalar_tensor_tensor(out=S[:, 7, :], in0=S[:, 2, :], scalar=0.0, in1=S[:, 6, :],
                                          op0=ALU.max, op1=ALU.add))
            step(dve.tensor_scalar(pcol[:, 3:4], pcol[:, 2:3], -1.0, None, ALU.mult))
            step(dve.tensor_copy(pxs[:, 0:NSAMP], S[:, 7, SEQ:T]))
            dve.tensor_scalar(S[:, 0, :], S[:, 7, :], pcol[:, 3:4], None, ALU.mult).then_inc(s["dt_ready"], 1)
            dve.wait_ge(s["dA_tok_ps"], 1)
            dve.tensor_copy(flat(dAtok[:, :, :]), M[1][:, 0:2 * HEADS]).then_inc(s["dA_tok"], 1)
            dve.tensor_copy(flat(dttok[:, :, :]), M[2][:, 0:2 * HEADS]).then_inc(s["dA_tok"], 1)
            dve.wait_ge(s["cum_ps"], 1)
            dve.tensor_copy(S[:, 1, 0:SEQ], M[3][0:HEADS, 0:SEQ]).then_inc(s["cum_sb"], 1)
            dve.wait_ge(s["cumt_ps"], 1)
            step(dve.tensor_scalar(flat(ncum[:, :, :]), M[1][:, 0:2 * HEADS], -1.0, None, ALU.mult))
            step(dve.tensor_tensor(wtok[:, 0, :], ncum[:, 0, :], M[0][:, 0:HEADS], ALU.add))
            dve.tensor_tensor(wtok[:, 1, :], ncum[:, 1, :], M[0][:, 0:HEADS], ALU.add).then_inc(s["w_sum"], 1)
            cw = vec[:, 0:CT * CONV_W].rearrange("p (c k) -> p c k", k=CONV_W)
            hv = hist[:, :, :].rearrange("p c (b k) -> p c b k", k=CONV_W - 1)
            for k in range(CONV_W - 1):
                dst = chist if k == 0 else ctmp
                step(dve.tensor_tensor(dst[:, :, :], hv[:, :, :, k], cw[:, :, k:k + 1].to_broadcast([P, CT, NSAMP]), ALU.mult))
                if k:
                    step(dve.tensor_tensor(chist[:, :, :], chist[:, :, :], ctmp[:, :, :], ALU.add))
            for g, w in enumerate(WINDOWS):
                last = dve.tensor_reduce(phs[:, 4 * g:4 * g + 4, :], hpool[:, 4 * g:4 * g + 4, :, POOL_HIST - (w - 1):POOL_HIST],
                                         AX_X, ALU.add)
            step(last)

            def conv_block():
                for j in range(2):
                    n = t["raw"]
                    r = n.k % 2
                    if n.reg is not None or n.k >= 2:
                        dve.wait_ge(s["xbc_ready"], n.now(1))
                    idx = n.now()
                    dve.wait_ge(s["raw_ready"], n.add())
                    w = lambda k: vcol("conv_w", idx * CONV_W + k)
                    ct = (lambda x: x[:, idx, :]) if isinstance(idx, int) else (lambda x: flat(x[:, bass.ds(idx, 1), :]))
                    dve.tensor_copy(ct(tails), R[:, r, SEQ:SEQ + 11])
                    step(dve.tensor_scalar(cacc[:, r, :], R[:, r, CONV_W - 1:CONV_W - 1 + T], w(CONV_W - 1), vcol("conv_b", idx),
                                           ALU.mult, ALU.add))
                    dve.tensor_tensor(cacc[:, r, SEQ:T], cacc[:, r, SEQ:T], ct(chist), ALU.add)
                    for k in range(CONV_W - 1):
                        ins = dve.scalar_tensor_tensor(out=cacc[:, r, 0:SEQ], in0=R[:, r, k:k + SEQ], scalar=w(k),
                                                       in1=cacc[:, r, 0:SEQ], op0=ALU.mult, op1=ALU.add)
                        if k < CONV_W - 2:
                            step(ins)
                    ins.then_inc(s["conv_done"], 1)

            def heads(h0):
                if h0 == 0:
                    dve.wait_ge(s["cum_in"], t["cum"].add() * 16)
                for h in (h0, h0 + 1):
                    if h >= 2:
                        dve.wait_ge(s["m_ready"], t["m"].now(1 - h % 2))
                    hc = t["g"].now() * HPG + h
                    n = [ncum[:, b, hc:hc + 1] if isinstance(hc, int) else ncum[:, b, bass.ds(hc, 1)] for b in range(2)]
                    dve.tensor_scalar(E[:, h % 2, 0:SEQ], cumbc[:, h, :], n[0], 0.0, ALU.add, ALU.min)
                    dve.tensor_scalar(E[:, h % 2, SEQ:384], cumbc[:, h, P:SEQ], n[1], 0.0, ALU.add, ALU.min)\
                       .then_inc(s["seg_ready"], 1)
                for h in (h0, h0 + 1):
                    m = t["m"]
                    if h >= 3:
                        dve.wait_ge(s["y_done"], m.now(2))
                    dve.wait_ge(s["e_ready"], m.add())
                    dve.tensor_tensor(MM[:, h % 3, :], E[:, h % 2, :], cbm[:, :], ALU.mult).then_inc(s["m_ready"], 1)

            def group(epi):
                gh = t["g"].now() * HPG
                gx = t["g"].now() * XPG
                per_head = (lambda x, b: x[:, b, gh:gh + HPG]) if isinstance(gh, int) else (
                    lambda x, b: x[:, b, bass.ds(gh, HPG)])
                split(2)
                dve.wait_ge(s["xtok_ps"], t["xtok"].add())
                for b in range(2):
                    dve.tensor_tensor(xdt[:, b, :].rearrange("p (h c) -> p h c", h=HPG),
                                      M[b][:, :].rearrange("p (h c) -> p h c", h=HPG),
                                      per_head(dttok, b).rearrange("p (h o) -> p h o", o=1).to_broadcast([P, HPG, 64]),
                                      ALU.mult).then_inc(s["xdt_ready"], 1)
                dve.wait_ge(s["cb_ps"], t["cb"].add())
                step(dve.tensor_tensor(cbm[:, :], M[3][:, 0:384], cmask[:, :], ALU.mult))
                split(1)
                heads(0)
                split(1)
                heads(2)
                split(1)
                heads(4)
                split(1)
                heads(6)
                split(2)
                t["done"].add(8)
                dve.wait_ge(s["y_done"], t["m"].now())
                for b in range(2):
                    ins = dve.tensor_tensor(xdt[:, b, :].rearrange("p (h c) -> p h c", h=HPG),
                                            xdt[:, b, :].rearrange("p (h c) -> p h c", h=HPG),
                                            per_head(wtok, b).rearrange("p (h o) -> p h o", o=1).to_broadcast([P, HPG, 64]),
                                            ALU.mult)
                ins.then_inc(s["xw_ready"], 1)
                sl = dts[:, gx:gx + XPG, :] if isinstance(gx, int) else dts[:, bass.ds(gx, XPG), :]
                dve.tensor_tensor(dtx[:, :, :], sl[:, :, 0:NSAMP], xs[:, :, SEQ:T], ALU.mult).then_inc(s["dtx_ready"], 1)
                for c in range(4):
                    split(1)
                    dve.wait_ge(s[f"st_in{c % 2}"], t[f"sti{c % 2}"].add() * 16)
                    for b in range(2):
                        dve.wait_ge(s["out_ready"], t["out"].add())
                        for i in range(XPG):
                            dcol = (dts[:, gx + i, NSAMP + 2 * c + b:NSAMP + 2 * c + b + 1] if isinstance(gx, int) else
                                    dts[:, bass.ds(gx + i, 1), NSAMP + 2 * c + b:NSAMP + 2 * c + b + 1].rearrange(
                                        "p a b -> p (a b)"))
                            ins = dve.scalar_tensor_tensor(out=st[:, c % 2, b, i, :], in0=st[:, c % 2, b, i, :],
                                                           scalar=dcol, in1=outer[:, i, :], op0=ALU.mult, op1=ALU.add)
                        ins.then_inc(s["st_done"], 1)
                        dve.wait_ge(s["st_done"], t["std"].add())
                        for i in range(XPG):
                            ins = dve.tensor_tensor_reduce(
                                out=flat(E[:, :, :])[:, i * P:i * P + P], in0=st[:, c % 2, b, i, :], in1=bcb[:, c % 2, b, P:2 * P], scale=1.0,
                                scalar=0.0, op0=ALU.mult, op1=ALU.add, accum_out=ysamp[:, i, 2 * c + b:2 * c + b + 1])
                        if b == 0:
                            step(ins)
                    ins.then_inc(s["bc_used"], 1)
                    dve.wait_ge(s["bc_used"], t["bcu"].add())
                for i in range(XPG):
                    d = vcol("d_skip", gx + i)
                    dve.scalar_tensor_tensor(out=yg[:, i, 0:SEQ], in0=xs[:, i, 0:SEQ], scalar=d,
                                             in1=M[i // 2][:, (i % 2) * SEQ:(i % 2) * SEQ + SEQ], op0=ALU.mult, op1=ALU.add)
                    step(dve.scalar_tensor_tensor(out=yg[:, i, SEQ:T], in0=xs[:, i, SEQ:T], scalar=d,
                                                  in1=ysamp[:, i, :], op0=ALU.mult, op1=ALU.add))
                dve.wait_ge(s["z_ready"], t["z"].add(XPG))
                for i in range(XPG):
                    dve.tensor_tensor(yg[:, i, :], yg[:, i, :], zs[:, i, :], ALU.mult).then_inc(s["y2_ready"], 1)
                epi[0]()
                split(4)
                dve.wait_ge(s["sd_ready"], t["sd"].add())
                step(dve.reciprocal(rstd, rstd))
                for i in range(XPG):
                    dve.scalar_tensor_tensor(out=yg[:, i, :], in0=yg[:, i, :], scalar=vcol("norm_w", gx + i),
                                             in1=rstd, op0=ALU.mult, op1=ALU.mult).then_inc(s["y3_ready"], 1)
                for i in range(XPG):
                    dve.wait_ge(s["yh_ready"], t["yh"].add())
                    one = (lambda x: x[:, gx + i, :]) if isinstance(gx, int) else (lambda x: flat(x[:, bass.ds(gx + i, 1), :]))
                    dve.tensor_tensor(one(yL), yg[:, i, :], one(yH).bitcast(F32), ALU.subtract).then_inc(s["yl_ready"], 1)
                epi[1]()
                t["g"].add()

            dve.wait_ge(s["dts_in"], 32)
            split(4)
            for i in range(3):
                split(4)
                t["done"].add(4)
                conv_block()
            with rounds(dve, GROUPS - 1, t, dict(unit=20, done=20, raw=6, m=8, g=1, xtok=1, cb=1, sti0=2, sti1=2, out=8,
                                                 std=8, z=4, sd=1, yh=4, bcu=4, cum=1, step=STEPS)):
                def first():
                    t["done"].add(4)
                    conv_block()

                def rest():
                    t["done"].add(4)
                    conv_block()
                    split(4)
                    t["done"].add(4)
                    conv_block()
                group([first, rest])
            group([lambda: None, lambda: None])
            dve.wait_ge(s["tails_out"], 16)
            dve.wait_ge(s["yl_ready"], YT)
            step(dve.memset(U[:, 0:POOL_HIST], 0.0))
            for n in range(KT):
                g, w = n // 4, WINDOWS[n // 4]
                dve.wait_ge(s["uraw"], n + 1)
                if n >= 2:
                    dve.wait_ge(s["mix_hi"], n - 1)
                dve.tensor_copy(utail[:, n, :], U[:, POOL_HIST + SEQ - POOL_HIST:POOL_HIST + T])
                cur, reach = U[:, :], 1
                while reach < w:
                    v = V[:, (reach.bit_length() - 1) % 2, :]
                    step(dve.tensor_tensor(v[:, 2 * reach - 1:POOL_HIST + SEQ], cur[:, 2 * reach - 1:POOL_HIST + SEQ],
                                           cur[:, reach - 1:POOL_HIST + SEQ - reach], ALU.add))
                    cur, reach = v, 2 * reach
                step(dve.tensor_tensor(cur[:, POOL_HIST + SEQ:POOL_HIST + T], U[:, POOL_HIST + SEQ:POOL_HIST + T],
                                       phs[:, n, :], ALU.add))
                step(dve.tensor_tensor(tmp[:, n % 2, 0:16], cur[:, POOL_HIST:POOL_HIST + 16], rc[:, g, :], ALU.mult))
                step(dve.tensor_tensor(tmp[:, n % 2, 0:16], tmp[:, n % 2, 0:16], U[:, POOL_HIST:POOL_HIST + 16], ALU.subtract))
                dve.scalar_tensor_tensor(out=tmp[:, n % 2, 16:T], in0=cur[:, POOL_HIST + 16:POOL_HIST + T], scalar=1.0 / w,
                                         in1=U[:, POOL_HIST + 16:POOL_HIST + T], op0=ALU.mult, op1=ALU.subtract)\
                   .then_inc(s["pool_f"], 1)
                if n >= 1:
                    dve.wait_ge(s["mix_hi"], n)
                    dve.tensor_tensor(mixL[:, n - 1, :], tmp[:, (n - 1) % 2, :], mixH[:, n - 1, :].bitcast(F32),
                                      ALU.subtract).then_inc(s["mix_lo"], 1)
                if n % 2:
                    t["done"].add(4)
                    if n < 12:
                        split(4)
            dve.wait_ge(s["mix_hi"], KT)
            dve.tensor_tensor(mixL[:, KT - 1, :], tmp[:, (KT - 1) % 2, :], mixH[:, KT - 1, :].bitcast(F32),
                              ALU.subtract).then_inc(s["mix_lo"], 1)
            for g in range(4):
                split(2)
                finished(2)
                for j in range(5):
                    if j < 4:
                        dve.wait_ge(s["mix_lo"], KT + 4 * g + j - 1)
                        dve.tensor_scalar(tmp[:, j % 2, :], SETS[j // 2][j % 2][:, 0:T], vcol("pool_scale", 4 * g + j), None,
                                          ALU.mult).then_inc(s["wp_ready"], 1)
                    if j >= 1:
                        n = 4 * g + j - 1
                        dve.wait_ge(s["mix_hi"], KT + n + 1)
                        dve.wait_ge(s["wp_ready"], n + 1)
                        dve.tensor_tensor(mixL[:, n, :], tmp[:, (j - 1) % 2, :], mixH[:, n, :].bitcast(F32),
                                          ALU.subtract).then_inc(s["mix_lo"], 1)
            for g in range(2):
                dve.wait_ge(s[f"st_out{g}"], 16 * 2 * GROUPS)
            for br in range(2):
                extra = 4 * br
                with rounds(dve, 8, t, dict(unit=8 + extra, done=8 + extra, sg=2, br=2,
                                            **({"step": 2, "mh": 2} if br else {}))):
                    split(8 + extra)
                    i = t["br"].now() if br == 0 else t["mh"].now()
                    dve.wait_ge(s["sgm"], START["sgm"] + t["sg"].add(2))
                    finished(8 + extra)
                    for j in range(2):
                        r = flat(resid[:, bass.ds(i + j, 1), :])
                        if br == 0:
                            dve.tensor_tensor(r, SETS[1][j][:, 0:T], sgA[:, j, :], ALU.mult).then_inc(s["br_read"], 1)
                            t["br"].add()
                        else:
                            step(dve.tensor_tensor(tmp[:, j, :], SETS[1][j][:, 0:T], sgA[:, j, :], ALU.mult))
                            dve.tensor_tensor(tmp[:, j, :], tmp[:, j, :], r, ALU.add).then_inc(s["br_read"], 1)
                            t["br"].add()
                    if br:
                        for j in range(2):
                            dve.wait_ge(s["mix_hi"], t["mh"].add() + 2 * KT)
                            m = lambda x: flat(x[:, bass.ds(i + j, 1), :])
                            dve.tensor_tensor(m(mixL), tmp[:, j, :], m(mixH).bitcast(F32), ALU.subtract)\
                               .then_inc(s["mix_lo"], 1)

            def residual(b, units):
                finished(units)
                for j in range(2):
                    k = 2 * b + j
                    step(dve.scalar_tensor_tensor(out=resid[:, k, :], in0=xH[:, k, :].bitcast(F32), scalar=ALPHA,
                                                  in1=SETS[b % 2][j][:, 0:T], op0=ALU.mult, op1=ALU.add))
                    dve.scalar_tensor_tensor(out=resid[:, k, :], in0=xL[:, k, :].bitcast(F32), scalar=ALPHA,
                                             in1=resid[:, k, :], op0=ALU.mult, op1=ALU.add).then_inc(s["res_ready"], 1)

            for b in range(8):
                split(4)
                residual(b, 4)
                if b % 2:
                    c = b // 2
                    dve.wait_ge(s["mem_hi"], c + 1)
                    dve.tensor_tensor(flat(memL[:, 4 * c:4 * c + 4, :]), memraw[:, c % 2, :],
                                      flat(memH[:, 4 * c:4 * c + 4, :]).bitcast(F32), ALU.subtract).then_inc(s["mem_lo"], 1)

            def chunk(c):
                return resid[:, 4 * c:4 * c + 4, :]

            def spread(v):
                return v[:, :].rearrange("p (o t) -> p o t", o=1).to_broadcast([P, 4, T])

            def ln_center(meanb):
                dve.wait_ge(s["mean_ready"], t["mean"].add())
                for c in range(4):
                    dve.tensor_tensor(chunk(c), chunk(c), spread(meanb), ALU.subtract).then_inc(s["cen_ready"], 1)

            def ln_rstd(rb):
                dve.wait_ge(s["lsd_ready"], t["lsd"].add())
                step(dve.reciprocal(rb[:, :], rb[:, :]))

            def ln_scale(c, rb, which, low=True):
                step(dve.tensor_tensor(chunk(c), chunk(c), spread(rb), ALU.mult))
                for k in range(4 * c, 4 * c + 4):
                    last = dve.tensor_scalar(resid[:, k, :], resid[:, k, :], vcol(f"ln_{which}_g", k), vcol(f"ln_{which}_b", k),
                                             ALU.mult, ALU.add)
                last.then_inc(s["xn_ready"], 1)

            def ln_low(c):
                dve.wait_ge(s["x_hi"], t["xh"].add() + 4)
                dve.tensor_tensor(flat(xL[:, 4 * c:4 * c + 4, :]), flat(chunk(c)),
                                  flat(xH[:, 4 * c:4 * c + 4, :]).bitcast(F32), ALU.subtract).then_inc(s["x_lo"], 1)

            ln_center(mean)
            split(4)
            ln_rstd(lrstd)
            ln_scale(0, lrstd, "mix")
            ln_scale(1, lrstd, "mix")
            ln_low(0)
            ln_low(1)
            split(4)
            ln_scale(2, lrstd, "mix")
            ln_scale(3, lrstd, "mix")
            ln_low(2)
            ln_low(3)
            split(16)
            t["done"].add(24)
            for h in range(MH):
                dve.wait_ge(s["sc_ps"], h + 1)
                step(dve.tensor_reduce(smx[:, 2 * h:2 * h + 2], M[h][:, :].rearrange("p (b m) -> p b m", b=2), AX_X, ALU.max))
                dve.tensor_scalar(snm[:, 2 * h:2 * h + 2], smx[:, 2 * h:2 * h + 2], -MHD ** -0.5, None, ALU.mult)\
                   .then_inc(s["mx_ready"], 1)
            for n in range(2 * MH):
                dve.wait_ge(s["p_ready"], n + 1)
                step(dve.reciprocal(sri[:, n:n + 1], srs[:, n:n + 1]))
                dve.tensor_scalar(Pe[:, n, :], Pe[:, n, :], sri[:, n:n + 1], None, ALU.mult).then_inc(s["pn_ready"], 1)
            dve.wait_ge(s["sst_ps"], 1)
            step(dve.tensor_reduce(smx[0:32, 8:9], G[0][1][0:32, 0:N_MEM], AX_X, ALU.max))
            dve.tensor_scalar(snm[0:32, 8:9], smx[0:32, 8:9], -MHD ** -0.5, None, ALU.mult).then_inc(s["mx_ready"], 1)
            dve.wait_ge(s["sp_exp"], 1)
            step(dve.reciprocal(sri[0:32, 8:9], srs[0:32, 8:9]))
            dve.tensor_scalar(sP[:, :], sP[:, :], sri[0:32, 8:9], None, ALU.mult).then_inc(s["sp_n"], 1)
            for h in range(MH):
                dve.wait_ge(s["o_ps"], h + 1)
                dve.tensor_copy(oT[:, h, 0:SEQ], M[h][:, 0:SEQ])
            dve.wait_ge(s["so_ps"], 1)
            for h in range(MH):
                dve.tensor_copy(oT[:, h, SEQ:T], G[0][1][:, h * NSAMP:h * NSAMP + NSAMP]).then_inc(s["o_f"], 1)
            for h in range(MH):
                dve.wait_ge(s["o_hi"], h + 1)
                dve.tensor_tensor(oL[:, h, :], oT[:, h, :], oH[:, h, :].bitcast(F32), ALU.subtract).then_inc(s["o_lo"], 1)
            for b in range(8):
                split(1)
                residual(b, 1)
            ln_center(mean2)
            ln_rstd(lrstd2)
            for c in range(4):
                ln_scale(c, lrstd2, "mem")
                ln_low(c)
            with rounds(dve, FT // 2, t, dict(unit=8, done=8, sg=2, h=2)):
                split(8)
                finished(8)
                dve.wait_ge(s["sgm"], START["sgm"] + t["sg"].add(2))
                i = t["h"].now()
                dve.wait_ge(s["h_hi"], START["h_hi"] + t["h"].now())
                for j in range(2):
                    dve.tensor_tensor(hf[:, j, :], SETS[1][j][:, 0:T], sgF[:, j, :], ALU.mult).then_inc(s["h_read"], 1)
                for j in range(2):
                    dve.wait_ge(s["h_hi"], START["h_hi"] + t["h"].add())
                    m = lambda x: flat(x[:, bass.ds(i + j, 1), :])
                    dve.tensor_tensor(m(hL), hf[:, j, :], m(hH).bitcast(F32), ALU.subtract).then_inc(s["h_lo"], 1)
            for b in range(8):
                split(11 if b < 7 else 7)
                residual(b, 11)
            ln_center(mean2)
            ln_rstd(lrstd2)
            for c in range(4):
                ln_scale(c, lrstd2, "ffn")


        @block.gpsimd
        def _(pool):
            t = Tallies()
            misc = ((ident[:, :], a["ident"]), (vec[:, :], a["vecs"]), (cmask[:, :], a["cmask"]),
                    (flat(rc[:, :, :]), a["rc"]), (flat(wdt[:, :, :]), a["wdt"]), (flat(hist[:, :, :]), a["hist"]),
                    (hpool[:, :, :, :].rearrange("p k b j -> p (k b j)"), a["hpool"]),
                    (pcol[:, 0:1], a["dt_bias"]), (pcol[:, 1:2], a["a_log"]))
            assert len(misc) == N_MISC
            for dst, src in misc:
                pool.dma_start(dst, src).then_inc(in_misc, 16)
            pool.dma_start(o["pass_conv"], a["state_conv"][:, 1:CONV_W - 1, :]).then_inc(s["outs"], 16)
            pool.dma_start(o["pass_pool"], a["state_pool"][:, 1:POOL_HIST, :]).then_inc(s["outs"], 16)
            pool.wait_ge(s["cum_sb"], 1)
            pool.dma_start(scr_cum, S[:, 1, 0:SEQ]).then_inc(s["scr_out"], 16)
            pool.wait_ge(s["pre_exp"], 1)
            pool.dma_start(scr_dts, pxs[:, :]).then_inc(s["scr_out"], 16)
            pool.wait_ge(s["scr_out"], 32)
            for half in range(2):
                src = scr_dts.rearrange("(t h) k -> h t k", h=2)[half:half + 1]
                pool.dma_start(dts[64 * half:64 * half + 64, :, :], src.to_broadcast([64, YT, 2 * NSAMP]))\
                    .then_inc(s["dts_in"], 16)

            def alone(semaphore, count):
                pool.wait_ge(semaphore, count)
                pool.sem_inc(s["pool_past"], 1)

            with rounds(pool, GROUPS, t, {}) as g:
                alone(s["seg_ready"], g * HPG + START["seg_ready"])
                pool.dma_start(flat(cumbc[:, :, :]), scr_cum[bass.ds(g * HPG, HPG), :].rearrange(
                    "(o h) l -> o (h l)", o=1).to_broadcast([P, HPG * SEQ])).then_inc(s["cum_in"], 16)

                def load_state(c):
                    pool.dma_start(st[:, c % 2].rearrange("p b i n -> p (b i n)"),
                                   a["state_ssd"][bass.ds(g, 1), c].rearrange("g p c -> (g p) c"))\
                        .then_inc(s[f"st_in{c % 2}"], 16)

                def store_state(c):
                    alone(s["bc_used"], g * 4 + (c + 1))
                    pool.dma_start(o["new_ssd_s"][bass.ds(g, 1), c].rearrange("g p c -> (g p) c"),
                                   st[:, c % 2].rearrange("p b i n -> p (b i n)")).then_inc(s[f"st_out{c % 2}"], 16)

                def load_bc(c):
                    pool.dma_start(bcb[:, c % 2].rearrange("p b n -> p (b n)"),
                                   scr_bc[2 * c:2 * c + 2, :].rearrange("(o b) n -> o (b n)", o=1).to_broadcast([P, 4 * P]))\
                        .then_inc(s[f"bc_in{c % 2}"], 16)

                load_state(0)
                load_state(1)
                alone(s["bc_rows"], g + 1)
                pool.dma_start(scr_bc, bcs[:, :]).then_inc(s["bc_out"], 16)
                alone(s["bc_out"], g * 16 + 16)
                load_bc(0)
                load_bc(1)
                for c in range(2):
                    store_state(c)
                    load_bc(c + 2)
                    alone(s[f"st_out{c}"], g * 32 + 16)
                    load_state(c + 2)
                store_state(2)
                store_state(3)
                alone(s["fst_ready"], g + 1)
                pool.dma_start(o["new_ssd_p"][bass.ds(g, 1)].rearrange("g p c -> (g p) c"), flat(outer[:, :, :]))\
                    .then_inc(s["fst_out"], 16)
                for c in range(2):
                    alone(s[f"st_out{c}"], g * 32 + 32)
                pool.wait_ge(s["fst_out"], g * 16 + 16)
                pool.sem_inc(s["outer_free"], 1)
            pool.wait_ge(s["conv_done"], CT)
            pool.dma_start(o["tails"], flat(tails[:, :, :])).then_inc(s["tails_out"], 16)
            pool.wait_ge(s["pool_f"], KT)
            pool.dma_start(o["utail"], flat(utail[:, :, :])).then_inc(s["outs"], 16)
            pool.wait_ge(s["mix_lo"], 3 * KT)
            for c in range(4):
                if c >= 2:
                    pool.wait_ge(s["mem_lo"], c - 1)
                pool.dma_start(memraw[:, c % 2, :], a["memT"][:, c * 4 * N_MEM:(c + 1) * 4 * N_MEM])\
                    .then_inc(s[f"mem_in{c % 2}"], 16)
            pool.wait_ge(s["kt_ready"], MH)
            pool.dma_start(o["mem_k"], flat(KTm[:, :, :])).then_inc(s["kv_out"], 16)
            pool.wait_ge(s["vn_ready"], 4)
            pool.dma_start(o["mem_v"], flat(Vn[:, :, :])).then_inc(s["kv_out"], 16)
            pool.wait_ge(s["outs"], 48)
            pool.dma_start(kc[:, :, :, :].rearrange("p b h m -> p (b h m)"), a["kc"]).then_inc(s["kv_in"], 16)
            pool.dma_start(vc[:, :, :, :].rearrange("p b m d -> p (b m d)"), a["vc"]).then_inc(s["kv_in"], 16)
            for c in range(4):
                pool.wait_ge(s["xn_ready"], 8 + c + 1)
                pool.dma_start(o["yT"][:, c * 4 * T:(c + 1) * 4 * T], flat(resid[:, 4 * c:4 * c + 4, :]))\
                    .then_inc(s["outs"], 16)
            pool.wait_ge(s["outs"], 16 * 7)
            pool.wait_ge(s["scr_out"], 32)
            pool.wait_ge(s["bc_out"], 16 * GROUPS)
            pool.wait_ge(s["st_out0"], 32 * GROUPS)
            pool.wait_ge(s["st_out1"], 32 * GROUPS)
            pool.wait_ge(s["fst_out"], 16 * GROUPS)
            pool.wait_ge(s["tails_out"], 16)
            pool.wait_ge(s["kv_out"], 32)


def group_tiles(x, axis=-1):
    bc = D_INNER // P
    order = [t for g in range(GROUPS) for t in (bc + g, bc + GROUPS + g, *range(XPG * g, XPG * g + XPG))]
    return order


def feature_major(x):
    n, f = x.shape
    return x.T.reshape(f // P, P, n).transpose(1, 0, 2)


def blocks(w, kts=4):
    K, N = w.shape
    return w.reshape(K // (P * kts), kts, P, N // BLK, BLK).transpose(3, 0, 2, 1, 4).reshape(-1, P, kts * BLK)


def narrow_blocks(w):
    K, N = w.shape
    return w.reshape(K // (P * 8), 8, P, N // P, P).transpose(3, 0, 2, 1, 4).reshape(-1, P, 8 * P)


def interleave(*parts):
    n, lists = parts[0]
    out = []
    for i in range(n):
        for m, x in parts:
            k = x.shape[0] // m
            out.append(x[i * k:(i + 1) * k])
    return np.concatenate(out)


def kernel(**inputs):
    import concourse.bacc as bacc
    from concourse.bass_utils import run_bass_kernel_spmd

    x = {n: np.asarray(v) for n, v in inputs.items()}
    w_in = x["w_in"][0]
    cuts = np.cumsum([0, D_MODEL, D_INNER, D_INNER, GROUPS * D_STATE, GROUPS * D_STATE, HEADS, D_MODEL, D_MODEL])
    w_u, w_z, w_x, w_b, w_c, w_dt, w_gp, w_gs = [w_in[:, p:q] for p, q in zip(cuts, cuts[1:])]

    def cols(w, g, n):
        return w[:, g * n:(g + 1) * n]

    def bcx(g):
        return [narrow_blocks(cols(w_b, g, P)), narrow_blocks(cols(w_c, g, P)), blocks(cols(w_x, g, XPG * P))]

    stream = list(bcx(0))
    for g in range(GROUPS):
        stream.append(blocks(cols(w_z, g, XPG * P)))
        if g < GROUPS - 1:
            stream += bcx(g + 1)
    stream.append(blocks(w_u))
    for g in range(4):
        stream.append(blocks(x["w_pool"][0, g]))
    stream.append(interleave((8, blocks(w_gp)), (8, blocks(x["w_pool_br"][0]))))
    stream.append(interleave((8, blocks(w_gs)), (8, blocks(x["w_ssd_br"][0]))))
    stream.append(blocks(x["w_out"][0]))
    stream += [blocks(x[n][0]) for n in ("w_mk", "w_mv", "w_mq", "w_mo")]
    stream.append(interleave((FT // 2, blocks(x["w_ffn_gate"][0])), (FT // 2, blocks(x["w_ffn_up"][0]))))
    stream.append(blocks(x["w_ffn_down"][0]))
    tiles = group_tiles(None)

    def per_feature(v):
        return v.reshape(-1, P).T

    conv_w = x["conv_w"][0].reshape(CONV_W, CT, P)[:, tiles].transpose(2, 1, 0).reshape(P, CT * CONV_W)
    conv_b = per_feature(x["conv_b"][0])[:, tiles]
    d_skip = np.repeat(x["d_skip"][0], 64).reshape(YT, P).T
    vecs = [conv_w, conv_b, per_feature(x["ssd_norm_w"][0]), d_skip] + [
        per_feature(x[n][0]) for n in ("pool_scale", "ln_mix_g", "ln_mix_b", "ln_mem_g", "ln_mem_b", "ln_ffn_g", "ln_ffn_b")]
    tri = (np.arange(P)[:, None] <= np.arange(P)[None, :]).astype(np.float32)
    counts = np.array([[1.0 / min(w, t + 1) for t in range(16)] for w in WINDOWS], np.float32)
    hist = x["state_conv"][0].reshape(NSAMP, CONV_W - 1, CT, P)[:, :, tiles].transpose(3, 2, 0, 1)
    arrays = {
        "wstream": np.concatenate(stream),
        "wdt": w_dt.reshape(KT, P, HEADS).transpose(1, 0, 2).reshape(P, KT * HEADS),
        "xT": feature_major(np.concatenate([x["x_prompt"][0], x["x_sample"][:, 0]])).reshape(P, KT * T),
        "memT": feature_major(x["mem_prompt"][0]).reshape(P, KT * N_MEM),
        "vecs": np.concatenate(vecs, axis=1),
        "hist": hist.reshape(P, -1),
        "hpool": x["state_pool"][0].reshape(NSAMP, POOL_HIST, KT, P).transpose(3, 2, 0, 1).reshape(P, -1),
        "dt_bias": x["dt_bias"][0][:, None],
        "a_log": x["a_log"][0][:, None],
        "ident": np.eye(P, dtype=np.float32),
        "cmask": np.concatenate([tri, np.ones((P, P), np.float32), tri], axis=1),
        "rc": np.broadcast_to(counts.reshape(1, -1), (P, 64)),
        "state_conv": x["state_conv"][0],
        "state_pool": x["state_pool"][0],
        "state_ssd": x["state_ssd"][0].reshape(4, 2, GROUPS, XPG, P, D_STATE).transpose(2, 0, 4, 1, 3, 5)
                      .reshape(GROUPS, 4, P, UNIT),
        "kc": x["cache_mem_k"][0].transpose(3, 0, 2, 1).reshape(P, -1),
        "vc": x["cache_mem_v"][0].reshape(NSAMP, 2, P, MEM_DIM).transpose(2, 0, 1, 3).reshape(P, -1),
    }
    arrays = {n: np.ascontiguousarray(v) for n, v in arrays.items()}
    assert arrays["wstream"].shape == (N_UNITS, P, UNIT), (arrays["wstream"].shape, N_UNITS)
    outs = {
        "yT": (P, KT * T), "new_ssd_p": (GROUPS, P, XPG * P), "tails": (P, CT * 11), "utail": (P, KT * 23),
        "mem_k": (P, MH * N_MEM), "mem_v": (P, 2 * MEM_DIM), "new_ssd_s": (GROUPS, 4, P, UNIT),
        "pass_conv": (NSAMP, CONV_W - 2, CONV_DIM), "pass_pool": (NSAMP, POOL_HIST - 1, D_MODEL),
    }
    nc = bacc.Bacc("TRN2", target_bir_lowering=False, num_devices=1, dynamic_dma_scratch_size=8192)
    ins = {n: nc.dram_tensor(f"in_{n}", v.shape, mybir.dt.from_np(v.dtype), kind="ExternalInput").ap() for n, v in arrays.items()}
    res = {n: nc.dram_tensor(f"out_{n}", v, F32, kind="ExternalOutput").ap() for n, v in outs.items()}
    build(nc, ins, res)
    r = run_bass_kernel_spmd(nc, [{f"in_{n}": v for n, v in arrays.items()}], core_ids=[0]).results[0]
    r = {n: np.asarray(r[f"out_{n}"]) for n in outs}

    y = r["yT"].reshape(P, KT, T).transpose(2, 1, 0).reshape(T, D_MODEL)
    back = np.argsort(tiles)
    tail = r["tails"].reshape(P, CT, 11)[:, back].transpose(2, 1, 0).reshape(11, CONV_DIM)
    utail = r["utail"].reshape(P, KT, 23).transpose(2, 1, 0).reshape(23, D_MODEL)
    new_conv_s = np.concatenate([r["pass_conv"], tail[3:, None]], axis=1)[None]
    new_pool_s = np.concatenate([r["pass_pool"], utail[15:, None]], axis=1)[None]
    new_ssd_p = r["new_ssd_p"].reshape(GROUPS, P, XPG, D_STATE).transpose(0, 2, 1, 3).reshape(1, 1, HEADS, 64, D_STATE)
    new_ssd_s = r["new_ssd_s"].reshape(GROUPS, 4, P, 2, XPG, D_STATE).transpose(1, 3, 0, 4, 2, 5)\
        .reshape(1, NSAMP, HEADS, 64, D_STATE)
    mem_k = r["mem_k"].reshape(P, MH, N_MEM).transpose(2, 1, 0)[None, None]
    mem_v = r["mem_v"].reshape(P, 2, MEM_DIM).transpose(1, 0, 2).reshape(1, 1, N_MEM, MH, MHD)
    return (y[None, :SEQ], y[SEQ:, None], new_ssd_p, tail[None, None, :3], utail[None, None, :15], mem_k, mem_v,
            new_ssd_s, new_conv_s, new_pool_s)
```

```python
from contextlib import ExitStack, contextmanager
import math

import numpy as np

import concourse.bass as bass
from concourse import mybir

F32 = mybir.dt.float32
F32R = mybir.dt.float32r
ALU = mybir.AluOpType
ACT = mybir.ActivationFunctionType
AX_X = mybir.AxisListType.X

P = 128
D_MODEL = 2048
SEQ = 256
NSAMP = 8
T = SEQ + NSAMP
KT = D_MODEL // P
WINDOWS = (2, 4, 8, 16)
POOL_HIST = 15
GROUPS = 8
HPG = 8
HEADS = 64
D_INNER = 4096
D_STATE = 128
CONV_W = 4
CONV_DIM = D_INNER + 2 * GROUPS * D_STATE
CT = CONV_DIM // P
CPG = CT // GROUPS
XPG = 4
YT = D_INNER // P
N_MEM = 256
MH = 4
MHD = 128
MEM_DIM = MH * MHD
D_FF = -(-8 * D_MODEL // (3 * 256)) * 256
FT = D_FF // P
ALPHA = 2 ** 0.25
LN_EPS = 1e-5
RMS_EPS = 1e-5
RING = 4
UNIT = 1024
BLK = 256

VECS = [("conv_w", CT * CONV_W), ("conv_b", CT), ("norm_w", YT), ("d_skip", YT), ("pool_scale", KT),
        ("ln_mix_g", KT), ("ln_mix_b", KT), ("ln_mem_g", KT), ("ln_mem_b", KT),
        ("ln_ffn_g", KT), ("ln_ffn_b", KT)]
VEC_AT, _at = {}, 0
for _name, _n in VECS:
    VEC_AT[_name] = _at
    _at += _n
NVEC = _at

U_BCX = 3 * 4
U_Z = 2 * 4
U_UP = 8 * 4
U_POOL = 4 * 2
U_BRA = 8 * 8
U_BRB = 8 * 12
U_OUT = 8 * 4
U_MEM = 4 * 4
U_Q = 2 * 4
U_MO = 8
U_F1 = (FT // 2) * 8
U_F2 = 8 * (FT // 4)
N_MISC = 9
START = {"sgm": 1, "br_read": 1, "h_read": 1, "h_hi": 1, "seg_ready": 1, "res_ready": 3,
         "fst_free": 1, "st_done": 3}
STEPS = 24
N_UNITS = GROUPS * (U_BCX + U_Z) + U_UP + U_POOL + U_BRA + U_BRB + U_OUT + U_MEM + U_Q + U_MO + U_F1 + U_F2


class Tally:

    def __init__(self):
        self.base, self.k, self.per, self.reg = 0, 0, 0, None

    def add(self, n=1):
        self.k += n
        return self.now()

    def now(self, less=0):
        v = self.base + self.k - less
        return v if self.reg is None else self.reg * self.per + v


class Tallies(dict):
    def __missing__(self, name):
        self[name] = Tally()
        return self[name]


@contextmanager
def rounds(eng, n, tallies, per):
    with eng.Fori(0, n) as i:
        frozen = {}
        for name, p in per.items():
            t = tallies[name]
            t.base, t.k, t.per, t.reg = t.base + t.k, 0, p, i
        for name, t in tallies.items():
            if name not in per:
                frozen[name] = t.k
        yield i
        for name, p in per.items():
            assert tallies[name].k == p, (name, tallies[name].k, p)
        for name, t in tallies.items():
            assert name in per or t.k == frozen.get(name, 0), (name, t.k)
    for name, p in per.items():
        t = tallies[name]
        t.base, t.k, t.reg = t.base + n * p, 0, None


class Event:

    def __init__(self, kind, i, block, unit, item):
        self.kind, self.i, self.item = kind, i, item
        self.blocks = [block] if kind == "in" else [block, block + 1]
        self.tiles = 2 if kind == "in" else 4
        self.end = unit + self.tiles_units(kind)

    @staticmethod
    def tiles_units(kind):
        return 4 if kind == "in" else 2


def plan_pooling():
    events, block, unit, item = [], 0, 0, 0
    order = []
    for b in range(8):
        order.append(("in", b))
        if b >= 3 and b % 2:
            order.append(("proj", b // 2 - 1))
    order.append(("proj", 3))
    for kind, i in order:
        e = Event(kind, i, block, unit, item)
        block, unit, item = block + len(e.blocks), e.end, item + e.tiles
        events.append(e)
    for e in events:
        if e.kind == "proj":
            e.needs = next(p.item + 2 for p in events if p.kind == "in" and p.i == 2 * e.i + 1)
    read = {}
    for e in events:
        for n, k in enumerate(e.blocks):
            read[k] = ("uraw", 2 * e.i + 2) if e.kind == "in" else ("wp_ready", 4 * e.i + 2 * n + 2)
    return events, read


EVENTS, READ = plan_pooling()


def flat(ap):
    return ap.rearrange("p a b -> p (a b)")


def build(nc, a, o):
    ctx = ExitStack()
    with ctx:
        def sem(name):
            return ctx.enter_context(nc.semaphore(name))

        def alloc(stack, name, shape, dt=F32):
            return stack.enter_context(nc.sbuf_tensor("sb_" + name, shape, dt))

        def overlay(skip, **tensors):
            out = []
            with ExitStack() as s:
                if skip:
                    alloc(s, f"skip_{next(iter(tensors))}", [P, skip // 4])
                for name, (shape, *dt) in tensors.items():
                    out.append(alloc(s, name, shape, *dt))
            return out

        raw = alloc(ctx, "raw", [P, RING, UNIT])
        whi = alloc(ctx, "whi", [P, RING, UNIT], F32R)
        wlo = alloc(ctx, "wlo", [P, RING, UNIT], F32R)
        xH = alloc(ctx, "xH", [P, KT, T], F32R)
        xL = alloc(ctx, "xL", [P, KT, T], F32R)
        resid = alloc(ctx, "resid", [P, KT, T])
        ident = alloc(ctx, "ident", [P, P])
        ones = alloc(ctx, "ones", [P, P])
        vec = alloc(ctx, "vec", [P, NVEC])
        rc = alloc(ctx, "rc", [P, 4, 16])
        phs = alloc(ctx, "phs", [P, KT, NSAMP])
        eps = alloc(ctx, "eps", [P, 2])
        total = alloc(ctx, "total", [P, T])
        dtxc = alloc(ctx, "dtxc", [P, GROUPS * NSAMP, XPG])
        decc = alloc(ctx, "decc", [P, GROUPS * NSAMP, XPG])

        def vcol(name, i, n=1):
            if isinstance(i, int):
                return vec[:, VEC_AT[name] + i:VEC_AT[name] + i + n]
            return vec[:, bass.ds(i + VEC_AT[name], n)]

        G = [[ctx.enter_context(nc.psum_tensor(f"G{s}{j}", [P, 512], F32)) for j in range(2)] for s in range(2)]
        M = [ctx.enter_context(nc.psum_tensor(f"M{j}", [P, 512], F32)) for j in range(4)]
        SETS = [G[0], G[1], [M[2], M[3]], [M[0], M[1]]]

        YB = 2 * YT * T * 4
        yH, yL = overlay(0, yH=([P, YT, T], F32R), yL=([P, YT, T], F32R))
        (zs, cumbc, xdt, BT, CTt, cbm, cmask, E, MM, Btok, bcs, fst, bcp, R, cacc, dttok, ncum, wtok,
         dts, dtx, ysamp, ysbc, chist, tails) = overlay(
            YB, zs=([P, XPG, T],), cumbc=([P, HPG, SEQ],), xdt=([P, 2, HPG * 64],),
            BT=([P, T],), CTt=([P, T],), cbm=([P, 384],), cmask=([P, 384],), E=([P, 2, 384],),
            MM=([P, 3, 384],), Btok=([P, 2, P],), bcs=([NSAMP, P],), fst=([P, XPG * P],), bcp=([P, NSAMP],),
            R=([P, 2, CONV_W - 1 + T],), cacc=([P, 2, T],), dttok=([P, 2, HEADS],), ncum=([P, 2, HEADS],),
            wtok=([P, 2, HEADS],), dts=([P, YT, 2 * NSAMP],), dtx=([P, XPG, NSAMP],),
            ysamp=([P, XPG, NSAMP],), ysbc=([P, XPG, NSAMP],), chist=([P, CT, NSAMP],), tails=([P, CT, 11],))
        rstd = E[:, 0, 0:T]
        xs = resid[:, 0:XPG, :]
        yg = resid[:, XPG:2 * XPG, :]
        stT = resid[:, 8:16, :].rearrange("p a b -> p (a b)")[:, 0:4 * XPG * P].rearrange(
            "p (s c) -> p s c", s=4)
        wdt, hist, hpool, S, dAtok, pcol, pxs, ctmp = overlay(
            0, wdt=([P, KT, HEADS],), hist=([P, CT, NSAMP * 3],), hpool=([P, KT, NSAMP, POOL_HIST],),
            S=([HEADS, 8, T],), dAtok=([P, 2, HEADS],), pcol=([HEADS, 4],), pxs=([HEADS, 2 * NSAMP],),
            ctmp=([P, CT, NSAMP],))
        mixH, mixL, tmp, utail, sgA = overlay(
            YB, mixH=([P, KT, T], F32R), mixL=([P, KT, T], F32R), tmp=([P, 4, T],), utail=([P, KT, 23],),
            sgA=([P, 2, T],))
        UT = POOL_HIST + T
        V = flat(resid[:, :, :])[:, XPG * T:XPG * T + 4 * UT].rearrange("p (l j t) -> p l j t", l=2, j=2)
        U = flat(resid[:, :, :])[:, 2176:2176 + 4 * UT].rearrange("p (r j t) -> p r j t", r=2, j=2)
        assert XPG * T + 4 * UT <= 2176 and 2176 >= 2 * XPG * T
        sq, KTm, Vn, mean, lrstd, memH, memL, memraw, PT, ssT, sP, sPT, smx, snm, srs, sri = overlay(
            0, sq=([P, 2, 4 * T],), KTm=([P, MH, N_MEM],), Vn=([P, 2, MEM_DIM],), mean=([P, T],),
            lrstd=([P, T],), memH=([P, KT, N_MEM], F32R), memL=([P, KT, N_MEM], F32R),
            memraw=([P, 2, 4 * N_MEM],), PT=([P, 2, 512],), ssT=([P, 2, 32],),
            sP=([32, N_MEM],), sPT=([P, 2, 32],), smx=([P, 9],), snm=([P, 9],), srs=([P, 9],), sri=([P, 9],))
        kc, qT = overlay(YB, kc=([P, NSAMP, MH, N_MEM],), qT=([P, MH, T],))
        (vc,) = overlay(YB, vc=([P, NSAMP, 2, MEM_DIM],))
        oH, oL = overlay(0, oH=([P, MH, T], F32R), oL=([P, MH, T], F32R))
        AT_MEM = (2 * 4 * T + 2 * MH * N_MEM + 2 * T) * 4
        (Pe,) = overlay(AT_MEM + 2 * KT * N_MEM * 4, Pe=([P, 2 * MH, N_MEM],))
        sq2, mean2, lrstd2, hH, hL, hf, sgF, outer, bcb = overlay(
            0, sq2=([P, 2, 4 * T],), mean2=([P, T],), lrstd2=([P, T],), hH=([P, FT, T], F32R),
            hL=([P, FT, T], F32R), hf=([P, 2, T],), sgF=([P, 2, T],),
            outer=([P, 2, XPG, P],), bcb=([P, 2, 2 * P],))
        st = flat(sq2[:, :, :])[:, 0:2 * UNIT].rearrange("p (s b i n) -> p s b i n", s=2, b=2, i=XPG)

        scr_cum = nc.dram_tensor("scr_cum", (HEADS, SEQ), F32, kind="Internal").ap()
        scr_dts = nc.dram_tensor("scr_dts", (HEADS, 2 * NSAMP), F32, kind="Internal").ap()
        scr_bc = nc.dram_tensor("scr_bc", (GROUPS * NSAMP, P), F32, kind="Internal").ap()

        landed = [sem(f"landed{k}") for k in range(RING)]
        hi_ready, lo_ready, used = sem("hi_ready"), sem("lo_ready"), sem("used")
        in_x, in_misc = [sem(f"in_x{c}") for c in range(4)], sem("in_misc")
        act_step, dve_step = sem("act_step"), sem("dve_step")
        s = {n: sem(n) for n in (
            "fst_free bcp_ready st_used ys_ps b_in0 b_in1 pool_past seg_ready w_sum y2_ready bc_used kv_out tails_out x_hi x_lo dt_psum dt_z dt_abs dt_exp dt_u dt_ln dt_ready dA_tok_ps dA_tok cum_ps cum_sb cumt_ps "
            "pre_exp pre_done scr_out dts_in ones_set "
            "raw_ready conv_done xbc_ready xtok_ps btok_ps btok_sb bc_rows cb_ps xdt_ready e_ready m_ready "
            "y_done xw_ready st_ps fst_ready z_ready dtx_ready out_ready st_done sq_ready rms_ps sd_ready "
            "y3_ready yh_ready yl_ready cum_in bc_out st_in0 st_in1 st_in2 st_in3 st_out0 st_out1 fst_out "
            "uraw pool_f mix_hi mix_lo wp_ready sgm br_read res_ready res_part "
            "ln_sum mean_ready cen_ready sqc_ready sqc_used  lsd_ready nrm_ready xn_ready "
            "mem_in0 mem_in1 mem_hi mem_lo kt_ready vn_ready kc_in vc_in sum_ready smx_ready q_ready sc_ps mx_ready p_ready pn_ready "
            "pt_ps pt_ready o_ps o_f o_hi o_lo ss_ps ss_sb sst_ps sp_exp sp_n spt_ps spt_sb so_ps "
            "h_read h_hi h_lo outs").split()}
        block = ctx.enter_context(nc.Block())

        @block.sync
        def _(sp):
            def load(u, k):
                sp.wait_ge(lo_ready, u + (k + 1))
                sp.dma_start(raw[:, k, :], a["wstream"][bass.ds(u + k, 1), :, :].rearrange("u p c -> (u p) c"))\
                    .then_inc(landed[k], 16)

            for c in range(4):
                sp.dma_start(flat(resid[:, 4 * c:4 * c + 4, :]), a["xT"][:, c * 4 * T:(c + 1) * 4 * T])\
                    .then_inc(in_x[c], 16)
                if c == 1 or c == 3:
                    load(0, c // 2)
            load(0, 2)
            load(0, 3)
            with sp.Fori(1, N_UNITS // RING) as i:
                for k in range(RING):
                    load(i * RING, k)

        @block.tensor
        def _(pe):
            t = Tallies()
            pe.sem_inc(used, RING)
            for name, value in START.items():
                pe.sem_inc(s[name], value)

            def mm3(slot, col, kH, kL, out, start, stop):
                w = whi[:, slot, col:col + P]
                pe.matmul(out, w, kH, start=start, stop=False)
                pe.matmul(out, w, kL, start=False, stop=False)
                return pe.matmul(out, wlo[:, slot, col:col + P], kH, start=False, stop=stop)

            def unit(plan):
                u = t["unit"]
                assert u.base % RING == 0 and (u.reg is None or u.per % RING == 0)
                slot = u.k % RING
                pe.wait_ge(lo_ready, u.add() + RING)
                for p in plan:
                    last = mm3(slot, *p)
                last.then_inc(used, 1)

            def block_units(H, L, kts, out, n=T, between=None, before=None):
                for q in range(0, kts, 4):
                    if before:
                        before(q // 4)
                    unit([(kk * BLK + j * P, H[:, q + kk, 0:n], L[:, q + kk, 0:n], out[j][:, 0:n],
                           q + kk == 0, q + kk == kts - 1) for kk in range(4) for j in range(2)])
                    if between:
                        between(q // 4)

            def bc_units(out, before=None):
                for j in range(2):
                    for q in (0, 8):
                        if before and j == 0:
                            before(q)
                        unit([(kk * P, xH[:, q + kk, :], xL[:, q + kk, :], out[j][:, 0:T],
                               q + kk == 0, q + kk == KT - 1) for kk in range(8)])

            def step_sizes():
                pe.wait_ge(in_misc, N_MISC * 16)
                for k in range(KT):
                    last = pe.matmul(M[0][0:HEADS, 0:T], wdt[:, k, :], resid[:, k, :], start=k == 0, stop=k == KT - 1)
                last.then_inc(s["dt_psum"], 1)

            def decays(part):
                if part == 0:
                    pe.wait_ge(s["dt_ready"], 1)
                    for r in range(2):
                        for b in range(2):
                            last = pe.transpose(M[1][:, r * P + b * 64:r * P + b * 64 + 64],
                                                S[:, 7 * r, b * P:b * P + P], ident[0:HEADS, 0:HEADS])
                    last.then_inc(s["dA_tok_ps"], 1)
                elif part == 1:
                    pe.wait_ge(s["dA_tok"], 2)
                    pe.wait_ge(s["ones_set"], 1)
                    pe.matmul(M[0][0:HEADS, 0:SEQ], dAtok[:, 0, :], cmask[:, 0:SEQ], start=True, stop=False)
                    pe.matmul(M[0][0:HEADS, P:SEQ], dAtok[:, 1, :], cmask[:, SEQ:384], start=False, stop=True)
                    for b in range(2):
                        last = pe.matmul(M[0][:, 384:384 + HEADS], ones[:, :], dAtok[:, b, :], start=b == 0, stop=b == 1)
                    last.then_inc(s["cum_ps"], 1)
                else:
                    pe.wait_ge(s["cum_sb"], 1)
                    for b in range(2):
                        last = pe.transpose(M[1][:, 256 + b * 64:256 + b * 64 + 64], S[:, 1, b * P:b * P + P],
                                            ident[0:HEADS, 0:HEADS])
                    last.then_inc(s["cumt_ps"], 1)

            def token_major():
                pe.wait_ge(s["xbc_ready"], t["xbc"].add(CPG))
                for b in range(2):
                    for j in range(XPG):
                        last = pe.transpose(M[b][:, j * P:j * P + P], xs[:, j, b * P:b * P + P], ident[:, :])
                last.then_inc(s["xtok_ps"], 1)
                for b in range(2):
                    pe.transpose(M[2][:, b * P:b * P + P], BT[:, b * P:b * P + P], ident[:, :])
                pe.transpose(M[2][0:NSAMP, 256:384], BT[:, SEQ:T], ident[:, :]).then_inc(s["btok_ps"], 1)
                pe.matmul(M[3][:, 0:SEQ], BT[:, 0:P], CTt[:, 0:SEQ], start=True, stop=True)
                pe.matmul(M[3][:, SEQ:384], BT[:, P:SEQ], CTt[:, P:SEQ], start=True, stop=True).then_inc(s["cb_ps"], 1)

            def head(h):
                if h == 0:
                    pe.wait_ge(s["xdt_ready"], t["xdt"].add(2))
                pe.wait_ge(s["m_ready"], t["m"].add())
                out = M[h // 4][64 * (h % 2):64 * (h % 2) + 64, (h // 2 % 2) * SEQ:(h // 2 % 2) * SEQ + SEQ]
                pe.matmul(out, xdt[:, 0, h * 64:h * 64 + 64], MM[:, h % 3, 0:SEQ], start=True, stop=False)
                pe.matmul(out[:, P:SEQ], xdt[:, 1, h * 64:h * 64 + 64], MM[:, h % 3, SEQ:384],
                          start=False, stop=True).then_inc(s["y_done"], 1)

            def sample(b):
                pe.wait_ge(s[f"st_in{b % 4}"], t[f"sti{b % 4}"].add() * 16)
                for i in range(XPG):
                    last = pe.matmul(M[3][:, 384 + i * NSAMP + b:385 + i * NSAMP + b], stT[:, b % 4, i * P:i * P + P],
                                     CTt[:, SEQ + b:SEQ + b + 1], start=True, stop=True)
                last.then_inc(s["st_used"], 1)
                if b == NSAMP - 1:
                    pe.wait_ge(s["bcp_ready"], t["bcp"].add())
                    pe.matmul(M[3][:, 416:416 + NSAMP], ones[:, :], bcp[:, :], start=True, stop=True)\
                      .then_inc(s["ys_ps"], 1)

            def state():
                pe.wait_ge(s["btok_sb"], t["btok"].add())
                pe.wait_ge(s["xw_ready"], t["xw"].add())
                for j in range(XPG):
                    for b in range(2):
                        last = pe.matmul(M[2][:, j * P:j * P + P], xdt[:, b, j * P:j * P + P], Btok[:, b, :],
                                         start=b == 0, stop=b == 1)
                last.then_inc(s["st_ps"], 1)

            def rms():
                pe.wait_ge(s["sq_ready"], t["sq"].add(XPG))
                for j in range(XPG):
                    last = pe.matmul(M[0][:, 0:T], ones[:, :], zs[:, j, :], start=j == 0, stop=j == XPG - 1)
                last.then_inc(s["rms_ps"], 1)

            def z_blocks():
                pe.wait_ge(s["raw_ready"], t["raw"].add(2))
                block_units(xH, xL, KT, SETS[0], between=lambda q: token_major() if q == 2 else None)
                pe.wait_ge(s["raw_ready"], t["raw"].add(2))
                block_units(xH, xL, KT, SETS[1], between=lambda q: [head(2 * q), head(2 * q + 1), sample(2 * q),
                                                                    sample(2 * q + 1)])

            def bcx_blocks():
                pe.wait_ge(s["z_ready"], t["z"].add(2))
                bc_units(SETS[0])
                state()
                pe.wait_ge(s["z_ready"], t["z"].add(2))
                block_units(xH, xL, KT, SETS[1])
                rms()
                pe.wait_ge(s["fst_ready"], t["fst"].add())
                block_units(xH, xL, KT, SETS[2])
                t["raw"].add(2)
                pe.wait_ge(s["sd_ready"], t["sd"].add())

            bc_units(SETS[0], before=lambda q: pe.wait_ge(s["x_lo"], q // 4 + 2))
            step_sizes()
            block_units(xH, xL, KT, SETS[1])
            decays(0)
            block_units(xH, xL, KT, SETS[2], between=lambda q: decays(q // 2 + 1) if q % 2 else None)
            pe.wait_ge(s["w_sum"], 1)
            with rounds(pe, GROUPS - 1, t, dict(unit=U_BCX + U_Z, raw=6, xbc=6, xdt=2, m=8, btok=1, xw=1, sq=4,
                                                z=4, fst=1, sd=1, bcp=1, sti0=2, sti1=2, sti2=2, sti3=2)):
                z_blocks()
                bcx_blocks()
            z_blocks()

            for e in EVENTS:
                sets = [SETS[k % 4] for k in e.blocks]
                for k in e.blocks:
                    if k >= 4:
                        pe.wait_ge(s[READ[k - 4][0]], READ[k - 4][1])
                if e.kind == "in":
                    if e.i < 2:
                        pe.wait_ge(s["z_ready"], t["z"].add(2))
                    if e.i == 2:
                        pe.wait_ge(s["fst_ready"], t["fst"].add())
                    if e.i == 3:
                        pe.wait_ge(s["sd_ready"], t["sd"].add())
                    block_units(xH, xL, KT, sets[0])
                    if e.i == 0:
                        state()
                    if e.i == 1:
                        rms()
                else:
                    pe.wait_ge(s["mix_lo"], e.needs)
                    for b in range(2):
                        unit([(kk * BLK + j * P, mixH[:, 4 * e.i + kk, :], mixL[:, 4 * e.i + kk, :], sets[b][j][:, 0:T],
                               kk == 0, kk == 3) for kk in range(4) for j in range(2)])

            pe.wait_ge(s["wp_ready"], 12)
            for H, L, kts in ((mixH, mixL, KT), (yH, yL, YT)):
                if kts == YT:
                    pe.wait_ge(s["yl_ready"], YT)
                with rounds(pe, 8, t, dict(unit=4 + kts // 4, sgm=2, br_read=2)):
                    pe.wait_ge(s["sgm"], START["sgm"] + t["sgm"].now())
                    block_units(xH, xL, KT, SETS[0])
                    pe.wait_ge(s["br_read"], START["br_read"] + t["br_read"].now())
                    pe.wait_ge(s["mix_lo"], 2 * KT)
                    block_units(H, L, kts, SETS[1])
                    t["sgm"].add(2)
                    t["br_read"].add(2)
            pe.wait_ge(s["br_read"], START["br_read"] + t["br_read"].now())

            def project(H, L, kts, pairs=4, before=None):
                with rounds(pe, pairs, t, dict(unit=2 * kts // 4 * (4 // pairs), res=16 // pairs)):
                    for b in range(8 // pairs):
                        pe.wait_ge(s["res_ready"], t["res"].now() + START["res_ready"] - 2)
                        block_units(H, L, kts, SETS[b % 2], before=before)
                        t["res"].add(2)

            def ln_sum():
                pe.wait_ge(s["sum_ready"], t["sum"].add())
                pe.matmul(M[0][:, 0:T], ones[:, :], total[:, :], start=True, stop=True).then_inc(s["ln_sum"], 1)

            def ln_var(sqb):
                for c in range(4):
                    pe.wait_ge(s["sqc_ready"], t["sqc"].add())
                    for k in range(4):
                        last = pe.matmul(M[1][:, 0:T], ones[:, :], sqb[:, c % 2, k * T:k * T + T],
                                         start=c == 0 and k == 0, stop=c == 3 and k == 3)
                    last.then_inc(s["sqc_used"], 1)

            project(mixH, mixL, KT, before=lambda q: pe.wait_ge(s["mix_lo"], 2 * KT + 4 * (q + 1)))
            ln_sum()
            pe.wait_ge(s["mem_lo"], 4)
            block_units(memH, memL, KT, SETS[0], n=N_MEM)
            ln_var(sq)
            block_units(memH, memL, KT, SETS[1], n=N_MEM)

            def weighted(h):
                pe.wait_ge(s["pt_ready"], h + 1)
                for m in range(2):
                    last = pe.matmul(M[h][:, 0:SEQ], Vn[:, m, h * MHD:h * MHD + MHD], PT[:, h % 2, m * SEQ:m * SEQ + SEQ],
                                     start=m == 0, stop=m == 1)
                last.then_inc(s["o_ps"], 1)
                if h == MH - 2:
                    pe.wait_ge(s["vc_in"], 16)
                    pe.wait_ge(s["spt_sb"], 1)
                    for k in range(MH):
                        for b in range(NSAMP):
                            for m in range(2):
                                last = pe.matmul(G[0][1][:, k * NSAMP + b:k * NSAMP + b + 1],
                                                 vc[:, b, m, k * MHD:k * MHD + MHD],
                                                 sPT[:, m, k * NSAMP + b:k * NSAMP + b + 1], start=m == 0, stop=m == 1)
                    last.then_inc(s["so_ps"], 1)

            def values(b, out, between=None):
                for q in range(4):
                    slot = t["unit"].k % RING
                    pe.wait_ge(lo_ready, t["unit"].add() + RING)
                    for kk in range(4):
                        for m in range(2):
                            k = 4 * q + kk
                            wH, wL = whi[:, slot, kk * BLK:kk * BLK + BLK], wlo[:, slot, kk * BLK:kk * BLK + BLK]
                            mH, mL = memH[:, k, m * P:m * P + P], memL[:, k, m * P:m * P + P]
                            o_ = out[m][:, 0:BLK]
                            pe.matmul(o_, mH, wH, start=k == 0, stop=False)
                            pe.matmul(o_, mH, wL, start=False, stop=False)
                            last = pe.matmul(o_, mL, wH, start=False, stop=k == KT - 1)
                    last.then_inc(used, 1)
                    if between:
                        between(q)

            for b in range(2):
                if b == 1:
                    pe.wait_ge(s["kt_ready"], 2)
                block_units(xH, xL, KT, SETS[2 - 2 * b], before=lambda q: pe.wait_ge(s["x_lo"], 4 + q + 1))
            for h in range(MH):
                pe.wait_ge(s["q_ready"], h + 1)
                for b in range(2):
                    last = pe.matmul(M[h][:, b * N_MEM:b * N_MEM + N_MEM], qT[:, h, b * P:b * P + P], KTm[:, h, :],
                                     start=True, stop=True)
                last.then_inc(s["sc_ps"], 1)
            pe.wait_ge(s["kc_in"], 16)
            for m in range(2):
                for h in range(MH):
                    for b in range(NSAMP):
                        c = m * 32 + h * NSAMP + b
                        last = pe.matmul(G[0][0][:, c:c + 1], kc[:, b, h, m * P:m * P + P], qT[:, h, SEQ + b:SEQ + b + 1],
                                         start=True, stop=True)
            last.then_inc(s["ss_ps"], 1)

            def sample_scores(q):
                if q == 0:
                    pe.wait_ge(s["ss_sb"], 1)
                    for m in range(2):
                        last = pe.transpose(G[0][1][0:32, m * P:m * P + P], ssT[:, m, :], ident[:, :])
                    last.then_inc(s["sst_ps"], 1)

            pe.wait_ge(s["kt_ready"], MH)
            values(0, SETS[1], between=sample_scores)
            pe.wait_ge(s["sp_exp"], 1)
            values(1, SETS[0])
            for h in range(MH):
                pe.wait_ge(s["pn_ready"], 2 * h + 2)
                if h == 0:
                    pe.wait_ge(s["vn_ready"], 2)
                if h >= 2:
                    pe.wait_ge(s["pt_ready"], h - 1)
                for m in range(2):
                    for b in range(2):
                        last = pe.transpose(G[1][h % 2][:, (m * 2 + b) * P:(m * 2 + b) * P + P],
                                            Pe[:, 2 * h + b, m * P:m * P + P], ident[:, :])
                last.then_inc(s["pt_ps"], 1)
                if h == 0:
                    pe.wait_ge(s["vn_ready"], 4)
                    pe.wait_ge(s["sp_n"], 1)
                    for m in range(2):
                        last = pe.transpose(G[0][0][:, m * 32:m * 32 + 32], sP[:, m * P:m * P + P], ident[0:32, 0:32])
                    last.then_inc(s["spt_ps"], 1)
                if h >= 1:
                    weighted(h - 1)
            weighted(MH - 1)
            pe.wait_ge(s["o_hi"], MH + 1)
            pe.wait_ge(s["o_lo"], MH + 1)
            for b in range(8):
                if b >= 4:
                    pe.wait_ge(s["res_ready"], t["res"].now() + START["res_ready"] - 6)
                unit([(kk * BLK + j * P, oH[:, kk, :], oL[:, kk, :], SETS[b % 4][j][:, 0:T],
                       kk == 0, kk == 3) for kk in range(4) for j in range(2)])
                t["res"].add(2)
            ln_sum()
            ln_var(sq2)
            with rounds(pe, FT // 2, t, dict(unit=8, sgm=2, h_read=2)):
                pe.wait_ge(s["sgm"], START["sgm"] + t["sgm"].now())
                block_units(xH, xL, KT, SETS[0], before=lambda q: pe.wait_ge(s["x_lo"], 8 + q + 1))
                pe.wait_ge(s["h_read"], START["h_read"] + t["h_read"].now())
                block_units(xH, xL, KT, SETS[1])
                t["sgm"].add(2)
                t["h_read"].add(2)
            project(hH, hL, FT, pairs=2, before=lambda q: pe.wait_ge(s["h_lo"], 4 * (q + 1)))
            ln_sum()
            ln_var(sq2)
            assert t["unit"].now() == N_UNITS, (t["unit"].now(), N_UNITS)

        @block.scalar
        def _(act):
            t = Tallies()

            def step(ins):
                ins.then_inc(act_step, 1)
                act.wait_ge(act_step, t["step"].add())

            def split(n):
                u = t["unit"]
                assert u.base % RING == 0 and (u.reg is None or u.per % RING == 0)
                for _ in range(n):
                    slot = u.k % RING
                    lap = u.base // RING + u.k // RING + 1
                    if u.reg is not None:
                        lap = u.reg * (u.per // RING) + lap
                    act.wait_ge(landed[slot], lap * 16)
                    act.wait_ge(used, u.add())
                    act.activation(whi[:, slot, :], raw[:, slot, :], ACT.Copy).then_inc(hi_ready, 1)

            def finished(units):
                act.wait_ge(used, t["done"].add(units) + RING)

            for c in range(4):
                act.wait_ge(in_x[c], 16)
                act.activation(flat(xH[:, 4 * c:4 * c + 4, :]), flat(resid[:, 4 * c:4 * c + 4, :]),
                               ACT.Copy).then_inc(s["x_hi"], 1)
                if c == 1:
                    split(1)
            split(3)

            def raws(outs):
                for j in range(2):
                    n = t["raw"]
                    if n.reg is not None or n.k >= 2:
                        act.wait_ge(s["conv_done"], n.now(1))
                    act.activation(R[:, n.k % 2, CONV_W - 1:CONV_W - 1 + T], outs[j][:, 0:T], ACT.Copy)\
                       .then_inc(s["raw_ready"], 1)
                    n.add()

            def silus(dests):
                for j in range(2):
                    c = t["conv"]
                    act.wait_ge(s["conv_done"], c.add())
                    act.activation(dests[j], cacc[:, (c.k - 1) % 2, :], ACT.Silu).then_inc(s["xbc_ready"], 1)

            def z_block(j):
                finished(4)
                for k in range(2):
                    act.activation(zs[:, 2 * j + k, :], SETS[j][k][:, 0:T], ACT.Silu).then_inc(s["z_ready"], 1)

            def heads(h0):
                for h in (h0, h0 + 1):
                    act.wait_ge(s["seg_ready"], START["seg_ready"] + t["e"].add())
                    act.activation(E[:, h % 2, :], E[:, h % 2, :], ACT.Exp).then_inc(s["e_ready"], 1)

            DESTS = [[BT[:, :], CTt[:, :]], [xs[:, 0, :], xs[:, 1, :]], [xs[:, 2, :], xs[:, 3, :]]]

            def raw_block(i):
                finished(4)
                raws(SETS[i])

            def group(last=False):
                split(2)
                act.wait_ge(s["btok_ps"], t["btok"].add())
                act.activation(flat(Btok[:, :, :]), M[2][:, 0:256], ACT.Copy).then_inc(s["btok_sb"], 1)
                act.activation(bcs[:, :], M[2][0:NSAMP, 256:384], ACT.Copy).then_inc(s["bc_rows"], 1)
                split(1)
                heads(0)
                split(1)
                heads(2)
                z_block(0)
                split(1)
                heads(4)
                split(1)
                heads(6)
                split(2)
                z_block(1)
                split(3)
                for i in range(XPG):
                    act.wait_ge(s["y2_ready"], t["y2"].add())
                    act.activation(zs[:, i, :], yg[:, i, :], ACT.Square).then_inc(s["sq_ready"], 1)
                split(1)
                if not last:
                    raw_block(0)
                act.wait_ge(s["fst_free"], t["fo"].add())
                act.wait_ge(s["st_ps"], t["st"].add())
                act.activation(fst[:, :], M[2][:, :], ACT.Copy).then_inc(s["fst_ready"], 1)
                if not last:
                    silus(DESTS[0])
                split(4)
                if not last:
                    raw_block(1)
                act.wait_ge(s["rms_ps"], t["rms"].add())
                act.activation(rstd, M[0][:, 0:T], ACT.Sqrt, scale=1.0 / (XPG * P), bias=eps[:, 0:1])\
                   .then_inc(s["sd_ready"], 1)
                split(1)
                if not last:
                    silus(DESTS[1])
                split(1)
                for i in range(XPG):
                    act.wait_ge(s["y3_ready"], t["y3"].add())
                    yt = t["g"].now() * XPG + i
                    dst = yH[:, yt:yt + 1, :] if isinstance(yt, int) else yH[:, bass.ds(yt, 1), :]
                    act.activation(flat(dst), yg[:, i, :], ACT.Copy).then_inc(s["yh_ready"], 1)
                if not last:
                    split(2)
                    raw_block(2)
                    silus(DESTS[2])
                t["g"].add()

            act.wait_ge(in_misc, N_MISC * 16)
            step(act.activation(pcol[:, 2:3], pcol[:, 1:2], ACT.Exp))
            split(4)
            raw_block(0)
            silus(DESTS[0])
            act.wait_ge(s["dt_z"], 1)
            step(act.activation(S[:, 3, :], S[:, 2, :], ACT.Abs))
            act.activation(S[:, 4, :], S[:, 3, :], ACT.Exp, scale=-1.0).then_inc(s["dt_exp"], 1)
            split(1)
            act.wait_ge(s["dt_u"], 1)
            act.activation(S[:, 6, :], S[:, 5, :], ACT.Ln).then_inc(s["dt_ln"], 1)
            split(1)
            act.wait_ge(s["dt_ready"], 1)
            act.activation(pxs[:, NSAMP:2 * NSAMP], S[:, 0, SEQ:T], ACT.Exp).then_inc(s["pre_exp"], 1)
            split(2)
            raw_block(1)
            silus(DESTS[1])
            split(4)
            act.wait_ge(s["w_sum"], 1)
            act.activation(flat(wtok[:, :, :]), flat(wtok[:, :, :]), ACT.Exp).then_inc(s["pre_done"], 1)
            raw_block(2)
            silus(DESTS[2])
            with rounds(act, GROUPS - 1, t, dict(unit=20, done=20, raw=6, conv=6, e=8, g=1, btok=1,
                                                 fo=1, st=1, y2=4, rms=1, y3=4)):
                group()
            group(last=True)

            pending = []

            def high(n):
                for _ in range(n):
                    item, tile, ready, count = pending.pop(0)
                    act.wait_ge(s[ready], count)
                    act.activation(mixH[:, tile, :], tmp[:, item % 4, :], ACT.Copy).then_inc(s["mix_hi"], 1)

            t["pu"].k = 14
            for e in EVENTS:
                n = max(0, e.end + 4 - t["pu"].k)
                split(n)
                t["pu"].add(n)
                if e.kind == "in":
                    finished(4)
                    if e.i == 0:
                        act.wait_ge(s["st_used"], GROUPS * NSAMP)
                    if e.i >= 2:
                        act.wait_ge(s["pool_f"], 2 * (e.i - 1))
                    for j in range(2):
                        act.activation(U[:, e.i % 2, j, POOL_HIST:UT], SETS[e.blocks[0] % 4][j][:, 0:T], ACT.Copy)\
                           .then_inc(s["uraw"], 1)
                    if e.i == 0:
                        act.wait_ge(s["tails_out"], 16)
                        act.wait_ge(s["fst_free"], GROUPS + 1)
                else:
                    t["done"].add(2)
                high(len(pending))
                for j in range(e.tiles):
                    if e.kind == "in":
                        pending.append((e.item + j, 2 * e.i + j, "pool_f", 2 * e.i + j + 1))
                    else:
                        pending.append((e.item + j, 4 * e.i + j, "wp_ready", 4 * e.i + j + 1))
                if e.kind == "proj":
                    high(len(pending))
            assert not pending
            for br in range(2):
                extra = 4 * br
                with rounds(act, 8, t, dict(unit=8 + extra, done=8 + extra, br=2, **({"mf": 2} if br else {}))):
                    split(4)
                    finished(4)
                    act.wait_ge(s["br_read"], START["br_read"] + t["br"].now())
                    for j in range(2):
                        act.activation(sgA[:, j, :], SETS[0][j][:, 0:T], ACT.Sigmoid).then_inc(s["sgm"], 1)
                    t["br"].add(2)
                    split(4 + extra)
                    t["done"].add(4 + extra)
                    if br:
                        i = t["mf"].now()
                        for j in range(2):
                            act.wait_ge(s["br_read"], START["br_read"] + t["br"].now(1 - j))
                            act.activation(flat(mixH[:, bass.ds(i + j, 1), :]), tmp[:, j, :], ACT.Copy)\
                               .then_inc(s["mix_hi"], 1)
                        t["mf"].add(2)
            for b in range(8):
                split(4)
                t["done"].add(4)
                if b % 2:
                    c = b // 2
                    act.wait_ge(s[f"mem_in{c % 2}"], 16 * (c // 2) + 16)
                    act.activation(flat(memH[:, 4 * c:4 * c + 4, :]), memraw[:, c % 2, :], ACT.Copy)\
                       .then_inc(s["mem_hi"], 1)

            def ln_stats(sqb, meanb):
                act.wait_ge(s["ln_sum"], t["ln"].add())
                act.activation(meanb[:, :], M[0][:, 0:T], ACT.Copy, scale=1.0 / D_MODEL).then_inc(s["mean_ready"], 1)
                for c in range(4):
                    act.wait_ge(s["cen_ready"], t["cen"].add())
                    if t["sqc"].k >= 2:
                        act.wait_ge(s["sqc_used"], t["sqc"].k - 1)
                    act.activation(sqb[:, c % 2, :], flat(resid[:, 4 * c:4 * c + 4, :]), ACT.Square)\
                       .then_inc(s["sqc_ready"], 1)
                    t["sqc"].add()

            def ln_sd(rb):
                act.wait_ge(s["sqc_used"], t["var"].add(4))
                act.activation(rb[:, :], M[1][:, 0:T], ACT.Sqrt, scale=1.0 / D_MODEL, bias=eps[:, 1:2])\
                   .then_inc(s["lsd_ready"], 1)

            def ln_high(c):
                act.wait_ge(s["xn_ready"], t["xn"].add())
                act.activation(flat(xH[:, 4 * c:4 * c + 4, :]), flat(resid[:, 4 * c:4 * c + 4, :]), ACT.Copy)\
                   .then_inc(s["x_hi"], 1)

            def keys(b):
                finished(4)
                for j in range(2):
                    act.activation(KTm[:, 2 * b + j, :], SETS[b][j][:, 0:N_MEM], ACT.Copy).then_inc(s["kt_ready"], 1)

            def values(b):
                finished(4)
                for m in range(2):
                    act.activation(Vn[:, m, b * BLK:b * BLK + BLK], SETS[1 - b][m][:, 0:BLK], ACT.Copy)\
                       .then_inc(s["vn_ready"], 1)

            def queries(b):
                finished(4)
                for j in range(2):
                    act.activation(qT[:, 2 * b + j, :], SETS[2 - 2 * b][j][:, 0:T], ACT.Copy).then_inc(s["q_ready"], 1)

            ln_stats(sq, mean)
            split(4)
            ln_sd(lrstd)
            ln_high(0)
            ln_high(1)
            keys(0)
            split(4)
            ln_high(2)
            ln_high(3)
            keys(1)
            split(4)
            queries(0)
            split(4)
            queries(1)

            def exps(h):
                act.wait_ge(s["mx_ready"], h + 1)
                for b in range(2):
                    n = 2 * h + b
                    act.activation(Pe[:, n, :], M[h][:, b * N_MEM:b * N_MEM + N_MEM], ACT.Exp, bias=snm[:, n:n + 1],
                                   scale=MHD ** -0.5, accum_out=srs[:, n:n + 1]).then_inc(s["p_ready"], 1)

            for h in range(MH):
                exps(h)
            act.wait_ge(s["ss_ps"], 1)
            act.activation(flat(ssT[:, :, :]), G[0][0][:, 0:64], ACT.Copy).then_inc(s["ss_sb"], 1)
            split(1)
            act.wait_ge(s["smx_ready"], 1)
            act.activation(sP[:, :], G[0][1][0:32, 0:N_MEM], ACT.Exp, bias=snm[0:32, 8:9],
                           scale=MHD ** -0.5, accum_out=srs[0:32, 8:9]).then_inc(s["sp_exp"], 1)
            split(3)
            values(0)
            split(4)
            values(1)
            for h in range(MH):
                act.wait_ge(s["pt_ps"], h + 1)
                if h >= 2:
                    act.wait_ge(s["o_ps"], h - 1)
                act.activation(PT[:, h % 2, :], G[1][h % 2][:, :], ACT.Copy).then_inc(s["pt_ready"], 1)
                if h == 0:
                    act.wait_ge(s["spt_ps"], 1)
                    act.activation(flat(sPT[:, :, :]), G[0][0][:, 0:64], ACT.Copy).then_inc(s["spt_sb"], 1)
                if h >= 1:
                    act.wait_ge(s["o_ps"], h)
                    act.activation(oH[:, h - 1, 0:SEQ], M[h - 1][:, 0:SEQ], ACT.Copy).then_inc(s["o_hi"], 1)
            act.wait_ge(s["so_ps"], 1)
            act.activation(oH[:, :, SEQ:T], G[0][1][:, 0:MH * NSAMP].rearrange("p (h b) -> p h b", h=MH), ACT.Copy)\
               .then_inc(s["o_hi"], 1)
            act.wait_ge(s["o_ps"], MH)
            act.activation(oH[:, MH - 1, 0:SEQ], M[MH - 1][:, 0:SEQ], ACT.Copy).then_inc(s["o_hi"], 1)
            split(7)
            t["done"].add(8)
            act.wait_ge(s["kv_out"], 32)
            ln_stats(sq2, mean2)
            split(1)
            ln_sd(lrstd2)
            for c in range(4):
                ln_high(c)
            def outers(r, c):
                act.wait_ge(s[f"b_in{c}"], t[f"b_in{c}"].add() * 16)
                for b in range(2):
                    act.wait_ge(s["st_done"], t["std"].add() + START["st_done"] - 2)
                    for i in range(XPG):
                        col = dtxc[:, bass.ds(r * 4 + (2 * c + b), 1), i:i + 1].rearrange("p a b -> p (a b)")
                        last = act.activation(outer[:, b, i, :], bcb[:, c, b * P:b * P + P], ACT.Copy, scale=col)
                    last.then_inc(s["out_ready"], 1)

            for n, with_states in ((16, True), (FT // 2 - 16, False)):
                extra = dict(std=4, b_in0=1, b_in1=1) if with_states else {}
                with rounds(act, n, t, dict(unit=8, done=8, h=2, **extra)) as r:
                    split(4)
                    if with_states:
                        outers(r, 0)
                    finished(4)
                    act.wait_ge(s["h_read"], START["h_read"] + t["h"].now())
                    for j in range(2):
                        act.activation(sgF[:, j, :], SETS[0][j][:, 0:T], ACT.Silu).then_inc(s["sgm"], 1)
                    split(4)
                    if with_states:
                        outers(r, 1)
                    t["done"].add(4)
                    i = t["h"].now()
                    for j in range(2):
                        act.wait_ge(s["h_read"], START["h_read"] + t["h"].add())
                        act.activation(flat(hH[:, bass.ds(i + j, 1), :]), hf[:, j, :], ACT.Copy).then_inc(s["h_hi"], 1)
            for b in range(8):
                split(11 if b < 7 else 7)
            act.wait_ge(s["st_out0"], 16 * 16)
            act.wait_ge(s["st_out1"], 16 * 16)
            ln_stats(sq2, mean2)
            ln_sd(lrstd2)

        @block.vector
        def _(dve):
            t = Tallies()

            def step(ins):
                ins.then_inc(dve_step, 1)
                dve.wait_ge(dve_step, t["step"].add())

            def mark(ins):
                ins.then_inc(dve_step, 1)
                return t["step"].add()

            def after(count):
                dve.wait_ge(dve_step, count)

            def split(n):
                u = t["unit"]
                for _ in range(n):
                    slot = u.k % RING
                    dve.wait_ge(hi_ready, u.add())
                    dve.tensor_tensor(wlo[:, slot, :], raw[:, slot, :], whi[:, slot, :].bitcast(F32), ALU.subtract)\
                       .then_inc(lo_ready, 1)

            def finished(units):
                dve.wait_ge(used, t["done"].add(units) + RING)

            dve.memset(eps[:, 0:1], RMS_EPS)
            dve.memset(eps[:, 1:2], LN_EPS)
            dve.memset(R[:, :, 0:CONV_W - 1], 0.0)
            dve.memset(ones[:, :], 1.0).then_inc(s["ones_set"], 1)
            dve.sem_inc(lo_ready, RING)
            for c in range(4):
                dve.wait_ge(s["x_hi"], c + 1)
                dve.tensor_tensor(flat(xL[:, 4 * c:4 * c + 4, :]), flat(resid[:, 4 * c:4 * c + 4, :]),
                                  flat(xH[:, 4 * c:4 * c + 4, :]).bitcast(F32), ALU.subtract).then_inc(s["x_lo"], 1)
                if c == 1:
                    split(1)
            split(3)

            def conv_block():
                n = t["raw"]
                if n.reg is not None or n.k >= 2:
                    dve.wait_ge(s["xbc_ready"], n.now())
                idx = [n.now() + j for j in range(2)]
                ct = lambda x, j: x[:, idx[j], :] if isinstance(idx[j], int) else flat(x[:, bass.ds(idx[j], 1), :])
                w = lambda k, j: vcol("conv_w", idx[j] * CONV_W + k)
                marks = []
                for j in range(2):
                    dve.wait_ge(s["raw_ready"], n.add())
                    marks.append(mark(dve.tensor_scalar(cacc[:, j, :], R[:, j, CONV_W - 1:CONV_W - 1 + T],
                                                        w(CONV_W - 1, j), vcol("conv_b", idx[j]), ALU.mult, ALU.add)))
                for j in range(2):
                    dve.tensor_copy(ct(tails, j), R[:, j, SEQ:SEQ + 11])
                for j in range(2):
                    after(marks[j])
                    last = dve.tensor_tensor(cacc[:, j, SEQ:T], cacc[:, j, SEQ:T], ct(chist, j), ALU.add)
                for k in range(CONV_W - 1):
                    for j in range(2):
                        if k:
                            after(marks[j])
                        ins = dve.scalar_tensor_tensor(out=cacc[:, j, 0:SEQ], in0=R[:, j, k:k + SEQ], scalar=w(k, j),
                                                       in1=cacc[:, j, 0:SEQ], op0=ALU.mult, op1=ALU.add)
                        if k < CONV_W - 2:
                            marks[j] = mark(ins)
                        else:
                            ins.then_inc(s["conv_done"], 1)

            dve.wait_ge(in_misc, N_MISC * 16)
            cw = vec[:, 0:CT * CONV_W].rearrange("p (c k) -> p c k", k=CONV_W)
            hv = hist[:, :, :].rearrange("p c (b k) -> p c b k", k=CONV_W - 1)
            for k in range(CONV_W - 1):
                dst = chist if k == 0 else ctmp
                step(dve.tensor_tensor(dst[:, :, :], hv[:, :, :, k], cw[:, :, k:k + 1].to_broadcast([P, CT, NSAMP]), ALU.mult))
                if k:
                    step(dve.tensor_tensor(chist[:, :, :], chist[:, :, :], ctmp[:, :, :], ALU.add))
            split(4)
            for g, w in enumerate(WINDOWS):
                last = dve.tensor_reduce(phs[:, 4 * g:4 * g + 4, :], hpool[:, 4 * g:4 * g + 4, :, POOL_HIST - (w - 1):POOL_HIST],
                                         AX_X, ALU.add)
            step(last)
            finished(4)
            conv_block()
            dve.wait_ge(s["dt_psum"], 1)
            dve.tensor_scalar(S[:, 2, :], M[0][0:HEADS, 0:T], pcol[:, 0:1], None, ALU.add).then_inc(s["dt_z"], 1)
            step(dve.tensor_scalar(pcol[:, 3:4], pcol[:, 2:3], -1.0, None, ALU.mult))
            dve.wait_ge(s["dt_exp"], 1)
            dve.tensor_scalar(S[:, 5, :], S[:, 4, :], 1.0, None, ALU.add).then_inc(s["dt_u"], 1)
            dve.wait_ge(s["dt_u"], 1)
            step(dve.tensor_scalar(S[:, 3, :], S[:, 5, :], -1.0, 1e-30, ALU.add, ALU.max))
            step(dve.reciprocal(S[:, 7, :], S[:, 3, :]))
            split(1)
            step(dve.tensor_tensor(S[:, 3, :], S[:, 7, :], S[:, 4, :], ALU.mult))
            dve.wait_ge(s["dt_ln"], 1)
            step(dve.tensor_tensor(S[:, 7, :], S[:, 3, :], S[:, 6, :], ALU.mult))
            step(dve.scalar_tensor_tensor(out=S[:, 3, :], in0=S[:, 5, :], scalar=1.0, in1=S[:, 4, :],
                                          op0=ALU.is_equal, op1=ALU.mult))
            step(dve.tensor_tensor(S[:, 6, :], S[:, 7, :], S[:, 3, :], ALU.add))
            step(dve.scalar_tensor_tensor(out=S[:, 7, :], in0=S[:, 2, :], scalar=0.0, in1=S[:, 6, :],
                                          op0=ALU.max, op1=ALU.add))
            step(dve.tensor_copy(pxs[:, 0:NSAMP], S[:, 7, SEQ:T]))
            dve.tensor_scalar(S[:, 0, :], S[:, 7, :], pcol[:, 3:4], None, ALU.mult).then_inc(s["dt_ready"], 1)
            split(3)
            finished(4)
            conv_block()
            dve.wait_ge(s["dA_tok_ps"], 1)
            dve.tensor_copy(flat(dAtok[:, :, :]), M[1][:, 0:2 * HEADS]).then_inc(s["dA_tok"], 1)
            dve.tensor_copy(flat(dttok[:, :, :]), M[1][:, P:P + 2 * HEADS]).then_inc(s["dA_tok"], 1)
            split(2)
            dve.wait_ge(s["cum_ps"], 1)
            dve.tensor_copy(S[:, 1, 0:SEQ], M[0][0:HEADS, 0:SEQ]).then_inc(s["cum_sb"], 1)
            split(2)
            dve.wait_ge(s["cumt_ps"], 1)
            step(dve.tensor_scalar(flat(ncum[:, :, :]), M[1][:, 256:256 + 2 * HEADS], -1.0, None, ALU.mult))
            dve.tensor_tensor(wtok[:, 0, :], ncum[:, 0, :], M[0][:, 384:384 + HEADS], ALU.add)
            dve.tensor_tensor(wtok[:, 1, :], ncum[:, 1, :], M[0][:, 384:384 + HEADS], ALU.add).then_inc(s["w_sum"], 1)
            finished(4)
            conv_block()

            def heads(h0):
                if h0 == 0:
                    dve.wait_ge(s["cum_in"], t["cum"].add() * 16)
                for h in (h0, h0 + 1):
                    if h >= 2:
                        dve.wait_ge(s["m_ready"], t["m"].now(1 - h % 2))
                    hc = t["g"].now() * HPG + h
                    n = [ncum[:, b, hc:hc + 1] if isinstance(hc, int) else ncum[:, b, bass.ds(hc, 1)] for b in range(2)]
                    dve.tensor_scalar(E[:, h % 2, 0:SEQ], cumbc[:, h, :], n[0], 0.0, ALU.add, ALU.min)
                    dve.tensor_scalar(E[:, h % 2, SEQ:384], cumbc[:, h, P:SEQ], n[1], 0.0, ALU.add, ALU.min)\
                       .then_inc(s["seg_ready"], 1)
                for h in (h0, h0 + 1):
                    m = t["m"]
                    if h >= 3:
                        dve.wait_ge(s["y_done"], m.now(2))
                    dve.wait_ge(s["e_ready"], m.add())
                    dve.tensor_tensor(MM[:, h % 3, :], E[:, h % 2, :], cbm[:, :], ALU.mult).then_inc(s["m_ready"], 1)

            def group(last=False):
                gh = t["g"].now() * HPG
                gx = t["g"].now() * XPG
                per_head = (lambda x, b: x[:, b, gh:gh + HPG]) if isinstance(gh, int) else (
                    lambda x, b: x[:, b, bass.ds(gh, HPG)])
                split(2)
                dve.wait_ge(s["xtok_ps"], t["xtok"].add())
                dve.tensor_tensor(bcp[:, :], BT[:, SEQ:T], CTt[:, SEQ:T], ALU.mult).then_inc(s["bcp_ready"], 1)
                for b in range(2):
                    dve.tensor_tensor(xdt[:, b, :].rearrange("p (h c) -> p h c", h=HPG),
                                      M[b][:, :].rearrange("p (h c) -> p h c", h=HPG),
                                      per_head(dttok, b).rearrange("p (h o) -> p h o", o=1).to_broadcast([P, HPG, 64]),
                                      ALU.mult).then_inc(s["xdt_ready"], 1)
                dve.wait_ge(s["cb_ps"], t["cb"].add())
                step(dve.tensor_tensor(cbm[:, :], M[3][:, 0:384], cmask[:, :], ALU.mult))
                split(1)
                heads(0)
                split(1)
                heads(2)
                split(1)
                heads(4)
                split(1)
                heads(6)
                split(2)
                t["done"].add(8)
                dve.wait_ge(s["y_done"], t["m"].now())
                for b in range(2):
                    ins = dve.tensor_tensor(xdt[:, b, :].rearrange("p (h c) -> p h c", h=HPG),
                                            xdt[:, b, :].rearrange("p (h c) -> p h c", h=HPG),
                                            per_head(wtok, b).rearrange("p (h o) -> p h o", o=1).to_broadcast([P, HPG, 64]),
                                            ALU.mult)
                ins.then_inc(s["xw_ready"], 1)
                sl = dts[:, gx:gx + XPG, :] if isinstance(gx, int) else dts[:, bass.ds(gx, XPG), :]
                step(dve.tensor_tensor(dtx[:, :, :], sl[:, :, 0:NSAMP], xs[:, :, SEQ:T], ALU.mult))
                gb = t["g"].now() * NSAMP
                kept = dtxc[:, gb:gb + NSAMP, :] if isinstance(gb, int) else dtxc[:, bass.ds(gb, NSAMP), :]
                dve.tensor_copy(kept.rearrange("p b i -> p i b"), dtx[:, :, :])
                dve.wait_ge(s["ys_ps"], t["ysp"].add())
                dve.tensor_tensor(ysbc[:, :, :], dtx[:, :, :], M[3][:, 416:416 + NSAMP].rearrange(
                    "p (o b) -> p o b", o=1).to_broadcast([P, XPG, NSAMP]), ALU.mult)
                step(dve.tensor_tensor(ysamp[:, :, :], sl[:, :, NSAMP:2 * NSAMP], M[3][:, 384:384 + XPG * NSAMP].rearrange(
                    "p (i b) -> p i b", b=NSAMP), ALU.mult))
                ys = mark(dve.tensor_tensor(ysamp[:, :, :], ysamp[:, :, :], ysbc[:, :, :], ALU.add))
                for i in range(XPG):
                    split(1)
                    if i < 2:
                        for k in (2 * i, 2 * i + 1):
                            dve.scalar_tensor_tensor(out=yg[:, k, 0:SEQ], in0=xs[:, k, 0:SEQ], scalar=vcol("d_skip", gx + k),
                                                     in1=M[k // 2][:, (k % 2) * SEQ:(k % 2) * SEQ + SEQ], op0=ALU.mult,
                                                     op1=ALU.add)
                    if i == 1:
                        after(ys)
                        for k in range(XPG):
                            ins = dve.scalar_tensor_tensor(out=yg[:, k, SEQ:T], in0=xs[:, k, SEQ:T],
                                                           scalar=vcol("d_skip", gx + k), in1=ysamp[:, k, :],
                                                           op0=ALU.mult, op1=ALU.add)
                        yd = mark(ins)
                    if i == 2:
                        dve.wait_ge(s["z_ready"], t["z"].add(XPG))
                        after(yd)
                        for k in range(XPG):
                            dve.tensor_tensor(yg[:, k, :], yg[:, k, :], zs[:, k, :], ALU.mult).then_inc(s["y2_ready"], 1)
                if not last:
                    t["done"].add(4)
                    conv_block()
                split(4)
                if not last:
                    t["done"].add(4)
                    conv_block()
                split(1)
                dve.wait_ge(s["sd_ready"], t["sd"].add())
                rs = mark(dve.reciprocal(rstd, rstd))
                split(1)
                after(rs)
                for i in range(XPG):
                    dve.scalar_tensor_tensor(out=yg[:, i, :], in0=yg[:, i, :], scalar=vcol("norm_w", gx + i),
                                             in1=rstd, op0=ALU.mult, op1=ALU.mult).then_inc(s["y3_ready"], 1)
                if not last:
                    split(1)
                for i in range(XPG):
                    dve.wait_ge(s["yh_ready"], t["yh"].add())
                    one = (lambda x: x[:, gx + i, :]) if isinstance(gx, int) else (lambda x: flat(x[:, bass.ds(gx + i, 1), :]))
                    dve.tensor_tensor(one(yL), yg[:, i, :], one(yH).bitcast(F32), ALU.subtract).then_inc(s["yl_ready"], 1)
                if not last:
                    split(1)
                    t["done"].add(4)
                    conv_block()
                t["g"].add()

            dve.wait_ge(s["dts_in"], 32)
            dve.tensor_copy(decc[:, :, :].rearrange("p (g b) i -> p g i b", g=GROUPS),
                            dts[:, :, NSAMP:2 * NSAMP].rearrange("p (g i) b -> p g i b", g=GROUPS))
            with rounds(dve, GROUPS - 1, t, dict(unit=20, done=20, raw=6, m=8, g=1, xtok=1, cb=1, ysp=1,
                                                 z=4, sd=1, yh=4, cum=1, step=STEPS)):
                group()
            group(last=True)
            dve.wait_ge(s["tails_out"], 16)
            dve.wait_ge(s["yl_ready"], YT)
            dve.wait_ge(s["st_used"], GROUPS * NSAMP)
            last = dve.memset(U[:, :, :, 0:POOL_HIST], 0.0)
            step(last)
            pending = []

            def low(n):
                for _ in range(n):
                    item, tile, ready, count = pending.pop(0)
                    dve.wait_ge(s["mix_hi"], item + 1)
                    dve.tensor_tensor(mixL[:, tile, :], tmp[:, item % 4, :], mixH[:, tile, :].bitcast(F32),
                                      ALU.subtract).then_inc(s["mix_lo"], 1)

            def pool_pair(e):
                g, w = e.i // 2, WINDOWS[e.i // 2]
                out = [tmp[:, (e.item + j) % 4, :] for j in range(2)]
                cur, reach, marks = [U[:, e.i % 2, j, :] for j in range(2)], 1, [None, None]
                src = list(cur)
                for j in range(2):
                    dve.wait_ge(s["uraw"], 2 * e.i + j + 1)
                    dve.tensor_copy(utail[:, 2 * e.i + j, :], src[j][:, SEQ:UT])
                if e.i:
                    dve.wait_ge(s["pool_f"], 2 * e.i)
                while reach < w:
                    for j in range(2):
                        v = V[:, (reach.bit_length() - 1) % 2, j, :]
                        if marks[j] is not None:
                            after(marks[j])
                        marks[j] = mark(dve.tensor_tensor(v[:, 2 * reach - 1:POOL_HIST + SEQ],
                                                          cur[j][:, 2 * reach - 1:POOL_HIST + SEQ],
                                                          cur[j][:, reach - 1:POOL_HIST + SEQ - reach], ALU.add))
                        cur[j] = v
                    reach *= 2
                for j in range(2):
                    after(marks[j])
                    dve.tensor_tensor(cur[j][:, POOL_HIST + SEQ:UT], src[j][:, POOL_HIST + SEQ:UT],
                                      phs[:, 2 * e.i + j, :], ALU.add)
                    marks[j] = mark(dve.tensor_tensor(out[j][:, 0:16], cur[j][:, POOL_HIST:POOL_HIST + 16], rc[:, g, :],
                                                      ALU.mult))
                for j in range(2):
                    after(marks[j])
                    marks[j] = mark(dve.tensor_tensor(out[j][:, 0:16], out[j][:, 0:16], src[j][:, POOL_HIST:POOL_HIST + 16],
                                                      ALU.subtract))
                for j in range(2):
                    dve.scalar_tensor_tensor(out=out[j][:, 16:T], in0=cur[j][:, POOL_HIST + 16:UT], scalar=1.0 / w,
                                             in1=src[j][:, POOL_HIST + 16:UT], op0=ALU.mult, op1=ALU.subtract)\
                       .then_inc(s["pool_f"], 1)

            t["pu"].k = 14
            for e in EVENTS:
                n = max(0, e.end + 4 - t["pu"].k)
                split(n)
                t["pu"].add(n)
                t["done"].add(e.end - (EVENTS[EVENTS.index(e) - 1].end if e.item else 0))
                low(max(0, len(pending) + e.tiles - 4))
                if e.item >= 4:
                    dve.wait_ge(s["mix_lo"], e.item + e.tiles - 4)
                if e.kind == "in":
                    pool_pair(e)
                    low(len(pending))
                    pending += [(e.item + j, 2 * e.i + j, None, None) for j in range(2)]
                else:
                    dve.wait_ge(used, t["done"].now() + RING)
                    for j in range(4):
                        dve.tensor_scalar(tmp[:, (e.item + j) % 4, :], SETS[e.blocks[j // 2] % 4][j % 2][:, 0:T],
                                          vcol("pool_scale", 4 * e.i + j), None, ALU.mult).then_inc(s["wp_ready"], 1)
                    pending += [(e.item + j, 4 * e.i + j, None, None) for j in range(4)]
                    low(4)
            low(len(pending))
            for br in range(2):
                extra = 4 * br
                with rounds(dve, 8, t, dict(unit=8 + extra, done=8 + extra, sg=2, br=2,
                                            **({"step": 2, "mh": 2} if br else {}))):
                    split(8 + extra)
                    i = t["br"].now() if br == 0 else t["mh"].now()
                    dve.wait_ge(s["sgm"], START["sgm"] + t["sg"].add(2))
                    finished(8 + extra)
                    for j in range(2):
                        r = flat(resid[:, bass.ds(i + j, 1), :])
                        if br == 0:
                            dve.tensor_tensor(r, SETS[1][j][:, 0:T], sgA[:, j, :], ALU.mult).then_inc(s["br_read"], 1)
                            t["br"].add()
                        else:
                            step(dve.tensor_tensor(tmp[:, j, :], SETS[1][j][:, 0:T], sgA[:, j, :], ALU.mult))
                            dve.tensor_tensor(tmp[:, j, :], tmp[:, j, :], r, ALU.add).then_inc(s["br_read"], 1)
                            t["br"].add()
                    if br:
                        for j in range(2):
                            dve.wait_ge(s["mix_hi"], t["mh"].add() + 2 * KT)
                            m = lambda x: flat(x[:, bass.ds(i + j, 1), :])
                            dve.tensor_tensor(m(mixL), tmp[:, j, :], m(mixH).bitcast(F32), ALU.subtract)\
                               .then_inc(s["mix_lo"], 1)

            def residual(b, units, sets=2, parts=False):
                finished(units)
                marks = []
                for j in range(2):
                    k = 2 * b + j
                    x = xH[:, k, :].bitcast(F32) if parts else resid[:, k, :]
                    ins = dve.scalar_tensor_tensor(out=resid[:, k, :], in0=x, scalar=ALPHA, in1=SETS[b % sets][j][:, 0:T],
                                                   op0=ALU.mult, op1=ALU.add)
                    if parts:
                        marks.append(mark(ins))
                    else:
                        ins.then_inc(s["res_ready"], 1)
                for j in range(2):
                    k = 2 * b + j
                    if parts:
                        after(marks[j])
                        dve.scalar_tensor_tensor(out=resid[:, k, :], in0=xL[:, k, :].bitcast(F32), scalar=ALPHA,
                                                 in1=resid[:, k, :], op0=ALU.mult, op1=ALU.add).then_inc(s["res_ready"], 1)
                t["rr"].add(2)
                for j in range(b == 0, 2):
                    dve.wait_ge(s["res_ready"], t["rr"].now(1 - j) + START["res_ready"])
                    if b or j == 0:
                        after(t["step"].now())
                    ins = dve.tensor_tensor(total[:, :], total[:, :] if b else resid[:, 0, :], resid[:, 2 * b + j, :], ALU.add)
                    if b == 7 and j == 1:
                        ins.then_inc(s["sum_ready"], 1)
                    else:
                        mark(ins)

            for b in range(8):
                split(4)
                residual(b, 4, parts=True)
                if b % 2:
                    c = b // 2
                    dve.wait_ge(s["mem_hi"], c + 1)
                    dve.tensor_tensor(flat(memL[:, 4 * c:4 * c + 4, :]), memraw[:, c % 2, :],
                                      flat(memH[:, 4 * c:4 * c + 4, :]).bitcast(F32), ALU.subtract).then_inc(s["mem_lo"], 1)

            def chunk(c):
                return resid[:, 4 * c:4 * c + 4, :]

            def spread(v):
                return v[:, :].rearrange("p (o t) -> p o t", o=1).to_broadcast([P, 4, T])

            def ln_center(meanb):
                dve.wait_ge(s["mean_ready"], t["mean"].add())
                for c in range(4):
                    dve.tensor_tensor(chunk(c), chunk(c), spread(meanb), ALU.subtract).then_inc(s["cen_ready"], 1)

            def ln_rstd(rb):
                dve.wait_ge(s["lsd_ready"], t["lsd"].add())
                step(dve.reciprocal(rb[:, :], rb[:, :]))

            def ln_scale(c, rb, which, low=True):
                step(dve.tensor_tensor(chunk(c), chunk(c), spread(rb), ALU.mult))
                for k in range(4 * c, 4 * c + 4):
                    last = dve.tensor_scalar(resid[:, k, :], resid[:, k, :], vcol(f"ln_{which}_g", k), vcol(f"ln_{which}_b", k),
                                             ALU.mult, ALU.add)
                last.then_inc(s["xn_ready"], 1)

            def ln_low(c):
                dve.wait_ge(s["x_hi"], t["xh"].add() + 4)
                dve.tensor_tensor(flat(xL[:, 4 * c:4 * c + 4, :]), flat(chunk(c)),
                                  flat(xH[:, 4 * c:4 * c + 4, :]).bitcast(F32), ALU.subtract).then_inc(s["x_lo"], 1)

            ln_center(mean)
            split(4)
            ln_rstd(lrstd)
            ln_scale(0, lrstd, "mix")
            ln_scale(1, lrstd, "mix")
            ln_low(0)
            ln_low(1)
            split(4)
            ln_scale(2, lrstd, "mix")
            ln_scale(3, lrstd, "mix")
            ln_low(2)
            ln_low(3)
            split(8)
            t["done"].add(16)
            for h in range(MH):
                dve.wait_ge(s["sc_ps"], h + 1)
                step(dve.tensor_reduce(smx[:, 2 * h:2 * h + 2], M[h][:, :].rearrange("p (b m) -> p b m", b=2), AX_X, ALU.max))
                dve.tensor_scalar(snm[:, 2 * h:2 * h + 2], smx[:, 2 * h:2 * h + 2], -MHD ** -0.5, None, ALU.mult)\
                   .then_inc(s["mx_ready"], 1)
            def normalised(h):
                for n in (2 * h, 2 * h + 1):
                    dve.wait_ge(s["p_ready"], n + 1)
                step(dve.reciprocal(sri[:, 2 * h:2 * h + 2], srs[:, 2 * h:2 * h + 2]))
                for n in (2 * h, 2 * h + 1):
                    dve.tensor_scalar(Pe[:, n, :], Pe[:, n, :], sri[:, n:n + 1], None, ALU.mult).then_inc(s["pn_ready"], 1)

            normalised(0)
            normalised(1)
            split(1)
            dve.wait_ge(s["sst_ps"], 1)
            step(dve.tensor_reduce(smx[0:32, 8:9], G[0][1][0:32, 0:N_MEM], AX_X, ALU.max))
            dve.tensor_scalar(snm[0:32, 8:9], smx[0:32, 8:9], -MHD ** -0.5, None, ALU.mult).then_inc(s["smx_ready"], 1)
            normalised(2)
            normalised(3)
            split(3)
            dve.wait_ge(s["sp_exp"], 1)
            step(dve.reciprocal(sri[0:32, 8:9], srs[0:32, 8:9]))
            dve.tensor_scalar(sP[:, :], sP[:, :], sri[0:32, 8:9], None, ALU.mult).then_inc(s["sp_n"], 1)
            split(4)
            t["done"].add(8)

            def output_low(h, n):
                dve.wait_ge(s["o_hi"], n)
                dve.tensor_tensor(oL[:, h, 0:SEQ], M[h][:, 0:SEQ], oH[:, h, 0:SEQ].bitcast(F32), ALU.subtract)\
                   .then_inc(s["o_lo"], 1)

            for h in range(MH - 1):
                output_low(h, h + 1)
            dve.wait_ge(s["o_hi"], MH)
            dve.tensor_tensor(oL[:, :, SEQ:T], G[0][1][:, 0:MH * NSAMP].rearrange("p (h b) -> p h b", h=MH),
                              oH[:, :, SEQ:T].bitcast(F32), ALU.subtract).then_inc(s["o_lo"], 1)
            output_low(MH - 1, MH + 1)
            for b in range(8):
                if b < 7:
                    split(1)
                residual(b, 1, sets=4)
            ln_center(mean2)
            split(1)
            ln_rstd(lrstd2)
            for c in range(4):
                ln_scale(c, lrstd2, "mem")
                ln_low(c)
            def states(r, c):
                dve.wait_ge(s[f"st_in{c}"], 16 * 2 * GROUPS + t[f"s_in{c}"].add() * 16)
                for b in range(2):
                    dve.wait_ge(s["out_ready"], t["out"].add())
                    for i in range(XPG):
                        col = decc[:, bass.ds(r * 4 + (2 * c + b), 1), i:i + 1].rearrange("p a b -> p (a b)")
                        ins = dve.scalar_tensor_tensor(out=st[:, c, b, i, :], in0=st[:, c, b, i, :], scalar=col,
                                                       in1=outer[:, b, i, :], op0=ALU.mult, op1=ALU.add)
                    ins.then_inc(s["st_done"], 1)

            for n, with_states in ((16, True), (FT // 2 - 16, False)):
                extra = dict(out=4, s_in0=1, s_in1=1) if with_states else {}
                with rounds(dve, n, t, dict(unit=8, done=8, sg=2, h=2, **extra)) as r:
                    split(4)
                    if with_states:
                        states(r, 0)
                    split(4)
                    if with_states:
                        states(r, 1)
                    finished(8)
                    dve.wait_ge(s["sgm"], START["sgm"] + t["sg"].add(2))
                    i = t["h"].now()
                    dve.wait_ge(s["h_hi"], START["h_hi"] + t["h"].now())
                    for j in range(2):
                        dve.tensor_tensor(hf[:, j, :], SETS[1][j][:, 0:T], sgF[:, j, :], ALU.mult).then_inc(s["h_read"], 1)
                    for j in range(2):
                        dve.wait_ge(s["h_hi"], START["h_hi"] + t["h"].add())
                        m = lambda x: flat(x[:, bass.ds(i + j, 1), :])
                        dve.tensor_tensor(m(hL), hf[:, j, :], m(hH).bitcast(F32), ALU.subtract).then_inc(s["h_lo"], 1)
            for b in range(8):
                split(11 if b < 7 else 7)
                residual(b, 11)
            ln_center(mean2)
            ln_rstd(lrstd2)
            for c in range(4):
                ln_scale(c, lrstd2, "ffn")


        @block.gpsimd
        def _(pool):
            t = Tallies()
            misc = ((ident[:, :], a["ident"]), (vec[:, :], a["vecs"]), (cmask[:, :], a["cmask"]),
                    (flat(rc[:, :, :]), a["rc"]), (flat(wdt[:, :, :]), a["wdt"]), (flat(hist[:, :, :]), a["hist"]),
                    (hpool[:, :, :, :].rearrange("p k b j -> p (k b j)"), a["hpool"]),
                    (pcol[:, 0:1], a["dt_bias"]), (pcol[:, 1:2], a["a_log"]))
            assert len(misc) == N_MISC
            for dst, src in misc:
                pool.dma_start(dst, src).then_inc(in_misc, 16)
            pool.dma_start(o["pass_conv"], a["state_conv"][:, 1:CONV_W - 1, :]).then_inc(s["outs"], 16)
            pool.dma_start(o["pass_pool"], a["state_pool"][:, 1:POOL_HIST, :]).then_inc(s["outs"], 16)
            pool.wait_ge(s["cum_sb"], 1)
            pool.dma_start(scr_cum, S[:, 1, 0:SEQ]).then_inc(s["scr_out"], 16)
            pool.wait_ge(s["pre_exp"], 1)
            pool.dma_start(scr_dts, pxs[:, :]).then_inc(s["scr_out"], 16)
            pool.wait_ge(s["scr_out"], 32)
            for half in range(2):
                src = scr_dts.rearrange("(t h) k -> h t k", h=2)[half:half + 1]
                pool.dma_start(dts[64 * half:64 * half + 64, :, :], src.to_broadcast([64, YT, 2 * NSAMP]))\
                    .then_inc(s["dts_in"], 16)

            def alone(semaphore, count):
                pool.wait_ge(semaphore, count)
                pool.sem_inc(s["pool_past"], 1)

            with rounds(pool, GROUPS, t, {}) as g:
                alone(s["seg_ready"], g * HPG + START["seg_ready"])
                pool.dma_start(flat(cumbc[:, :, :]), scr_cum[bass.ds(g * HPG, HPG), :].rearrange(
                    "(o h) l -> o (h l)", o=1).to_broadcast([P, HPG * SEQ])).then_inc(s["cum_in"], 16)

                def load_state(b):
                    pool.dma_start(stT[:, b % 4, :], a["state_T"][bass.ds(g * NSAMP + b, 1)].rearrange("g p c -> (g p) c"))\
                        .then_inc(s[f"st_in{b % 4}"], 16)

                for b in range(4):
                    load_state(b)
                alone(s["bc_rows"], g + 1)
                pool.dma_start(scr_bc[bass.ds(g * NSAMP, NSAMP), :], bcs[:, :]).then_inc(s["bc_out"], 16)
                for b in range(4, NSAMP):
                    alone(s["st_used"], g * NSAMP + (b - 3))
                    load_state(b)
                alone(s["fst_ready"], g + 1)
                pool.dma_start(o["new_ssd_p"][bass.ds(g, 1)].rearrange("g p c -> (g p) c"), fst[:, :])\
                    .then_inc(s["fst_out"], 16)
                alone(s["st_used"], g * NSAMP + NSAMP)
                alone(s["bc_out"], g * 16 + 16)
                alone(s["fst_out"], g * 16 + 16)
                pool.sem_inc(s["fst_free"], 1)
            pool.wait_ge(s["conv_done"], CT)
            pool.dma_start(o["tails"], flat(tails[:, :, :])).then_inc(s["tails_out"], 16)
            pool.wait_ge(s["pool_f"], KT)
            pool.dma_start(o["utail"], flat(utail[:, :, :])).then_inc(s["outs"], 16)
            pool.wait_ge(s["mix_lo"], 3 * KT)
            for c in range(4):
                if c >= 2:
                    pool.wait_ge(s["mem_lo"], c - 1)
                pool.dma_start(memraw[:, c % 2, :], a["memT"][:, c * 4 * N_MEM:(c + 1) * 4 * N_MEM])\
                    .then_inc(s[f"mem_in{c % 2}"], 16)
            pool.wait_ge(s["sum_ready"], 1)
            pool.wait_ge(s["outs"], 48)
            pool.dma_start(kc[:, :, :, :].rearrange("p b h m -> p (b h m)"), a["kc"]).then_inc(s["kc_in"], 16)
            pool.wait_ge(s["ss_ps"], 1)
            pool.dma_start(vc[:, :, :, :].rearrange("p b m d -> p (b m d)"), a["vc"]).then_inc(s["vc_in"], 16)
            pool.wait_ge(s["kt_ready"], MH)
            pool.dma_start(o["mem_k"], flat(KTm[:, :, :])).then_inc(s["kv_out"], 16)
            pool.wait_ge(s["vn_ready"], 4)
            pool.dma_start(o["mem_v"], flat(Vn[:, :, :])).then_inc(s["kv_out"], 16)
            pool.wait_ge(s["x_lo"], 12)
            def load_pair(r, c):
                pool.dma_start(st[:, c].rearrange("p b i n -> p (b i n)"),
                               a["state_ssd"][bass.ds(r * 2 + c, 1)].rearrange("g p c -> (g p) c"))\
                    .then_inc(s[f"st_in{c}"], 16)
                pool.dma_start(bcb[:, c, :], scr_bc[bass.ds(r * 4 + 2 * c, 2), :].rearrange(
                    "(o b) n -> o (b n)", o=1).to_broadcast([P, 2 * P])).then_inc(s[f"b_in{c}"], 16)

            def store_pair(r, c):
                pool.dma_start(o["new_ssd_s"][bass.ds(r * 2 + c, 1)].rearrange("g p c -> (g p) c"),
                               st[:, c].rearrange("p b i n -> p (b i n)")).then_inc(s[f"st_out{c}"], 16)

            for c in range(2):
                load_pair(0, c)
            with rounds(pool, 15, t, {}) as r:
                for c in range(2):
                    alone(s["st_done"], r * 4 + (2 * c + 2 + START["st_done"]))
                    store_pair(r, c)
                    alone(s[f"st_out{c}"], r * 16 + 16)
                    load_pair(r + 1, c)
            for c in range(2):
                pool.wait_ge(s["st_done"], 15 * 4 + 2 * c + 2 + START["st_done"])
                store_pair(15, c)
            for c in range(4):
                pool.wait_ge(s["xn_ready"], 8 + c + 1)
                pool.dma_start(o["yT"][:, c * 4 * T:(c + 1) * 4 * T], flat(resid[:, 4 * c:4 * c + 4, :]))\
                    .then_inc(s["outs"], 16)
            pool.wait_ge(s["outs"], 16 * 7)
            pool.wait_ge(s["scr_out"], 32)
            pool.wait_ge(s["bc_out"], 16 * GROUPS)
            pool.wait_ge(s["st_out0"], 16 * 16)
            pool.wait_ge(s["st_out1"], 16 * 16)
            pool.wait_ge(s["fst_out"], 16 * GROUPS)
            pool.wait_ge(s["tails_out"], 16)
            pool.wait_ge(s["kv_out"], 32)


def group_tiles(x, axis=-1):
    bc = D_INNER // P
    order = [t for g in range(GROUPS) for t in (bc + g, bc + GROUPS + g, *range(XPG * g, XPG * g + XPG))]
    return order


def feature_major(x):
    n, f = x.shape
    return x.T.reshape(f // P, P, n).transpose(1, 0, 2)


def blocks(w, kts=4):
    K, N = w.shape
    return w.reshape(K // (P * kts), kts, P, N // BLK, BLK).transpose(3, 0, 2, 1, 4).reshape(-1, P, kts * BLK)


def narrow_blocks(w):
    K, N = w.shape
    return w.reshape(K // (P * 8), 8, P, N // P, P).transpose(3, 0, 2, 1, 4).reshape(-1, P, 8 * P)


def interleave(*parts):
    n, lists = parts[0]
    out = []
    for i in range(n):
        for m, x in parts:
            k = x.shape[0] // m
            out.append(x[i * k:(i + 1) * k])
    return np.concatenate(out)


def kernel(**inputs):
    import concourse.bacc as bacc
    from concourse.bass_utils import run_bass_kernel_spmd

    x = {n: np.asarray(v) for n, v in inputs.items()}
    w_in = x["w_in"][0]
    cuts = np.cumsum([0, D_MODEL, D_INNER, D_INNER, GROUPS * D_STATE, GROUPS * D_STATE, HEADS, D_MODEL, D_MODEL])
    w_u, w_z, w_x, w_b, w_c, w_dt, w_gp, w_gs = [w_in[:, p:q] for p, q in zip(cuts, cuts[1:])]

    def cols(w, g, n):
        return w[:, g * n:(g + 1) * n]

    def bcx(g):
        return [narrow_blocks(cols(w_b, g, P)), narrow_blocks(cols(w_c, g, P)), blocks(cols(w_x, g, XPG * P))]

    stream = list(bcx(0))
    for g in range(GROUPS):
        stream.append(blocks(cols(w_z, g, XPG * P)))
        if g < GROUPS - 1:
            stream += bcx(g + 1)
    for e in EVENTS:
        stream.append(blocks(cols(w_u, e.i, BLK)) if e.kind == "in" else blocks(x["w_pool"][0, e.i]))
    stream.append(interleave((8, blocks(w_gp)), (8, blocks(x["w_pool_br"][0]))))
    stream.append(interleave((8, blocks(w_gs)), (8, blocks(x["w_ssd_br"][0]))))
    stream.append(blocks(x["w_out"][0]))
    stream += [blocks(x[n][0]) for n in ("w_mk", "w_mq", "w_mv", "w_mo")]
    stream.append(interleave((FT // 2, blocks(x["w_ffn_gate"][0])), (FT // 2, blocks(x["w_ffn_up"][0]))))
    stream.append(blocks(x["w_ffn_down"][0]))
    tiles = group_tiles(None)

    def per_feature(v):
        return v.reshape(-1, P).T

    conv_w = x["conv_w"][0].reshape(CONV_W, CT, P)[:, tiles].transpose(2, 1, 0).reshape(P, CT * CONV_W)
    conv_b = per_feature(x["conv_b"][0])[:, tiles]
    d_skip = np.repeat(x["d_skip"][0], 64).reshape(YT, P).T
    vecs = [conv_w, conv_b, per_feature(x["ssd_norm_w"][0]), d_skip] + [
        per_feature(x[n][0]) for n in ("pool_scale", "ln_mix_g", "ln_mix_b", "ln_mem_g", "ln_mem_b", "ln_ffn_g", "ln_ffn_b")]
    tri = (np.arange(P)[:, None] <= np.arange(P)[None, :]).astype(np.float32)
    counts = np.array([[1.0 / min(w, t + 1) for t in range(16)] for w in WINDOWS], np.float32)
    hist = x["state_conv"][0].reshape(NSAMP, CONV_W - 1, CT, P)[:, :, tiles].transpose(3, 2, 0, 1)
    arrays = {
        "wstream": np.concatenate(stream),
        "wdt": w_dt.reshape(KT, P, HEADS).transpose(1, 0, 2).reshape(P, KT * HEADS),
        "xT": feature_major(np.concatenate([x["x_prompt"][0], x["x_sample"][:, 0]])).reshape(P, KT * T),
        "memT": feature_major(x["mem_prompt"][0]).reshape(P, KT * N_MEM),
        "vecs": np.concatenate(vecs, axis=1),
        "hist": hist.reshape(P, -1),
        "hpool": x["state_pool"][0].reshape(NSAMP, POOL_HIST, KT, P).transpose(3, 2, 0, 1).reshape(P, -1),
        "dt_bias": x["dt_bias"][0][:, None],
        "a_log": x["a_log"][0][:, None],
        "ident": np.eye(P, dtype=np.float32),
        "cmask": np.concatenate([tri, np.ones((P, P), np.float32), tri], axis=1),
        "rc": np.broadcast_to(counts.reshape(1, -1), (P, 64)),
        "state_conv": x["state_conv"][0],
        "state_pool": x["state_pool"][0],
        "state_ssd": x["state_ssd"][0].reshape(4, 2, GROUPS, XPG, P, D_STATE).transpose(2, 0, 4, 1, 3, 5)
                      .reshape(GROUPS * 4, P, UNIT),
        "state_T": x["state_ssd"][0].reshape(NSAMP, GROUPS, XPG * P, D_STATE).transpose(1, 0, 3, 2)
                    .reshape(GROUPS * NSAMP, D_STATE, XPG * P),
        "kc": x["cache_mem_k"][0].transpose(3, 0, 2, 1).reshape(P, -1),
        "vc": x["cache_mem_v"][0].reshape(NSAMP, 2, P, MEM_DIM).transpose(2, 0, 1, 3).reshape(P, -1),
    }
    arrays = {n: np.ascontiguousarray(v) for n, v in arrays.items()}
    assert arrays["wstream"].shape == (N_UNITS, P, UNIT), (arrays["wstream"].shape, N_UNITS)
    outs = {
        "yT": (P, KT * T), "new_ssd_p": (GROUPS, P, XPG * P), "tails": (P, CT * 11), "utail": (P, KT * 23),
        "mem_k": (P, MH * N_MEM), "mem_v": (P, 2 * MEM_DIM), "new_ssd_s": (GROUPS * 4, P, UNIT),
        "pass_conv": (NSAMP, CONV_W - 2, CONV_DIM), "pass_pool": (NSAMP, POOL_HIST - 1, D_MODEL),
    }
    nc = bacc.Bacc("TRN2", target_bir_lowering=False, num_devices=1, dynamic_dma_scratch_size=8192)
    ins = {n: nc.dram_tensor(f"in_{n}", v.shape, mybir.dt.from_np(v.dtype), kind="ExternalInput").ap() for n, v in arrays.items()}
    res = {n: nc.dram_tensor(f"out_{n}", v, F32, kind="ExternalOutput").ap() for n, v in outs.items()}
    build(nc, ins, res)
    r = run_bass_kernel_spmd(nc, [{f"in_{n}": v for n, v in arrays.items()}], core_ids=[0]).results[0]
    r = {n: np.asarray(r[f"out_{n}"]) for n in outs}

    y = r["yT"].reshape(P, KT, T).transpose(2, 1, 0).reshape(T, D_MODEL)
    back = np.argsort(tiles)
    tail = r["tails"].reshape(P, CT, 11)[:, back].transpose(2, 1, 0).reshape(11, CONV_DIM)
    utail = r["utail"].reshape(P, KT, 23).transpose(2, 1, 0).reshape(23, D_MODEL)
    new_conv_s = np.concatenate([r["pass_conv"], tail[3:, None]], axis=1)[None]
    new_pool_s = np.concatenate([r["pass_pool"], utail[15:, None]], axis=1)[None]
    new_ssd_p = r["new_ssd_p"].reshape(GROUPS, P, XPG, D_STATE).transpose(0, 2, 1, 3).reshape(1, 1, HEADS, 64, D_STATE)
    new_ssd_s = r["new_ssd_s"].reshape(GROUPS, 4, P, 2, XPG, D_STATE).transpose(1, 3, 0, 4, 2, 5)\
        .reshape(1, NSAMP, HEADS, 64, D_STATE)
    mem_k = r["mem_k"].reshape(P, MH, N_MEM).transpose(2, 1, 0)[None, None]
    mem_v = r["mem_v"].reshape(P, 2, MEM_DIM).transpose(1, 0, 2).reshape(1, 1, N_MEM, MH, MHD)
    return (y[None, :SEQ], y[SEQ:, None], new_ssd_p, tail[None, None, :3], utail[None, None, :15], mem_k, mem_v,
            new_ssd_s, new_conv_s, new_pool_s)
```

```python
from contextlib import ExitStack, contextmanager
import math

import numpy as np

import concourse.bass as bass
from concourse import mybir

F32 = mybir.dt.float32
F32R = mybir.dt.float32r
ALU = mybir.AluOpType
ACT = mybir.ActivationFunctionType
AX_X = mybir.AxisListType.X

P = 128
D_MODEL = 2048
SEQ = 256
NSAMP = 8
T = SEQ + NSAMP
KT = D_MODEL // P
WINDOWS = (2, 4, 8, 16)
POOL_HIST = 15
GROUPS = 8
HPG = 8
HEADS = 64
D_INNER = 4096
D_STATE = 128
CONV_W = 4
CONV_DIM = D_INNER + 2 * GROUPS * D_STATE
CT = CONV_DIM // P
CPG = CT // GROUPS
XPG = 4
YT = D_INNER // P
N_MEM = 256
MH = 4
MHD = 128
MEM_DIM = MH * MHD
D_FF = -(-8 * D_MODEL // (3 * 256)) * 256
FT = D_FF // P
ALPHA = 2 ** 0.25
LN_EPS = 1e-5
RMS_EPS = 1e-5
RING = 4
UNIT = 1024
BLK = 256

VECS = [("conv_w", CT * CONV_W), ("conv_b", CT), ("norm_w", YT), ("d_skip", YT), ("pool_scale", KT),
        ("ln_mix_g", KT), ("ln_mix_b", KT), ("ln_mem_g", KT), ("ln_mem_b", KT),
        ("ln_ffn_g", KT), ("ln_ffn_b", KT)]
VEC_AT, _at = {}, 0
for _name, _n in VECS:
    VEC_AT[_name] = _at
    _at += _n
NVEC = _at

U_BCX = 3 * 4
U_Z = 2 * 4
U_UP = 8 * 4
U_POOL = 4 * 2
U_BRA = 8 * 8
U_BRB = 8 * 12
U_OUT = 8 * 4
U_MEM = 4 * 4
U_Q = 2 * 4
U_MO = 8
U_F1 = (FT // 2) * 8
U_F2 = 8 * (FT // 4)
N_MISC = 9
START = {"sgm": 1, "br_read": 1, "h_read": 1, "h_hi": 1, "seg_ready": 1, "res_ready": 3,
         "fst_free": 1, "st_done": 3}
STEPS = 26
SPLIT_IN_SSD = 14
N_UNITS = GROUPS * (U_BCX + U_Z) + U_UP + U_POOL + U_BRA + U_BRB + U_OUT + U_MEM + U_Q + U_MO + U_F1 + U_F2


class Tally:

    def __init__(self):
        self.base, self.k, self.per, self.reg = 0, 0, 0, None

    def add(self, n=1):
        self.k += n
        return self.now()

    def now(self, less=0):
        v = self.base + self.k - less
        return v if self.reg is None else self.reg * self.per + v


class Tallies(dict):
    def __missing__(self, name):
        self[name] = Tally()
        return self[name]


@contextmanager
def rounds(eng, n, tallies, per):
    with eng.Fori(0, n) as i:
        frozen = {}
        for name, p in per.items():
            t = tallies[name]
            t.base, t.k, t.per, t.reg = t.base + t.k, 0, p, i
        for name, t in tallies.items():
            if name not in per:
                frozen[name] = t.k
        yield i
        for name, p in per.items():
            assert tallies[name].k == p, (name, tallies[name].k, p)
        for name, t in tallies.items():
            assert name in per or t.k == frozen.get(name, 0), (name, t.k)
    for name, p in per.items():
        t = tallies[name]
        t.base, t.k, t.reg = t.base + n * p, 0, None


class Event:

    def __init__(self, kind, i, block, unit, item):
        self.kind, self.i, self.item = kind, i, item
        self.group = 3 - (i // 2 if kind == "in" else i)
        self.tile = 4 * self.group + (2 * (i % 2) if kind == "in" else 0)
        self.blocks = [block] if kind == "in" else [block, block + 1]
        self.tiles = 2 if kind == "in" else 4
        self.start, self.end = unit, unit + (4 if kind == "in" else 2)


def plan_pooling():
    order = []
    for b in range(8):
        order.append(("in", b))
        if b >= 5 and b % 2:
            order.append(("proj", b // 2 - 2))
    order += [("proj", 2), ("proj", 3)]
    events, block, unit, item = [], 0, 0, 0
    for kind, i in order:
        e = Event(kind, i, block, unit, item)
        block, unit, item = block + len(e.blocks), e.end, item + e.tiles
        events.append(e)
    read = {}
    for n, e in enumerate(events):
        e.ahead = max(e.end + RING, SPLIT_IN_SSD + min(n + 1, 3))
        if e.kind == "proj":
            e.needs = next(p.item + 2 for p in events if p.kind == "in" and p.i == 2 * e.i + 1)
        for m, k in enumerate(e.blocks):
            read[k] = (e.kind, e.i * e.tiles + 2 * m + 2)
    return events, read


EVENTS, READ = plan_pooling()


def flat(ap):
    return ap.rearrange("p a b -> p (a b)")


def build(nc, a, o):
    ctx = ExitStack()
    with ctx:
        def sem(name):
            return ctx.enter_context(nc.semaphore(name))

        def alloc(stack, name, shape, dt=F32):
            return stack.enter_context(nc.sbuf_tensor("sb_" + name, shape, dt))

        def overlay(skip, **tensors):
            out = []
            with ExitStack() as s:
                if skip:
                    alloc(s, f"skip_{next(iter(tensors))}", [P, skip // 4])
                for name, (shape, *dt) in tensors.items():
                    out.append(alloc(s, name, shape, *dt))
            return out

        raw = alloc(ctx, "raw", [P, RING, UNIT])
        whi = alloc(ctx, "whi", [P, RING, UNIT], F32R)
        wlo = alloc(ctx, "wlo", [P, RING, UNIT], F32R)
        xH = alloc(ctx, "xH", [P, KT, T], F32R)
        xL = alloc(ctx, "xL", [P, KT, T], F32R)
        resid = alloc(ctx, "resid", [P, KT, T])
        ident = alloc(ctx, "ident", [P, P])
        ones = alloc(ctx, "ones", [P, P])
        vec = alloc(ctx, "vec", [P, NVEC])
        rc = alloc(ctx, "rc", [P, 4, 16])
        phs = alloc(ctx, "phs", [P, KT, NSAMP])
        eps = alloc(ctx, "eps", [P, 2])
        total = alloc(ctx, "total", [P, T])
        dtxc = alloc(ctx, "dtxc", [P, GROUPS * NSAMP, XPG])
        decc = alloc(ctx, "decc", [P, GROUPS * NSAMP, XPG])

        def vcol(name, i, n=1):
            if isinstance(i, int):
                return vec[:, VEC_AT[name] + i:VEC_AT[name] + i + n]
            return vec[:, bass.ds(i + VEC_AT[name], n)]

        G = [[ctx.enter_context(nc.psum_tensor(f"G{s}{j}", [P, 512], F32)) for j in range(2)] for s in range(2)]
        M = [ctx.enter_context(nc.psum_tensor(f"M{j}", [P, 512], F32)) for j in range(4)]
        SETS = [G[0], G[1], [M[2], M[3]], [M[0], M[1]]]

        def attended(h):
            return (M[2], M[3], G[0][0], M[0])[h][:, 0:SEQ]

        YB = 2 * YT * T * 4
        yH, yL = overlay(0, yH=([P, YT, T], F32R), yL=([P, YT, T], F32R))
        (zs, cumbc, xdt, BT, CTt, cbm, cmask, E, MM, Btok, bcs, fst, bcp, R, cacc, dttok, ncum, wtok,
         dts, dtx, ysamp, ysbc, chist, tails) = overlay(
            YB, zs=([P, XPG, T],), cumbc=([P, HPG, SEQ],), xdt=([P, 2, HPG * 64],),
            BT=([P, T],), CTt=([P, T],), cbm=([P, 384],), cmask=([P, 384],), E=([P, 2, 384],),
            MM=([P, 3, 384],), Btok=([P, 2, P],), bcs=([NSAMP, P],), fst=([P, XPG * P],), bcp=([P, NSAMP],),
            R=([P, 2, CONV_W - 1 + T],), cacc=([P, 2, T],), dttok=([P, 2, HEADS],), ncum=([P, 2, HEADS],),
            wtok=([P, 2, HEADS],), dts=([P, YT, 2 * NSAMP],), dtx=([P, XPG, NSAMP],),
            ysamp=([P, XPG, NSAMP],), ysbc=([P, XPG, NSAMP],), chist=([P, CT, NSAMP],), tails=([P, CT, 11],))
        rstd = E[:, 0, 0:T]
        xs = resid[:, 0:XPG, :]
        yg = resid[:, XPG:2 * XPG, :]
        stT = resid[:, 8:16, :].rearrange("p a b -> p (a b)")[:, 0:4 * XPG * P].rearrange(
            "p (s c) -> p s c", s=4)
        wdt, hist, hpool, S, dAtok, pcol, pxs, ctmp = overlay(
            0, wdt=([P, KT, HEADS],), hist=([P, CT, NSAMP * 3],), hpool=([P, KT, NSAMP, POOL_HIST],),
            S=([HEADS, 8, T],), dAtok=([P, 2, HEADS],), pcol=([HEADS, 4],), pxs=([HEADS, 2 * NSAMP],),
            ctmp=([P, CT, NSAMP],))
        mixH, mixL, tmp, utail, sgA = overlay(
            YB, mixH=([P, KT, T], F32R), mixL=([P, KT, T], F32R), tmp=([P, 4, T],), utail=([P, KT, 23],),
            sgA=([P, 2, T],))
        UT = POOL_HIST + T
        V = flat(resid[:, :, :])[:, XPG * T:XPG * T + 4 * UT].rearrange("p (l j t) -> p l j t", l=2, j=2)
        U_AT = XPG * T + 4 * UT
        U = flat(resid[:, :, :])[:, U_AT:U_AT + 4 * UT].rearrange("p (r j t) -> p r j t", r=2, j=2)
        assert U_AT >= 2 * XPG * T and U_AT + 4 * UT <= KT * T
        sq, KTm, Vn, mean, lrstd, memH, memL, memraw, PT, ssT, sP, sPT, smx, snm, srs, sri = overlay(
            0, sq=([P, 2, 4 * T],), KTm=([P, MH, N_MEM],), Vn=([P, 2, MEM_DIM],), mean=([P, T],),
            lrstd=([P, T],), memH=([P, KT, N_MEM], F32R), memL=([P, KT, N_MEM], F32R),
            memraw=([P, 2, 4 * N_MEM],), PT=([P, 2, 512],), ssT=([P, 2, 32],),
            sP=([32, N_MEM],), sPT=([P, 2, 32],), smx=([P, 9],), snm=([P, 9],), srs=([P, 9],), sri=([P, 9],))
        kc, qT = overlay(YB, kc=([P, MH, NSAMP, N_MEM],), qT=([P, MH, T],))
        (vc,) = overlay(YB, vc=([P, MH, NSAMP, 2, MHD],))
        oH, oL = overlay(0, oH=([P, MH, T], F32R), oL=([P, MH, T], F32R))
        AT_MEM = (2 * 4 * T + 2 * MH * N_MEM + 2 * T) * 4
        (Pe,) = overlay(AT_MEM + 2 * KT * N_MEM * 4, Pe=([P, 2 * MH, N_MEM],))
        sq2, mean2, lrstd2, hH, hL, hf, sgF, outer, bcb = overlay(
            0, sq2=([P, 2, 4 * T],), mean2=([P, T],), lrstd2=([P, T],), hH=([P, FT, T], F32R),
            hL=([P, FT, T], F32R), hf=([P, 2, T],), sgF=([P, 2, T],),
            outer=([P, 2, XPG, P],), bcb=([P, 2, 2 * P],))
        st = flat(sq2[:, :, :])[:, 0:2 * UNIT].rearrange("p (s b i n) -> p s b i n", s=2, b=2, i=XPG)

        scr_cum = nc.dram_tensor("scr_cum", (HEADS, SEQ), F32, kind="Internal").ap()
        scr_dts = nc.dram_tensor("scr_dts", (HEADS, 2 * NSAMP), F32, kind="Internal").ap()
        scr_bc = nc.dram_tensor("scr_bc", (GROUPS * NSAMP, P), F32, kind="Internal").ap()

        landed = [sem(f"landed{k}") for k in range(RING)]
        hi_ready, lo_ready, used = sem("hi_ready"), sem("lo_ready"), sem("used")
        in_x, in_misc = [sem(f"in_x{c}") for c in range(4)], sem("in_misc")
        act_step, dve_step = sem("act_step"), sem("dve_step")
        s = {n: sem(n) for n in (
            "fst_free bcp_ready st_used ys_ps b_in0 b_in1 pool_past seg_ready w_sum y2_ready kv_out tails_out x_hi x_lo dt_psum dt_z dt_exp dt_u dt_ln dt_ready dA_tok_ps dA_tok cum_ps cum_sb cumt_ps "
            "pre_exp pre_done scr_out dts_in ones_set "
            "raw_ready conv_done xbc_ready xtok_ps btok_ps btok_sb bc_rows cb_ps xdt_ready e_ready m_ready "
            "y_done xw_ready st_ps fst_ready z_ready out_ready st_done sq_ready sq_sum rms_ps sd_ready "
            "y3_ready yh_ready yl_ready cum_in bc_out st_in0 st_in1 st_in2 st_in3 st_out0 st_out1 fst_out "
            "uraw pool_f mix_hi mix_lo wp_ready sgm br_read res_ready "
            "ln_sum mean_ready cen_ready sqc_ready sqc_used  lsd_ready xn_ready "
            "mem_in0 mem_in1 mem_hi mem_lo kt_ready vn_ready kc_in0 kc_in1 vc_in0 vc_in1 sum_ready smx_ready q_ready sc_ps mx_ready p_ready pn_ready "
            "pt_ps pt_ready o_ps o_hi o_lo ss_ps ss_sb sst_ps sp_exp sp_n spt_ps spt_sb so_ps "
            "h_read h_hi h_lo outs").split()}
        block = ctx.enter_context(nc.Block())

        @block.sync
        def _(sp):
            def load(u, k):
                sp.wait_ge(lo_ready, u + (k + 1))
                sp.dma_start(raw[:, k, :], a["wstream"][bass.ds(u + k, 1), :, :].rearrange("u p c -> (u p) c"))\
                    .then_inc(landed[k], 16)

            for c in range(4):
                sp.dma_start(flat(resid[:, 4 * c:4 * c + 4, :]), a["xT"][:, c * 4 * T:(c + 1) * 4 * T])\
                    .then_inc(in_x[c], 16)
                if c == 1 or c == 3:
                    load(0, c // 2)
            load(0, 2)
            load(0, 3)
            with sp.Fori(1, N_UNITS // RING) as i:
                for k in range(RING):
                    load(i * RING, k)

        @block.tensor
        def _(pe):
            t = Tallies()
            pe.sem_inc(used, RING)
            for name, value in START.items():
                pe.sem_inc(s[name], value)

            def mm3(slot, col, kH, kL, out, start, stop):
                w = whi[:, slot, col:col + P]
                pe.matmul(out, w, kH, start=start, stop=False)
                pe.matmul(out, w, kL, start=False, stop=False)
                return pe.matmul(out, wlo[:, slot, col:col + P], kH, start=False, stop=stop)

            def unit(plan):
                u = t["unit"]
                assert u.base % RING == 0 and (u.reg is None or u.per % RING == 0)
                slot = u.k % RING
                pe.wait_ge(lo_ready, u.add() + RING)
                for p in plan:
                    last = mm3(slot, *p)
                last.then_inc(used, 1)

            def block_units(H, L, kts, out, n=T, between=None, before=None):
                for q in range(0, kts, 4):
                    if before:
                        before(q // 4)
                    unit([(kk * BLK + j * P, H[:, q + kk, 0:n], L[:, q + kk, 0:n], out[j][:, 0:n],
                           q + kk == 0, q + kk == kts - 1) for kk in range(4) for j in range(2)])
                    if between:
                        between(q // 4)

            def bc_units(out, before=None):
                for j in range(2):
                    for q in (0, 8):
                        if before and j == 0:
                            before(q)
                        unit([(kk * P, xH[:, q + kk, :], xL[:, q + kk, :], out[j][:, 0:T],
                               q + kk == 0, q + kk == KT - 1) for kk in range(8)])

            def step_sizes():
                pe.wait_ge(in_misc, N_MISC * 16)
                for k in range(KT):
                    last = pe.matmul(M[0][0:HEADS, 0:T], wdt[:, k, :], resid[:, k, :], start=k == 0, stop=k == KT - 1)
                last.then_inc(s["dt_psum"], 1)

            def decays(part):
                if part == 0:
                    pe.wait_ge(s["dt_ready"], 1)
                    for r in range(2):
                        for b in range(2):
                            last = pe.transpose(M[1][:, r * P + b * 64:r * P + b * 64 + 64],
                                                S[:, 7 * r, b * P:b * P + P], ident[0:HEADS, 0:HEADS])
                    last.then_inc(s["dA_tok_ps"], 1)
                elif part == 1:
                    pe.wait_ge(s["dA_tok"], 2)
                    pe.wait_ge(s["ones_set"], 1)
                    pe.matmul(M[0][0:HEADS, 0:SEQ], dAtok[:, 0, :], cmask[:, 0:SEQ], start=True, stop=False)
                    pe.matmul(M[0][0:HEADS, P:SEQ], dAtok[:, 1, :], cmask[:, SEQ:384], start=False, stop=True)
                    for b in range(2):
                        last = pe.matmul(M[0][:, 384:384 + HEADS], ones[:, :], dAtok[:, b, :], start=b == 0, stop=b == 1)
                    last.then_inc(s["cum_ps"], 1)
                else:
                    pe.wait_ge(s["cum_sb"], 1)
                    for b in range(2):
                        last = pe.transpose(M[1][:, 256 + b * 64:256 + b * 64 + 64], S[:, 1, b * P:b * P + P],
                                            ident[0:HEADS, 0:HEADS])
                    last.then_inc(s["cumt_ps"], 1)

            def token_major():
                pe.wait_ge(s["w_sum"], 1)
                pe.wait_ge(s["xbc_ready"], t["xbc"].add(CPG))
                for b in range(2):
                    for j in range(XPG):
                        last = pe.transpose(M[b][:, j * P:j * P + P], xs[:, j, b * P:b * P + P], ident[:, :])
                last.then_inc(s["xtok_ps"], 1)
                for b in range(2):
                    pe.transpose(M[2][:, b * P:b * P + P], BT[:, b * P:b * P + P], ident[:, :])
                pe.transpose(M[2][0:NSAMP, 256:384], BT[:, SEQ:T], ident[:, :]).then_inc(s["btok_ps"], 1)
                pe.matmul(M[3][:, 0:SEQ], BT[:, 0:P], CTt[:, 0:SEQ], start=True, stop=True)
                pe.matmul(M[3][:, SEQ:384], BT[:, P:SEQ], CTt[:, P:SEQ], start=True, stop=True).then_inc(s["cb_ps"], 1)

            def head(h):
                if h == 0:
                    pe.wait_ge(s["xdt_ready"], t["xdt"].add(2))
                pe.wait_ge(s["m_ready"], t["m"].add())
                out = M[h // 4][64 * (h % 2):64 * (h % 2) + 64, (h // 2 % 2) * SEQ:(h // 2 % 2) * SEQ + SEQ]
                pe.matmul(out, xdt[:, 0, h * 64:h * 64 + 64], MM[:, h % 3, 0:SEQ], start=True, stop=False)
                pe.matmul(out[:, P:SEQ], xdt[:, 1, h * 64:h * 64 + 64], MM[:, h % 3, SEQ:384],
                          start=False, stop=True).then_inc(s["y_done"], 1)

            def sample(b):
                pe.wait_ge(s[f"st_in{b % 4}"], t[f"sti{b % 4}"].add() * 16)
                for i in range(XPG):
                    last = pe.matmul(M[3][:, 384 + i * NSAMP + b:385 + i * NSAMP + b], stT[:, b % 4, i * P:i * P + P],
                                     CTt[:, SEQ + b:SEQ + b + 1], start=True, stop=True)
                last.then_inc(s["st_used"], 1)
                if b == NSAMP - 1:
                    pe.wait_ge(s["bcp_ready"], t["bcp"].add())
                    pe.matmul(M[3][:, 416:416 + NSAMP], ones[:, :], bcp[:, :], start=True, stop=True)\
                      .then_inc(s["ys_ps"], 1)

            def state():
                pe.wait_ge(s["btok_sb"], t["btok"].add())
                pe.wait_ge(s["xw_ready"], t["xw"].add())
                for j in range(XPG):
                    for b in range(2):
                        last = pe.matmul(M[2][:, j * P:j * P + P], xdt[:, b, j * P:j * P + P], Btok[:, b, :],
                                         start=b == 0, stop=b == 1)
                last.then_inc(s["st_ps"], 1)

            def rms():
                pe.wait_ge(s["sq_sum"], t["sq"].add())
                pe.matmul(M[0][:, 0:T], ones[:, :], zs[:, 0, :], start=True, stop=True).then_inc(s["rms_ps"], 1)

            def z_blocks():
                pe.wait_ge(s["raw_ready"], t["raw"].add(2))
                block_units(xH, xL, KT, SETS[0], between=lambda q: token_major() if q == 2 else None)
                pe.wait_ge(s["raw_ready"], t["raw"].add(2))
                block_units(xH, xL, KT, SETS[1], between=lambda q: [head(2 * q), head(2 * q + 1), sample(2 * q),
                                                                    sample(2 * q + 1)])

            def bcx_blocks():
                pe.wait_ge(s["z_ready"], t["z"].add(2))
                bc_units(SETS[0])
                state()
                pe.wait_ge(s["z_ready"], t["z"].add(2))
                block_units(xH, xL, KT, SETS[1])
                rms()
                pe.wait_ge(s["fst_ready"], t["fst"].add())
                block_units(xH, xL, KT, SETS[2])
                t["raw"].add(2)
                pe.wait_ge(s["sd_ready"], t["sd"].add())

            bc_units(SETS[0], before=lambda q: pe.wait_ge(s["x_lo"], q // 4 + 2))
            step_sizes()
            block_units(xH, xL, KT, SETS[1])
            block_units(xH, xL, KT, SETS[2], between=lambda q: decays({0: 0, 2: 1, 3: 2}[q]) if q != 1 else None)
            with rounds(pe, GROUPS - 1, t, dict(unit=U_BCX + U_Z, raw=6, xbc=6, xdt=2, m=8, btok=1, xw=1, sq=1,
                                                z=4, fst=1, sd=1, bcp=1, sti0=2, sti1=2, sti2=2, sti3=2)):
                z_blocks()
                bcx_blocks()
            z_blocks()

            for e in EVENTS:
                sets = [SETS[k % 4] for k in e.blocks]
                for k in e.blocks:
                    if k >= 4:
                        kind, count = READ[k - 4]
                        if kind == "in":
                            pe.wait_ge(s["uraw"], count)
                        else:
                            pe.wait_ge(s["wp_ready"], count)
                if e.kind == "in":
                    if e.i < 2:
                        pe.wait_ge(s["z_ready"], t["z"].add(2))
                    if e.i == 2:
                        pe.wait_ge(s["fst_ready"], t["fst"].add())
                    if e.i == 3:
                        pe.wait_ge(s["sd_ready"], t["sd"].add())
                    block_units(xH, xL, KT, sets[0])
                    if e.i == 0:
                        state()
                    if e.i == 1:
                        rms()
                else:
                    pe.wait_ge(s["mix_lo"], e.needs)
                    for b in range(2):
                        unit([(kk * BLK + j * P, mixH[:, e.tile + kk, :], mixL[:, e.tile + kk, :], sets[b][j][:, 0:T],
                               kk == 0, kk == 3) for kk in range(4) for j in range(2)])

            pe.wait_ge(s["wp_ready"], 12)
            for H, L, kts in ((mixH, mixL, KT), (yH, yL, YT)):
                if kts == YT:
                    pe.wait_ge(s["yl_ready"], YT)
                with rounds(pe, 8, t, dict(unit=4 + kts // 4, sgm=2, br_read=2)):
                    pe.wait_ge(s["sgm"], START["sgm"] + t["sgm"].now())
                    block_units(xH, xL, KT, SETS[0])
                    pe.wait_ge(s["br_read"], START["br_read"] + t["br_read"].now())
                    pe.wait_ge(s["mix_lo"], 2 * KT)
                    block_units(H, L, kts, SETS[1])
                    t["sgm"].add(2)
                    t["br_read"].add(2)
            pe.wait_ge(s["wp_ready"], KT)

            def project(H, L, kts, pairs=4, first=0, before=None):
                with rounds(pe, pairs, t, dict(unit=2 * kts // 4 * (4 // pairs), res=16 // pairs)):
                    for b in range(8 // pairs):
                        pe.wait_ge(s["res_ready"], t["res"].now() + START["res_ready"] - 2)
                        block_units(H, L, kts, SETS[first + b % 2], before=before)
                        t["res"].add(2)

            def ln_sum():
                pe.wait_ge(s["sum_ready"], t["sum"].add())
                pe.wait_ge(s["res_ready"], t["res"].now() + START["res_ready"])
                pe.matmul(M[0][:, 0:T], ones[:, :], total[:, :], start=True, stop=False)
                for k in (KT - 2, KT - 1):
                    last = pe.matmul(M[0][:, 0:T], ones[:, :], resid[:, k, :], start=False, stop=k == KT - 1)
                last.then_inc(s["ln_sum"], 1)

            def ln_var(sqb, chunks=range(4)):
                for c in chunks:
                    pe.wait_ge(s["sqc_ready"], t["sqc"].add())
                    for k in range(4):
                        last = pe.matmul(M[1][:, 0:T], ones[:, :], sqb[:, c % 2, k * T:k * T + T],
                                         start=c == 0 and k == 0, stop=c == 3 and k == 3)
                    last.then_inc(s["sqc_used"], 1)

            project(mixH, mixL, KT, first=2, before=lambda q: pe.wait_ge(s["mix_lo"], 2 * KT + 4 * (q + 1)))
            pe.wait_ge(s["mem_lo"], 4)
            pe.wait_ge(s["sgm"], START["sgm"] + t["sgm"].now())
            pe.wait_ge(s["br_read"], START["br_read"] + t["br_read"].now())
            block_units(memH, memL, KT, SETS[0], n=N_MEM, between=lambda q: ln_sum() if q == 1 else None)
            ln_var(sq, (0, 1))
            block_units(memH, memL, KT, SETS[1], n=N_MEM, between=lambda q: ln_var(sq, (2, 3)) if q == 0 else None)

            X = G[1][0]

            def sample_scores(h):
                pe.wait_ge(s["q_ready"], h + 1)
                pe.wait_ge(s[f"kc_in{h // 2}"], 16)
                for m in range(2):
                    for b in range(NSAMP):
                        c = m * 32 + h * NSAMP + b
                        last = pe.matmul(X[:, c:c + 1], kc[:, h, b, m * P:m * P + P], qT[:, h, SEQ + b:SEQ + b + 1],
                                         start=True, stop=True)
                last.then_inc(s["ss_ps"], 1)

            def sample_rows():
                pe.wait_ge(s["ss_sb"], 1)
                for m in range(2):
                    last = pe.transpose(X[0:32, 64 + m * P:64 + m * P + P], ssT[:, m, :], ident[:, :])
                last.then_inc(s["sst_ps"], 1)

            def sample_probs():
                pe.wait_ge(s["sp_n"], 1)
                for m in range(2):
                    last = pe.transpose(X[:, 320 + m * 32:352 + m * 32], sP[:, m * P:m * P + P], ident[0:32, 0:32])
                last.then_inc(s["spt_ps"], 1)

            def sample_out(h):
                pe.wait_ge(s[f"vc_in{h // 2}"], 16)
                pe.wait_ge(s["spt_sb"], 1)
                for b in range(NSAMP):
                    c = h * NSAMP + b
                    for m in range(2):
                        last = pe.matmul(X[:, 384 + c:385 + c], vc[:, h, b, m, :], sPT[:, m, c:c + 1],
                                         start=m == 0, stop=m == 1)
                last.then_inc(s["so_ps"], 1)

            def probs(h):
                pe.wait_ge(s["pn_ready"], 2 * h + 2)
                if h == 1:
                    pe.wait_ge(s["vn_ready"], 2)
                if h >= 2:
                    pe.wait_ge(s["pt_ready"], h - 1)
                for m in range(2):
                    for b in range(2):
                        last = pe.transpose(G[1 - h % 2][1][:, (m * 2 + b) * P:(m * 2 + b) * P + P],
                                            Pe[:, 2 * h + b, m * P:m * P + P], ident[:, :])
                last.then_inc(s["pt_ps"], 1)

            def weighted(h):
                pe.wait_ge(s["vn_ready"], 2 * (h // 2) + 2)
                pe.wait_ge(s["pt_ready"], h + 1)
                for m in range(2):
                    last = pe.matmul(attended(h), Vn[:, m, h * MHD:h * MHD + MHD], PT[:, h % 2, m * SEQ:m * SEQ + SEQ],
                                     start=m == 0, stop=m == 1)
                last.then_inc(s["o_ps"], 1)

            def values(b, out, between=None):
                for q in range(4):
                    slot = t["unit"].k % RING
                    pe.wait_ge(lo_ready, t["unit"].add() + RING)
                    for kk in range(4):
                        for m in range(2):
                            k = 4 * q + kk
                            wH, wL = whi[:, slot, kk * BLK:kk * BLK + BLK], wlo[:, slot, kk * BLK:kk * BLK + BLK]
                            mH, mL = memH[:, k, m * P:m * P + P], memL[:, k, m * P:m * P + P]
                            o_ = out[m][:, 0:BLK]
                            pe.matmul(o_, mH, wH, start=k == 0, stop=False)
                            pe.matmul(o_, mH, wL, start=False, stop=False)
                            last = pe.matmul(o_, mL, wH, start=False, stop=k == KT - 1)
                    last.then_inc(used, 1)
                    between(q)

            for b in range(2):
                if b == 1:
                    pe.wait_ge(s["kt_ready"], MH)
                block_units(xH, xL, KT, SETS[2 + b], before=lambda q: pe.wait_ge(s["x_lo"], 4 + q + 1),
                            between=lambda q: sample_scores(q - 1) if b == 1 and q in (1, 2) else None)

            def scores():
                pe.wait_ge(s["q_ready"], MH)
                for h in range(MH):
                    for b in range(2):
                        last = pe.matmul(M[h][:, b * N_MEM:b * N_MEM + N_MEM], qT[:, h, b * P:b * P + P], KTm[:, h, :],
                                         start=True, stop=True)
                    last.then_inc(s["sc_ps"], 1)

            def among_first_values(q):
                if q == 0:
                    scores()
                    sample_scores(2)
                elif q == 1:
                    sample_scores(3)
                elif q == 2:
                    sample_rows()

            def among_second_values(q):
                if q == 0:
                    sample_probs()
                probs(q)
                if q in (1, 2):
                    sample_out(q - 1)
                    weighted(q - 1)
                elif q == 3:
                    sample_out(2)
                    sample_out(3)

            values(0, SETS[0], among_first_values)
            pe.wait_ge(s["p_ready"], 4)
            values(1, SETS[3], among_second_values)
            weighted(2)
            weighted(3)
            pe.wait_ge(s["o_hi"], MH + 1)
            pe.wait_ge(s["o_lo"], MH + 1)
            for b in range(8):
                if b >= 4:
                    pe.wait_ge(s["res_ready"], t["res"].now() + START["res_ready"] - 6)
                unit([(kk * BLK + j * P, oH[:, kk, :], oL[:, kk, :], SETS[b % 4][j][:, 0:T],
                       kk == 0, kk == 3) for kk in range(4) for j in range(2)])
                t["res"].add(2)
            ln_sum()
            ln_var(sq2)
            with rounds(pe, FT // 2, t, dict(unit=8, sgm=2, h_read=2)):
                pe.wait_ge(s["sgm"], START["sgm"] + t["sgm"].now())
                block_units(xH, xL, KT, SETS[0], before=lambda q: pe.wait_ge(s["x_lo"], 8 + q + 1))
                pe.wait_ge(s["h_read"], START["h_read"] + t["h_read"].now())
                block_units(xH, xL, KT, SETS[1])
                t["sgm"].add(2)
                t["h_read"].add(2)
            project(hH, hL, FT, pairs=2, before=lambda q: pe.wait_ge(s["h_lo"], 4 * (q + 1)))
            ln_sum()
            ln_var(sq2)
            assert t["unit"].now() == N_UNITS, (t["unit"].now(), N_UNITS)

        @block.scalar
        def _(act):
            t = Tallies()

            def step(ins):
                ins.then_inc(act_step, 1)
                act.wait_ge(act_step, t["step"].add())

            def split(n):
                u = t["unit"]
                assert u.base % RING == 0 and (u.reg is None or u.per % RING == 0)
                for _ in range(n):
                    slot = u.k % RING
                    lap = u.base // RING + u.k // RING + 1
                    if u.reg is not None:
                        lap = u.reg * (u.per // RING) + lap
                    act.wait_ge(landed[slot], lap * 16)
                    act.wait_ge(used, u.add())
                    act.activation(whi[:, slot, :], raw[:, slot, :], ACT.Copy).then_inc(hi_ready, 1)

            def finished(units):
                act.wait_ge(used, t["done"].add(units) + RING)

            for c in range(4):
                act.wait_ge(in_x[c], 16)
                act.activation(flat(xH[:, 4 * c:4 * c + 4, :]), flat(resid[:, 4 * c:4 * c + 4, :]),
                               ACT.Copy).then_inc(s["x_hi"], 1)
                if c == 1:
                    split(1)
            split(3)

            def raws(outs):
                for j in range(2):
                    n = t["raw"]
                    if n.reg is not None or n.k >= 2:
                        act.wait_ge(s["conv_done"], n.now(1))
                    act.activation(R[:, n.k % 2, CONV_W - 1:CONV_W - 1 + T], outs[j][:, 0:T], ACT.Copy)\
                       .then_inc(s["raw_ready"], 1)
                    n.add()

            def silus(dests):
                for j in range(2):
                    c = t["conv"]
                    act.wait_ge(s["conv_done"], c.add())
                    act.activation(dests[j], cacc[:, (c.k - 1) % 2, :], ACT.Silu).then_inc(s["xbc_ready"], 1)

            def z_block(j):
                finished(4)
                for k in range(2):
                    act.activation(zs[:, 2 * j + k, :], SETS[j][k][:, 0:T], ACT.Silu).then_inc(s["z_ready"], 1)

            def heads(h0):
                for h in (h0, h0 + 1):
                    act.wait_ge(s["seg_ready"], START["seg_ready"] + t["e"].add())
                    act.activation(E[:, h % 2, :], E[:, h % 2, :], ACT.Exp).then_inc(s["e_ready"], 1)

            DESTS = [[BT[:, :], CTt[:, :]], [xs[:, 0, :], xs[:, 1, :]], [xs[:, 2, :], xs[:, 3, :]]]

            def raw_block(i):
                finished(4)
                raws(SETS[i])

            def group(last=False):
                split(2)
                heads(0)
                act.wait_ge(s["btok_ps"], t["btok"].add())
                act.activation(flat(Btok[:, :, :]), M[2][:, 0:256], ACT.Copy).then_inc(s["btok_sb"], 1)
                act.activation(bcs[:, :], M[2][0:NSAMP, 256:384], ACT.Copy).then_inc(s["bc_rows"], 1)
                split(2)
                heads(2)
                z_block(0)
                split(1)
                heads(4)
                split(1)
                heads(6)
                split(2)
                z_block(1)
                split(3)
                for i in range(XPG):
                    act.wait_ge(s["y2_ready"], t["y2"].add())
                    act.activation(zs[:, i, :], yg[:, i, :], ACT.Square).then_inc(s["sq_ready"], 1)
                split(1)
                if not last:
                    raw_block(0)
                act.wait_ge(s["fst_free"], t["fo"].add())
                act.wait_ge(s["st_ps"], t["st"].add())
                act.activation(fst[:, :], M[2][:, :], ACT.Copy).then_inc(s["fst_ready"], 1)
                if not last:
                    silus(DESTS[0])
                split(4)
                if not last:
                    raw_block(1)
                act.wait_ge(s["rms_ps"], t["rms"].add())
                act.activation(rstd, M[0][:, 0:T], ACT.Sqrt, scale=1.0 / (XPG * P), bias=eps[:, 0:1])\
                   .then_inc(s["sd_ready"], 1)
                split(1)
                if not last:
                    silus(DESTS[1])
                split(1)
                if not last:
                    split(1)
                for i in range(XPG):
                    act.wait_ge(s["y3_ready"], t["y3"].add())
                    yt = t["g"].now() * XPG + i
                    dst = yH[:, yt:yt + 1, :] if isinstance(yt, int) else yH[:, bass.ds(yt, 1), :]
                    act.activation(flat(dst), yg[:, i, :], ACT.Copy).then_inc(s["yh_ready"], 1)
                if not last:
                    split(1)
                    raw_block(2)
                    silus(DESTS[2])
                t["g"].add()

            act.wait_ge(in_misc, N_MISC * 16)
            step(act.activation(pcol[:, 2:3], pcol[:, 1:2], ACT.Exp))
            split(4)
            raw_block(0)
            act.wait_ge(s["dt_z"], 1)
            step(act.activation(S[:, 3, :], S[:, 2, :], ACT.Abs))
            act.activation(S[:, 4, :], S[:, 3, :], ACT.Exp, scale=-1.0).then_inc(s["dt_exp"], 1)
            split(1)
            act.wait_ge(s["dt_u"], 1)
            act.activation(S[:, 6, :], S[:, 5, :], ACT.Ln).then_inc(s["dt_ln"], 1)
            silus(DESTS[0])
            split(1)
            act.wait_ge(s["dt_ready"], 1)
            act.activation(pxs[:, NSAMP:2 * NSAMP], S[:, 0, SEQ:T], ACT.Exp).then_inc(s["pre_exp"], 1)
            split(2)
            raw_block(1)
            silus(DESTS[1])
            split(4)
            act.wait_ge(s["w_sum"], 1)
            act.activation(flat(wtok[:, :, :]), flat(wtok[:, :, :]), ACT.Exp).then_inc(s["pre_done"], 1)
            raw_block(2)
            silus(DESTS[2])
            with rounds(act, GROUPS - 1, t, dict(unit=20, done=20, raw=6, conv=6, e=8, g=1, btok=1,
                                                 fo=1, st=1, y2=4, rms=1, y3=4)):
                group()
            group(last=True)

            def high(e):
                for j in range(e.tiles):
                    if e.kind == "in":
                        act.wait_ge(s["pool_f"], 2 * e.i + j + 1)
                    else:
                        act.wait_ge(s["wp_ready"], 4 * e.i + j + 1)
                    act.activation(mixH[:, e.tile + j, :], tmp[:, (e.item + j) % 4, :], ACT.Copy).then_inc(s["mix_hi"], 1)

            t["pu"].k = SPLIT_IN_SSD
            pooled = None
            for e in EVENTS:
                n = e.ahead - t["pu"].k
                t["pu"].add(n)
                if e.kind == "in":
                    if e.i >= 2:
                        split(n)
                        act.wait_ge(s["pool_f"], 2 * (e.i - 1))
                    else:
                        act.wait_ge(s["st_used"], GROUPS * NSAMP)
                    finished(4)
                    for j in range(2):
                        act.activation(U[:, e.i % 2, j, POOL_HIST:UT], SETS[e.blocks[0] % 4][j][:, 0:T], ACT.Copy)\
                           .then_inc(s["uraw"], 1)
                    if e.i < 2:
                        split(n)
                    if e.i == 0:
                        act.wait_ge(s["tails_out"], 16)
                        act.wait_ge(s["fst_free"], GROUPS + 1)
                else:
                    split(n)
                    t["done"].add(2)
                if pooled:
                    high(pooled)
                pooled = e if e.kind == "in" else None
                if e.kind == "proj":
                    high(e)
            for br in range(2):
                extra = 4 * br
                with rounds(act, 8, t, dict(unit=8 + extra, done=8 + extra, br=2, **({"mf": 2} if br else {}))):
                    split(4)
                    finished(4)
                    act.wait_ge(s["br_read"], START["br_read"] + t["br"].now())
                    for j in range(2):
                        act.activation(sgA[:, j, :], SETS[0][j][:, 0:T], ACT.Sigmoid).then_inc(s["sgm"], 1)
                    t["br"].add(2)
                    split(4 + extra)
                    t["done"].add(4 + extra)
                    if br:
                        i = t["mf"].now()
                        for j in range(2):
                            act.wait_ge(s["br_read"], START["br_read"] + t["br"].now(1 - j))
                            act.activation(flat(mixH[:, bass.ds(i + j, 1), :]), tmp[:, j, :], ACT.Copy)\
                               .then_inc(s["mix_hi"], 1)
                        t["mf"].add(2)
            for b in range(8):
                if b % 2:
                    c = b // 2
                    act.wait_ge(s[f"mem_in{c % 2}"], 16 * (c // 2) + 16)
                    act.activation(flat(memH[:, 4 * c:4 * c + 4, :]), memraw[:, c % 2, :], ACT.Copy)\
                       .then_inc(s["mem_hi"], 1)
                split(4)
                t["done"].add(4)

            def ln_stats(sqb, meanb, splits=0):
                act.wait_ge(s["ln_sum"], t["ln"].add())
                act.activation(meanb[:, :], M[0][:, 0:T], ACT.Copy, scale=1.0 / D_MODEL).then_inc(s["mean_ready"], 1)
                for c in range(4):
                    act.wait_ge(s["cen_ready"], t["cen"].add())
                    if t["sqc"].k >= 2:
                        act.wait_ge(s["sqc_used"], t["sqc"].k - 1)
                    act.activation(sqb[:, c % 2, :], flat(resid[:, 4 * c:4 * c + 4, :]), ACT.Square)\
                       .then_inc(s["sqc_ready"], 1)
                    t["sqc"].add()
                    if c % 2:
                        split(splits)

            def ln_sd(rb):
                act.wait_ge(s["sqc_used"], t["var"].add(4))
                act.activation(rb[:, :], M[1][:, 0:T], ACT.Sqrt, scale=1.0 / D_MODEL, bias=eps[:, 1:2])\
                   .then_inc(s["lsd_ready"], 1)

            def ln_high(c):
                act.wait_ge(s["xn_ready"], t["xn"].add())
                act.activation(flat(xH[:, 4 * c:4 * c + 4, :]), flat(resid[:, 4 * c:4 * c + 4, :]), ACT.Copy)\
                   .then_inc(s["x_hi"], 1)

            def keys(b):
                finished(4)
                for j in range(2):
                    act.activation(KTm[:, 2 * b + j, :], SETS[b][j][:, 0:N_MEM], ACT.Copy).then_inc(s["kt_ready"], 1)

            def values(b):
                finished(4)
                for m in range(2):
                    act.activation(Vn[:, m, b * BLK:b * BLK + BLK], SETS[3 * b][m][:, 0:BLK], ACT.Copy)\
                       .then_inc(s["vn_ready"], 1)

            def queries(b):
                finished(4)
                for j in range(2):
                    act.activation(qT[:, 2 * b + j, :], SETS[2 + b][j][:, 0:T], ACT.Copy).then_inc(s["q_ready"], 1)

            ln_stats(sq, mean, splits=2)
            ln_sd(lrstd)
            split(1)
            ln_high(0)
            keys(0)
            split(1)
            ln_high(1)
            split(1)
            ln_high(2)
            split(1)
            ln_high(3)
            keys(1)
            split(4)
            queries(0)
            split(4)
            queries(1)

            def exps(h):
                act.wait_ge(s["mx_ready"], h + 1)
                for b in range(2):
                    n = 2 * h + b
                    act.activation(Pe[:, n, :], M[h][:, b * N_MEM:b * N_MEM + N_MEM], ACT.Exp, bias=snm[:, n:n + 1],
                                   scale=MHD ** -0.5, accum_out=srs[:, n:n + 1]).then_inc(s["p_ready"], 1)

            for h in range(MH):
                exps(h)
            split(1)
            act.wait_ge(s["ss_ps"], MH)
            act.activation(flat(ssT[:, :, :]), G[1][0][:, 0:64], ACT.Copy).then_inc(s["ss_sb"], 1)
            split(1)
            act.wait_ge(s["smx_ready"], 1)
            act.activation(sP[:, :], G[1][0][0:32, 64:64 + N_MEM], ACT.Exp, bias=snm[0:32, 8:9],
                           scale=MHD ** -0.5, accum_out=srs[0:32, 8:9]).then_inc(s["sp_exp"], 1)
            split(2)
            values(0)

            def transposed(h):
                act.wait_ge(s["pt_ps"], h + 1)
                if h >= 2:
                    act.wait_ge(s["o_ps"], h - 1)
                act.activation(PT[:, h % 2, :], G[1 - h % 2][1][:, :], ACT.Copy).then_inc(s["pt_ready"], 1)

            def output_high(h):
                act.wait_ge(s["o_ps"], h + 1)
                act.activation(oH[:, h, 0:SEQ], attended(h), ACT.Copy).then_inc(s["o_hi"], 1)

            split(1)
            act.wait_ge(s["spt_ps"], 1)
            act.activation(flat(sPT[:, :, :]), G[1][0][:, 320:384], ACT.Copy).then_inc(s["spt_sb"], 1)
            transposed(0)
            split(1)
            transposed(1)
            split(1)
            transposed(2)
            output_high(0)
            split(1)
            transposed(3)
            output_high(1)
            values(1)
            act.wait_ge(s["so_ps"], MH)
            act.activation(oH[:, :, SEQ:T], G[1][0][:, 384:384 + MH * NSAMP].rearrange("p (h b) -> p h b", h=MH), ACT.Copy)\
               .then_inc(s["o_hi"], 1)
            output_high(2)
            output_high(3)
            split(7)
            t["done"].add(8)
            act.wait_ge(s["kv_out"], 32)
            ln_stats(sq2, mean2)
            split(1)
            ln_sd(lrstd2)
            for c in range(4):
                ln_high(c)
            def outers(r, c):
                act.wait_ge(s[f"b_in{c}"], t[f"b_in{c}"].add() * 16)
                for b in range(2):
                    act.wait_ge(s["st_done"], t["std"].add() + START["st_done"] - 2)
                    for i in range(XPG):
                        col = dtxc[:, bass.ds(r * 4 + (2 * c + b), 1), i:i + 1].rearrange("p a b -> p (a b)")
                        last = act.activation(outer[:, b, i, :], bcb[:, c, b * P:b * P + P], ACT.Copy, scale=col)
                    last.then_inc(s["out_ready"], 1)

            for n, with_states in ((16, True), (FT // 2 - 16, False)):
                extra = dict(std=4, b_in0=1, b_in1=1) if with_states else {}
                with rounds(act, n, t, dict(unit=8, done=8, h=2, **extra)) as r:
                    split(4)
                    if with_states:
                        outers(r, 0)
                    finished(4)
                    act.wait_ge(s["h_read"], START["h_read"] + t["h"].now())
                    for j in range(2):
                        act.activation(sgF[:, j, :], SETS[0][j][:, 0:T], ACT.Silu).then_inc(s["sgm"], 1)
                    split(4)
                    if with_states:
                        outers(r, 1)
                    t["done"].add(4)
                    i = t["h"].now()
                    for j in range(2):
                        act.wait_ge(s["h_read"], START["h_read"] + t["h"].add())
                        act.activation(flat(hH[:, bass.ds(i + j, 1), :]), hf[:, j, :], ACT.Copy).then_inc(s["h_hi"], 1)
            for b in range(8):
                split(11 if b < 7 else 7)
            act.wait_ge(s["st_out0"], 16 * 16)
            act.wait_ge(s["st_out1"], 16 * 16)
            ln_stats(sq2, mean2)
            ln_sd(lrstd2)

        @block.vector
        def _(dve):
            t = Tallies()

            def step(ins):
                ins.then_inc(dve_step, 1)
                dve.wait_ge(dve_step, t["step"].add())

            def mark(ins):
                ins.then_inc(dve_step, 1)
                return t["step"].add()

            def after(count):
                dve.wait_ge(dve_step, count)

            def split(n):
                u = t["unit"]
                for _ in range(n):
                    slot = u.k % RING
                    dve.wait_ge(hi_ready, u.add())
                    dve.tensor_tensor(wlo[:, slot, :], raw[:, slot, :], whi[:, slot, :].bitcast(F32), ALU.subtract)\
                       .then_inc(lo_ready, 1)

            def finished(units):
                dve.wait_ge(used, t["done"].add(units) + RING)

            dve.memset(eps[:, 0:1], RMS_EPS)
            dve.memset(eps[:, 1:2], LN_EPS)
            dve.memset(R[:, :, 0:CONV_W - 1], 0.0)
            dve.memset(ones[:, :], 1.0).then_inc(s["ones_set"], 1)
            dve.sem_inc(lo_ready, RING)
            for c in range(4):
                dve.wait_ge(s["x_hi"], c + 1)
                dve.tensor_tensor(flat(xL[:, 4 * c:4 * c + 4, :]), flat(resid[:, 4 * c:4 * c + 4, :]),
                                  flat(xH[:, 4 * c:4 * c + 4, :]).bitcast(F32), ALU.subtract).then_inc(s["x_lo"], 1)
                if c == 1:
                    split(1)
            split(3)

            def conv_block():
                n = t["raw"]
                if n.reg is not None or n.k >= 2:
                    dve.wait_ge(s["xbc_ready"], n.now())
                idx = [n.now() + j for j in range(2)]
                ct = lambda x, j: x[:, idx[j], :] if isinstance(idx[j], int) else flat(x[:, bass.ds(idx[j], 1), :])
                w = lambda k, j: vcol("conv_w", idx[j] * CONV_W + k)
                marks = []
                for j in range(2):
                    dve.wait_ge(s["raw_ready"], n.add())
                    marks.append(mark(dve.tensor_scalar(cacc[:, j, :], R[:, j, CONV_W - 1:CONV_W - 1 + T],
                                                        w(CONV_W - 1, j), vcol("conv_b", idx[j]), ALU.mult, ALU.add)))
                for j in range(2):
                    dve.tensor_copy(ct(tails, j), R[:, j, SEQ:SEQ + 11])
                for j in range(2):
                    after(marks[j])
                    last = dve.tensor_tensor(cacc[:, j, SEQ:T], cacc[:, j, SEQ:T], ct(chist, j), ALU.add)
                for k in range(CONV_W - 1):
                    for j in range(2):
                        if k:
                            after(marks[j])
                        ins = dve.scalar_tensor_tensor(out=cacc[:, j, 0:SEQ], in0=R[:, j, k:k + SEQ], scalar=w(k, j),
                                                       in1=cacc[:, j, 0:SEQ], op0=ALU.mult, op1=ALU.add)
                        if k < CONV_W - 2:
                            marks[j] = mark(ins)
                        else:
                            ins.then_inc(s["conv_done"], 1)

            dve.wait_ge(in_misc, N_MISC * 16)
            cw = vec[:, 0:CT * CONV_W].rearrange("p (c k) -> p c k", k=CONV_W)
            hv = hist[:, :, :].rearrange("p c (b k) -> p c b k", k=CONV_W - 1)
            for k in range(CONV_W - 1):
                dst = chist if k == 0 else ctmp
                step(dve.tensor_tensor(dst[:, :, :], hv[:, :, :, k], cw[:, :, k:k + 1].to_broadcast([P, CT, NSAMP]), ALU.mult))
                if k:
                    step(dve.tensor_tensor(chist[:, :, :], chist[:, :, :], ctmp[:, :, :], ALU.add))
            split(4)
            for g, w in enumerate(WINDOWS):
                last = dve.tensor_reduce(phs[:, 4 * g:4 * g + 4, :], hpool[:, 4 * g:4 * g + 4, :, POOL_HIST - (w - 1):POOL_HIST],
                                         AX_X, ALU.add)
            step(last)
            dve.wait_ge(s["dt_psum"], 1)
            dve.tensor_scalar(S[:, 2, :], M[0][0:HEADS, 0:T], pcol[:, 0:1], None, ALU.add).then_inc(s["dt_z"], 1)
            step(dve.tensor_scalar(pcol[:, 3:4], pcol[:, 2:3], -1.0, None, ALU.mult))
            finished(4)
            conv_block()
            dve.wait_ge(s["dt_exp"], 1)
            dve.tensor_scalar(S[:, 5, :], S[:, 4, :], 1.0, None, ALU.add).then_inc(s["dt_u"], 1)
            dve.wait_ge(s["dt_u"], 1)
            step(dve.tensor_scalar(S[:, 3, :], S[:, 5, :], -1.0, 1e-30, ALU.add, ALU.max))
            step(dve.reciprocal(S[:, 7, :], S[:, 3, :]))
            split(1)
            step(dve.tensor_tensor(S[:, 3, :], S[:, 7, :], S[:, 4, :], ALU.mult))
            dve.wait_ge(s["dt_ln"], 1)
            step(dve.tensor_tensor(S[:, 7, :], S[:, 3, :], S[:, 6, :], ALU.mult))
            step(dve.scalar_tensor_tensor(out=S[:, 3, :], in0=S[:, 5, :], scalar=1.0, in1=S[:, 4, :],
                                          op0=ALU.is_equal, op1=ALU.mult))
            step(dve.tensor_tensor(S[:, 6, :], S[:, 7, :], S[:, 3, :], ALU.add))
            step(dve.scalar_tensor_tensor(out=S[:, 7, :], in0=S[:, 2, :], scalar=0.0, in1=S[:, 6, :],
                                          op0=ALU.max, op1=ALU.add))
            step(dve.tensor_copy(pxs[:, 0:NSAMP], S[:, 7, SEQ:T]))
            dve.tensor_scalar(S[:, 0, :], S[:, 7, :], pcol[:, 3:4], None, ALU.mult).then_inc(s["dt_ready"], 1)
            split(3)
            finished(4)
            conv_block()
            dve.wait_ge(s["dA_tok_ps"], 1)
            dve.tensor_copy(flat(dAtok[:, :, :]), M[1][:, 0:2 * HEADS]).then_inc(s["dA_tok"], 1)
            dve.tensor_copy(flat(dttok[:, :, :]), M[1][:, P:P + 2 * HEADS]).then_inc(s["dA_tok"], 1)
            split(2)
            dve.wait_ge(s["cum_ps"], 1)
            dve.tensor_copy(S[:, 1, 0:SEQ], M[0][0:HEADS, 0:SEQ]).then_inc(s["cum_sb"], 1)
            split(2)
            dve.wait_ge(s["cumt_ps"], 1)
            step(dve.tensor_scalar(flat(ncum[:, :, :]), M[1][:, 256:256 + 2 * HEADS], -1.0, None, ALU.mult))
            dve.tensor_tensor(wtok[:, 0, :], ncum[:, 0, :], M[0][:, 384:384 + HEADS], ALU.add)
            dve.tensor_tensor(wtok[:, 1, :], ncum[:, 1, :], M[0][:, 384:384 + HEADS], ALU.add).then_inc(s["w_sum"], 1)
            finished(4)
            conv_block()

            def heads(h0, parts=(0, 1)):
                if 0 in parts:
                    exponents(h0)
                if 1 in parts:
                    for h in (h0, h0 + 1):
                        m = t["m"]
                        if h >= 3:
                            dve.wait_ge(s["y_done"], m.now(2))
                        dve.wait_ge(s["e_ready"], m.add())
                        dve.tensor_tensor(MM[:, h % 3, :], E[:, h % 2, :], cbm[:, :], ALU.mult).then_inc(s["m_ready"], 1)

            def exponents(h0):
                if h0 == 0:
                    dve.wait_ge(s["cum_in"], t["cum"].add() * 16)
                for h in (h0, h0 + 1):
                    if h >= 2:
                        dve.wait_ge(s["m_ready"], t["m"].now(1 - h % 2))
                    hc = t["g"].now() * HPG + h
                    n = [ncum[:, b, hc:hc + 1] if isinstance(hc, int) else ncum[:, b, bass.ds(hc, 1)] for b in range(2)]
                    dve.tensor_scalar(E[:, h % 2, 0:SEQ], cumbc[:, h, :], n[0], 0.0, ALU.add, ALU.min)
                    dve.tensor_scalar(E[:, h % 2, SEQ:384], cumbc[:, h, P:SEQ], n[1], 0.0, ALU.add, ALU.min)\
                       .then_inc(s["seg_ready"], 1)

            def group(last=False):
                gh = t["g"].now() * HPG
                gx = t["g"].now() * XPG
                per_head = (lambda x, b: x[:, b, gh:gh + HPG]) if isinstance(gh, int) else (
                    lambda x, b: x[:, b, bass.ds(gh, HPG)])
                split(2)
                exponents(0)
                dve.wait_ge(s["xtok_ps"], t["xtok"].add())
                dve.tensor_tensor(bcp[:, :], BT[:, SEQ:T], CTt[:, SEQ:T], ALU.mult).then_inc(s["bcp_ready"], 1)
                for b in range(2):
                    dve.tensor_tensor(xdt[:, b, :].rearrange("p (h c) -> p h c", h=HPG),
                                      M[b][:, :].rearrange("p (h c) -> p h c", h=HPG),
                                      per_head(dttok, b).rearrange("p (h o) -> p h o", o=1).to_broadcast([P, HPG, 64]),
                                      ALU.mult).then_inc(s["xdt_ready"], 1)
                dve.wait_ge(s["cb_ps"], t["cb"].add())
                step(dve.tensor_tensor(cbm[:, :], M[3][:, 0:384], cmask[:, :], ALU.mult))
                heads(0, parts=(1,))
                split(2)
                heads(2)
                split(1)
                heads(4)
                split(1)
                heads(6)
                split(2)
                t["done"].add(8)
                dve.wait_ge(s["y_done"], t["m"].now())
                for b in range(2):
                    ins = dve.tensor_tensor(xdt[:, b, :].rearrange("p (h c) -> p h c", h=HPG),
                                            xdt[:, b, :].rearrange("p (h c) -> p h c", h=HPG),
                                            per_head(wtok, b).rearrange("p (h o) -> p h o", o=1).to_broadcast([P, HPG, 64]),
                                            ALU.mult)
                ins.then_inc(s["xw_ready"], 1)
                sl = dts[:, gx:gx + XPG, :] if isinstance(gx, int) else dts[:, bass.ds(gx, XPG), :]
                step(dve.tensor_tensor(dtx[:, :, :], sl[:, :, 0:NSAMP], xs[:, :, SEQ:T], ALU.mult))
                gb = t["g"].now() * NSAMP
                kept = dtxc[:, gb:gb + NSAMP, :] if isinstance(gb, int) else dtxc[:, bass.ds(gb, NSAMP), :]
                dve.tensor_copy(kept.rearrange("p b i -> p i b"), dtx[:, :, :])
                dve.wait_ge(s["ys_ps"], t["ysp"].add())
                dve.tensor_tensor(ysbc[:, :, :], dtx[:, :, :], M[3][:, 416:416 + NSAMP].rearrange(
                    "p (o b) -> p o b", o=1).to_broadcast([P, XPG, NSAMP]), ALU.mult)
                step(dve.tensor_tensor(ysamp[:, :, :], sl[:, :, NSAMP:2 * NSAMP], M[3][:, 384:384 + XPG * NSAMP].rearrange(
                    "p (i b) -> p i b", b=NSAMP), ALU.mult))
                ys = mark(dve.tensor_tensor(ysamp[:, :, :], ysamp[:, :, :], ysbc[:, :, :], ALU.add))
                for i in range(XPG):
                    split(1)
                    if i < 2:
                        for k in (2 * i, 2 * i + 1):
                            dve.scalar_tensor_tensor(out=yg[:, k, 0:SEQ], in0=xs[:, k, 0:SEQ], scalar=vcol("d_skip", gx + k),
                                                     in1=M[k // 2][:, (k % 2) * SEQ:(k % 2) * SEQ + SEQ], op0=ALU.mult,
                                                     op1=ALU.add)
                    if i == 1:
                        after(ys)
                        for k in range(XPG):
                            ins = dve.scalar_tensor_tensor(out=yg[:, k, SEQ:T], in0=xs[:, k, SEQ:T],
                                                           scalar=vcol("d_skip", gx + k), in1=ysamp[:, k, :],
                                                           op0=ALU.mult, op1=ALU.add)
                        yd = mark(ins)
                    if i == 2:
                        dve.wait_ge(s["z_ready"], t["z"].add(XPG))
                        after(yd)
                        for k in range(XPG):
                            dve.tensor_tensor(yg[:, k, :], yg[:, k, :], zs[:, k, :], ALU.mult).then_inc(s["y2_ready"], 1)
                for k in (1, 3):
                    dve.wait_ge(s["sq_ready"], t["sq"].add(2))
                    sq_pair = mark(dve.tensor_tensor(zs[:, k - 1, :], zs[:, k - 1, :], zs[:, k, :], ALU.add))
                if not last:
                    t["done"].add(4)
                    conv_block()
                after(sq_pair)
                dve.tensor_tensor(zs[:, 0, :], zs[:, 0, :], zs[:, 2, :], ALU.add).then_inc(s["sq_sum"], 1)
                split(4)
                if not last:
                    t["done"].add(4)
                    conv_block()
                split(1)
                dve.wait_ge(s["sd_ready"], t["sd"].add())
                rs = mark(dve.reciprocal(rstd, rstd))
                split(1)
                after(rs)
                for i in range(XPG):
                    dve.scalar_tensor_tensor(out=yg[:, i, :], in0=yg[:, i, :], scalar=vcol("norm_w", gx + i),
                                             in1=rstd, op0=ALU.mult, op1=ALU.mult).then_inc(s["y3_ready"], 1)
                if not last:
                    split(2)
                    t["done"].add(4)
                    conv_block()
                for i in range(XPG):
                    dve.wait_ge(s["yh_ready"], t["yh"].add())
                    one = (lambda x: x[:, gx + i, :]) if isinstance(gx, int) else (lambda x: flat(x[:, bass.ds(gx + i, 1), :]))
                    dve.tensor_tensor(one(yL), yg[:, i, :], one(yH).bitcast(F32), ALU.subtract).then_inc(s["yl_ready"], 1)
                t["g"].add()

            dve.wait_ge(s["pre_done"], 1)
            dve.wait_ge(s["dts_in"], 32)
            dve.tensor_copy(decc[:, :, :].rearrange("p (g b) i -> p g i b", g=GROUPS),
                            dts[:, :, NSAMP:2 * NSAMP].rearrange("p (g i) b -> p g i b", g=GROUPS))
            with rounds(dve, GROUPS - 1, t, dict(unit=20, done=20, raw=6, m=8, g=1, xtok=1, cb=1, ysp=1,
                                                 z=4, sd=1, yh=4, cum=1, sq=4, step=STEPS)):
                group()
            group(last=True)
            dve.wait_ge(s["tails_out"], 16)
            dve.wait_ge(s["yl_ready"], YT)
            dve.wait_ge(s["st_used"], GROUPS * NSAMP)
            last = dve.memset(U[:, :, :, 0:POOL_HIST], 0.0)
            step(last)

            def low(e):
                for j in range(e.tiles):
                    dve.wait_ge(s["mix_hi"], e.item + j + 1)
                    dve.tensor_tensor(mixL[:, e.tile + j, :], tmp[:, (e.item + j) % 4, :],
                                      mixH[:, e.tile + j, :].bitcast(F32), ALU.subtract).then_inc(s["mix_lo"], 1)

            def pool_pair(e):
                g, w = e.group, WINDOWS[e.group]
                out = [tmp[:, (e.item + j) % 4, :] for j in range(2)]
                cur, reach, marks = [U[:, e.i % 2, j, :] for j in range(2)], 1, [None, None]
                src = list(cur)
                for j in range(2):
                    dve.wait_ge(s["uraw"], 2 * e.i + j + 1)
                    dve.tensor_copy(utail[:, e.tile + j, :], src[j][:, SEQ:UT])
                if e.i:
                    dve.wait_ge(s["pool_f"], 2 * e.i)
                while reach < w:
                    for j in range(2):
                        v = V[:, (reach.bit_length() - 1) % 2, j, :]
                        if marks[j] is not None:
                            after(marks[j])
                        marks[j] = mark(dve.tensor_tensor(v[:, 2 * reach - 1:POOL_HIST + SEQ],
                                                          cur[j][:, 2 * reach - 1:POOL_HIST + SEQ],
                                                          cur[j][:, reach - 1:POOL_HIST + SEQ - reach], ALU.add))
                        cur[j] = v
                    reach *= 2
                for j in range(2):
                    after(marks[j])
                    dve.tensor_tensor(cur[j][:, POOL_HIST + SEQ:UT], src[j][:, POOL_HIST + SEQ:UT],
                                      phs[:, e.tile + j, :], ALU.add)
                    marks[j] = mark(dve.tensor_tensor(out[j][:, 0:16], cur[j][:, POOL_HIST:POOL_HIST + 16], rc[:, g, :],
                                                      ALU.mult))
                for j in range(2):
                    after(marks[j])
                    marks[j] = mark(dve.tensor_tensor(out[j][:, 0:16], out[j][:, 0:16], src[j][:, POOL_HIST:POOL_HIST + 16],
                                                      ALU.subtract))
                for j in range(2):
                    dve.scalar_tensor_tensor(out=out[j][:, 16:T], in0=cur[j][:, POOL_HIST + 16:UT], scalar=1.0 / w,
                                             in1=src[j][:, POOL_HIST + 16:UT], op0=ALU.mult, op1=ALU.subtract)\
                       .then_inc(s["pool_f"], 1)

            t["pu"].k = SPLIT_IN_SSD
            pooled = None
            for e in EVENTS:
                n = e.ahead - t["pu"].k
                split(n)
                t["pu"].add(n)
                t["done"].add(e.end - e.start)
                if pooled and e.kind == "proj":
                    low(pooled)
                    pooled = None
                if e.item >= 4:
                    dve.wait_ge(s["mix_lo"], e.item + e.tiles - 4)
                if e.kind == "in":
                    pool_pair(e)
                    if pooled:
                        low(pooled)
                    pooled = e
                else:
                    dve.wait_ge(used, t["done"].now() + RING)
                    for j in range(4):
                        dve.tensor_scalar(tmp[:, (e.item + j) % 4, :], SETS[e.blocks[j // 2] % 4][j % 2][:, 0:T],
                                          vcol("pool_scale", e.tile + j), None, ALU.mult).then_inc(s["wp_ready"], 1)
                    low(e)
            for br in range(2):
                extra = 4 * br
                with rounds(dve, 8, t, dict(unit=8 + extra, done=8 + extra, sg=2, br=2,
                                            **({"step": 2, "mh": 2} if br else {}))):
                    split(8 + extra)
                    i = t["br"].now() if br == 0 else t["mh"].now()
                    dve.wait_ge(s["sgm"], START["sgm"] + t["sg"].add(2))
                    finished(8 + extra)
                    for j in range(2):
                        r = flat(resid[:, bass.ds(i + j, 1), :])
                        if br == 0:
                            dve.tensor_tensor(r, SETS[1][j][:, 0:T], sgA[:, j, :], ALU.mult).then_inc(s["br_read"], 1)
                            t["br"].add()
                        else:
                            step(dve.tensor_tensor(tmp[:, j, :], SETS[1][j][:, 0:T], sgA[:, j, :], ALU.mult))
                            dve.tensor_tensor(tmp[:, j, :], tmp[:, j, :], r, ALU.add).then_inc(s["br_read"], 1)
                            t["br"].add()
                    if br:
                        for j in range(2):
                            dve.wait_ge(s["mix_hi"], t["mh"].add() + 2 * KT)
                            m = lambda x: flat(x[:, bass.ds(i + j, 1), :])
                            dve.tensor_tensor(m(mixL), tmp[:, j, :], m(mixH).bitcast(F32), ALU.subtract)\
                               .then_inc(s["mix_lo"], 1)

            def residual(b, units, first=0, sets=2, parts=False):
                finished(units)
                marks = []
                for j in range(2):
                    k = 2 * b + j
                    x = xH[:, k, :].bitcast(F32) if parts else resid[:, k, :]
                    ins = dve.scalar_tensor_tensor(out=resid[:, k, :], in0=x, scalar=ALPHA,
                                                   in1=SETS[first + b % sets][j][:, 0:T], op0=ALU.mult, op1=ALU.add)
                    if parts:
                        marks.append(mark(ins))
                    else:
                        ins.then_inc(s["res_ready"], 1)
                for j in range(2):
                    k = 2 * b + j
                    if parts:
                        after(marks[j])
                        dve.scalar_tensor_tensor(out=resid[:, k, :], in0=xL[:, k, :].bitcast(F32), scalar=ALPHA,
                                                 in1=resid[:, k, :], op0=ALU.mult, op1=ALU.add).then_inc(s["res_ready"], 1)
                t["rr"].add(2)
                if b == 7:
                    return
                for j in range(1 if b == 0 else 0, 2):
                    dve.wait_ge(s["res_ready"], t["rr"].now(1 - j) + START["res_ready"])
                    if b or j == 0:
                        after(t["step"].now())
                    ins = dve.tensor_tensor(total[:, :], total[:, :] if b else resid[:, 0, :], resid[:, 2 * b + j, :], ALU.add)
                    if b == 6 and j == 1:
                        ins.then_inc(s["sum_ready"], 1)
                    else:
                        mark(ins)

            for b in range(8):
                if b % 2:
                    c = b // 2
                    dve.wait_ge(s["mem_hi"], c + 1)
                    dve.tensor_tensor(flat(memL[:, 4 * c:4 * c + 4, :]), memraw[:, c % 2, :],
                                      flat(memH[:, 4 * c:4 * c + 4, :]).bitcast(F32), ALU.subtract).then_inc(s["mem_lo"], 1)
                split(4)
                residual(b, 4, first=2, parts=True)

            def chunk(c):
                return resid[:, 4 * c:4 * c + 4, :]

            def spread(v):
                return v[:, :].rearrange("p (o t) -> p o t", o=1).to_broadcast([P, 4, T])

            def ln_center(meanb):
                dve.wait_ge(s["mean_ready"], t["mean"].add())
                for c in range(4):
                    dve.tensor_tensor(chunk(c), chunk(c), spread(meanb), ALU.subtract).then_inc(s["cen_ready"], 1)

            def ln_rstd(rb):
                dve.wait_ge(s["lsd_ready"], t["lsd"].add())
                step(dve.reciprocal(rb[:, :], rb[:, :]))

            def ln_scale(c, rb, which):
                step(dve.tensor_tensor(chunk(c), chunk(c), spread(rb), ALU.mult))
                for k in range(4 * c, 4 * c + 4):
                    last = dve.tensor_scalar(resid[:, k, :], resid[:, k, :], vcol(f"ln_{which}_g", k), vcol(f"ln_{which}_b", k),
                                             ALU.mult, ALU.add)
                last.then_inc(s["xn_ready"], 1)

            def ln_low(c):
                dve.wait_ge(s["x_hi"], t["xh"].add() + 4)
                dve.tensor_tensor(flat(xL[:, 4 * c:4 * c + 4, :]), flat(chunk(c)),
                                  flat(xH[:, 4 * c:4 * c + 4, :]).bitcast(F32), ALU.subtract).then_inc(s["x_lo"], 1)

            ln_center(mean)
            split(4)
            ln_rstd(lrstd)
            for c in range(4):
                ln_scale(c, lrstd, "mix")
                split(1)
                ln_low(c)
            split(8)
            t["done"].add(16)
            for h in range(MH):
                dve.wait_ge(s["sc_ps"], h + 1)
                step(dve.tensor_reduce(smx[:, 2 * h:2 * h + 2], M[h][:, :].rearrange("p (b m) -> p b m", b=2), AX_X, ALU.max))
                dve.tensor_scalar(snm[:, 2 * h:2 * h + 2], smx[:, 2 * h:2 * h + 2], -MHD ** -0.5, None, ALU.mult)\
                   .then_inc(s["mx_ready"], 1)
            def normalised(h):
                for n in (2 * h, 2 * h + 1):
                    dve.wait_ge(s["p_ready"], n + 1)
                step(dve.reciprocal(sri[:, 2 * h:2 * h + 2], srs[:, 2 * h:2 * h + 2]))
                for n in (2 * h, 2 * h + 1):
                    dve.tensor_scalar(Pe[:, n, :], Pe[:, n, :], sri[:, n:n + 1], None, ALU.mult).then_inc(s["pn_ready"], 1)

            normalised(0)
            normalised(1)
            split(1)
            normalised(2)
            normalised(3)
            split(1)
            dve.wait_ge(s["sst_ps"], 1)
            step(dve.tensor_reduce(smx[0:32, 8:9], G[1][0][0:32, 64:64 + N_MEM], AX_X, ALU.max))
            dve.tensor_scalar(snm[0:32, 8:9], smx[0:32, 8:9], -MHD ** -0.5, None, ALU.mult).then_inc(s["smx_ready"], 1)
            dve.wait_ge(s["sp_exp"], 1)
            step(dve.reciprocal(sri[0:32, 8:9], srs[0:32, 8:9]))
            dve.tensor_scalar(sP[:, :], sP[:, :], sri[0:32, 8:9], None, ALU.mult).then_inc(s["sp_n"], 1)
            split(6)
            t["done"].add(8)

            def output_low(h, n):
                dve.wait_ge(s["o_hi"], n)
                dve.tensor_tensor(oL[:, h, 0:SEQ], attended(h), oH[:, h, 0:SEQ].bitcast(F32), ALU.subtract)\
                   .then_inc(s["o_lo"], 1)

            output_low(0, 1)
            output_low(1, 2)
            dve.wait_ge(s["o_hi"], 3)
            dve.tensor_tensor(oL[:, :, SEQ:T], G[1][0][:, 384:384 + MH * NSAMP].rearrange("p (h b) -> p h b", h=MH),
                              oH[:, :, SEQ:T].bitcast(F32), ALU.subtract).then_inc(s["o_lo"], 1)
            output_low(2, 4)
            output_low(3, 5)
            for b in range(8):
                if b < 7:
                    split(1)
                residual(b, 1, sets=4)
            ln_center(mean2)
            split(1)
            ln_rstd(lrstd2)
            for c in range(4):
                ln_scale(c, lrstd2, "mem")
                ln_low(c)
            def states(r, c):
                dve.wait_ge(s[f"st_in{c}"], 16 * 2 * GROUPS + t[f"s_in{c}"].add() * 16)
                for b in range(2):
                    dve.wait_ge(s["out_ready"], t["out"].add())
                    for i in range(XPG):
                        col = decc[:, bass.ds(r * 4 + (2 * c + b), 1), i:i + 1].rearrange("p a b -> p (a b)")
                        ins = dve.scalar_tensor_tensor(out=st[:, c, b, i, :], in0=st[:, c, b, i, :], scalar=col,
                                                       in1=outer[:, b, i, :], op0=ALU.mult, op1=ALU.add)
                    ins.then_inc(s["st_done"], 1)

            for n, with_states in ((16, True), (FT // 2 - 16, False)):
                extra = dict(out=4, s_in0=1, s_in1=1) if with_states else {}
                with rounds(dve, n, t, dict(unit=8, done=8, sg=2, h=2, **extra)) as r:
                    split(4)
                    if with_states:
                        states(r, 0)
                    split(4)
                    if with_states:
                        states(r, 1)
                    finished(8)
                    dve.wait_ge(s["sgm"], START["sgm"] + t["sg"].add(2))
                    i = t["h"].now()
                    dve.wait_ge(s["h_hi"], START["h_hi"] + t["h"].now())
                    for j in range(2):
                        dve.tensor_tensor(hf[:, j, :], SETS[1][j][:, 0:T], sgF[:, j, :], ALU.mult).then_inc(s["h_read"], 1)
                    for j in range(2):
                        dve.wait_ge(s["h_hi"], START["h_hi"] + t["h"].add())
                        m = lambda x: flat(x[:, bass.ds(i + j, 1), :])
                        dve.tensor_tensor(m(hL), hf[:, j, :], m(hH).bitcast(F32), ALU.subtract).then_inc(s["h_lo"], 1)
            for b in range(8):
                split(11 if b < 7 else 7)
                residual(b, 11)
            ln_center(mean2)
            ln_rstd(lrstd2)
            for c in range(4):
                ln_scale(c, lrstd2, "ffn")


        @block.gpsimd
        def _(pool):
            t = Tallies()
            misc = ((ident[:, :], a["ident"]), (vec[:, :], a["vecs"]), (cmask[:, :], a["cmask"]),
                    (flat(rc[:, :, :]), a["rc"]), (flat(wdt[:, :, :]), a["wdt"]), (flat(hist[:, :, :]), a["hist"]),
                    (hpool[:, :, :, :].rearrange("p k b j -> p (k b j)"), a["hpool"]),
                    (pcol[:, 0:1], a["dt_bias"]), (pcol[:, 1:2], a["a_log"]))
            assert len(misc) == N_MISC
            for dst, src in misc:
                pool.dma_start(dst, src).then_inc(in_misc, 16)
            pool.dma_start(o["pass_conv"], a["state_conv"][:, 1:CONV_W - 1, :]).then_inc(s["outs"], 16)
            pool.dma_start(o["pass_pool"], a["state_pool"][:, 1:POOL_HIST, :]).then_inc(s["outs"], 16)
            pool.wait_ge(s["cum_sb"], 1)
            pool.dma_start(scr_cum, S[:, 1, 0:SEQ]).then_inc(s["scr_out"], 16)
            pool.wait_ge(s["pre_exp"], 1)
            pool.dma_start(scr_dts, pxs[:, :]).then_inc(s["scr_out"], 16)
            pool.wait_ge(s["scr_out"], 32)
            for half in range(2):
                src = scr_dts.rearrange("(t h) k -> h t k", h=2)[half:half + 1]
                pool.dma_start(dts[64 * half:64 * half + 64, :, :], src.to_broadcast([64, YT, 2 * NSAMP]))\
                    .then_inc(s["dts_in"], 16)

            def alone(semaphore, count):
                pool.wait_ge(semaphore, count)
                pool.sem_inc(s["pool_past"], 1)

            with rounds(pool, GROUPS, t, {}) as g:
                alone(s["seg_ready"], g * HPG + START["seg_ready"])
                pool.dma_start(flat(cumbc[:, :, :]), scr_cum[bass.ds(g * HPG, HPG), :].rearrange(
                    "(o h) l -> o (h l)", o=1).to_broadcast([P, HPG * SEQ])).then_inc(s["cum_in"], 16)

                def load_state(b):
                    pool.dma_start(stT[:, b % 4, :], a["state_T"][bass.ds(g * NSAMP + b, 1)].rearrange("g p c -> (g p) c"))\
                        .then_inc(s[f"st_in{b % 4}"], 16)

                for b in range(4):
                    load_state(b)
                alone(s["bc_rows"], g + 1)
                pool.dma_start(scr_bc[bass.ds(g * NSAMP, NSAMP), :], bcs[:, :]).then_inc(s["bc_out"], 16)
                for b in range(4, NSAMP):
                    alone(s["st_used"], g * NSAMP + (b - 3))
                    load_state(b)
                alone(s["fst_ready"], g + 1)
                pool.dma_start(o["new_ssd_p"][bass.ds(g, 1)].rearrange("g p c -> (g p) c"), fst[:, :])\
                    .then_inc(s["fst_out"], 16)
                alone(s["st_used"], g * NSAMP + NSAMP)
                alone(s["bc_out"], g * 16 + 16)
                alone(s["fst_out"], g * 16 + 16)
                pool.sem_inc(s["fst_free"], 1)
            pool.wait_ge(s["conv_done"], CT)
            pool.dma_start(o["tails"], flat(tails[:, :, :])).then_inc(s["tails_out"], 16)
            pool.wait_ge(s["pool_f"], KT)
            pool.dma_start(o["utail"], flat(utail[:, :, :])).then_inc(s["outs"], 16)
            pool.wait_ge(s["mix_lo"], 3 * KT)
            for c in range(4):
                if c >= 2:
                    pool.wait_ge(s["mem_lo"], c - 1)
                pool.dma_start(memraw[:, c % 2, :], a["memT"][:, c * 4 * N_MEM:(c + 1) * 4 * N_MEM])\
                    .then_inc(s[f"mem_in{c % 2}"], 16)
            pool.wait_ge(s["ln_sum"], 1)
            pool.wait_ge(s["outs"], 48)
            HALF = 2 * NSAMP * N_MEM
            for half in range(2):
                pool.dma_start(kc[:, 2 * half:2 * half + 2].rearrange("p h b m -> p (h b m)"),
                               a["kc"][:, half * HALF:(half + 1) * HALF]).then_inc(s[f"kc_in{half}"], 16)
            for half in range(2):
                pool.wait_ge(s["ss_ps"], 2 * half + 2)
                pool.dma_start(vc[:, 2 * half:2 * half + 2].rearrange("p h b m d -> p (h b m d)"),
                               a["vc"][:, half * HALF:(half + 1) * HALF]).then_inc(s[f"vc_in{half}"], 16)
            pool.wait_ge(s["kt_ready"], MH)
            pool.dma_start(o["mem_k"], flat(KTm[:, :, :])).then_inc(s["kv_out"], 16)
            pool.wait_ge(s["vn_ready"], 4)
            pool.dma_start(o["mem_v"], flat(Vn[:, :, :])).then_inc(s["kv_out"], 16)
            pool.wait_ge(s["x_lo"], 12)
            def load_pair(r, c):
                pool.dma_start(st[:, c].rearrange("p b i n -> p (b i n)"),
                               a["state_ssd"][bass.ds(r * 2 + c, 1)].rearrange("g p c -> (g p) c"))\
                    .then_inc(s[f"st_in{c}"], 16)
                pool.dma_start(bcb[:, c, :], scr_bc[bass.ds(r * 4 + 2 * c, 2), :].rearrange(
                    "(o b) n -> o (b n)", o=1).to_broadcast([P, 2 * P])).then_inc(s[f"b_in{c}"], 16)

            def store_pair(r, c):
                pool.dma_start(o["new_ssd_s"][bass.ds(r * 2 + c, 1)].rearrange("g p c -> (g p) c"),
                               st[:, c].rearrange("p b i n -> p (b i n)")).then_inc(s[f"st_out{c}"], 16)

            for c in range(2):
                load_pair(0, c)
            with rounds(pool, 15, t, {}) as r:
                for c in range(2):
                    alone(s["st_done"], r * 4 + (2 * c + 2 + START["st_done"]))
                    store_pair(r, c)
                    alone(s[f"st_out{c}"], r * 16 + 16)
                    load_pair(r + 1, c)
            for c in range(2):
                pool.wait_ge(s["st_done"], 15 * 4 + 2 * c + 2 + START["st_done"])
                store_pair(15, c)
            for c in range(4):
                pool.wait_ge(s["xn_ready"], 8 + c + 1)
                pool.dma_start(o["yT"][:, c * 4 * T:(c + 1) * 4 * T], flat(resid[:, 4 * c:4 * c + 4, :]))\
                    .then_inc(s["outs"], 16)
            pool.wait_ge(s["outs"], 16 * 7)
            pool.wait_ge(s["scr_out"], 32)
            pool.wait_ge(s["bc_out"], 16 * GROUPS)
            pool.wait_ge(s["st_out0"], 16 * 16)
            pool.wait_ge(s["st_out1"], 16 * 16)
            pool.wait_ge(s["fst_out"], 16 * GROUPS)
            pool.wait_ge(s["tails_out"], 16)
            pool.wait_ge(s["kv_out"], 32)


def conv_tiles():
    bc = D_INNER // P
    return [t for g in range(GROUPS) for t in (bc + g, bc + GROUPS + g, *range(XPG * g, XPG * g + XPG))]


def feature_major(x):
    n, f = x.shape
    return x.T.reshape(f // P, P, n).transpose(1, 0, 2)


def blocks(w, kts=4):
    K, N = w.shape
    return w.reshape(K // (P * kts), kts, P, N // BLK, BLK).transpose(3, 0, 2, 1, 4).reshape(-1, P, kts * BLK)


def narrow_blocks(w):
    K, N = w.shape
    return w.reshape(K // (P * 8), 8, P, N // P, P).transpose(3, 0, 2, 1, 4).reshape(-1, P, 8 * P)


def interleave(*parts):
    n = parts[0][0]
    out = []
    for i in range(n):
        for m, x in parts:
            k = x.shape[0] // m
            out.append(x[i * k:(i + 1) * k])
    return np.concatenate(out)


def kernel(**inputs):
    import concourse.bacc as bacc
    from concourse.bass_utils import run_bass_kernel_spmd

    x = {n: np.asarray(v) for n, v in inputs.items()}
    w_in = x["w_in"][0]
    cuts = np.cumsum([0, D_MODEL, D_INNER, D_INNER, GROUPS * D_STATE, GROUPS * D_STATE, HEADS, D_MODEL, D_MODEL])
    w_u, w_z, w_x, w_b, w_c, w_dt, w_gp, w_gs = [w_in[:, p:q] for p, q in zip(cuts, cuts[1:])]

    def cols(w, g, n):
        return w[:, g * n:(g + 1) * n]

    def bcx(g):
        return [narrow_blocks(cols(w_b, g, P)), narrow_blocks(cols(w_c, g, P)), blocks(cols(w_x, g, XPG * P))]

    stream = list(bcx(0))
    for g in range(GROUPS):
        stream.append(blocks(cols(w_z, g, XPG * P)))
        if g < GROUPS - 1:
            stream += bcx(g + 1)
    for e in EVENTS:
        stream.append(blocks(cols(w_u, e.tile // 2, BLK)) if e.kind == "in" else blocks(x["w_pool"][0, e.group]))
    stream.append(interleave((8, blocks(w_gp)), (8, blocks(x["w_pool_br"][0]))))
    stream.append(interleave((8, blocks(w_gs)), (8, blocks(x["w_ssd_br"][0]))))
    stream.append(blocks(x["w_out"][0]))
    stream += [blocks(x[n][0]) for n in ("w_mk", "w_mq", "w_mv", "w_mo")]
    stream.append(interleave((FT // 2, blocks(x["w_ffn_gate"][0])), (FT // 2, blocks(x["w_ffn_up"][0]))))
    stream.append(blocks(x["w_ffn_down"][0]))
    tiles = conv_tiles()

    def per_feature(v):
        return v.reshape(-1, P).T

    conv_w = x["conv_w"][0].reshape(CONV_W, CT, P)[:, tiles].transpose(2, 1, 0).reshape(P, CT * CONV_W)
    conv_b = per_feature(x["conv_b"][0])[:, tiles]
    d_skip = np.repeat(x["d_skip"][0], 64).reshape(YT, P).T
    vecs = [conv_w, conv_b, per_feature(x["ssd_norm_w"][0]), d_skip] + [
        per_feature(x[n][0]) for n in ("pool_scale", "ln_mix_g", "ln_mix_b", "ln_mem_g", "ln_mem_b", "ln_ffn_g", "ln_ffn_b")]
    tri = (np.arange(P)[:, None] <= np.arange(P)[None, :]).astype(np.float32)
    counts = np.array([[1.0 / min(w, t + 1) for t in range(16)] for w in WINDOWS], np.float32)
    hist = x["state_conv"][0].reshape(NSAMP, CONV_W - 1, CT, P)[:, :, tiles].transpose(3, 2, 0, 1)
    arrays = {
        "wstream": np.concatenate(stream),
        "wdt": w_dt.reshape(KT, P, HEADS).transpose(1, 0, 2).reshape(P, KT * HEADS),
        "xT": feature_major(np.concatenate([x["x_prompt"][0], x["x_sample"][:, 0]])).reshape(P, KT * T),
        "memT": feature_major(x["mem_prompt"][0]).reshape(P, KT * N_MEM),
        "vecs": np.concatenate(vecs, axis=1),
        "hist": hist.reshape(P, -1),
        "hpool": x["state_pool"][0].reshape(NSAMP, POOL_HIST, KT, P).transpose(3, 2, 0, 1).reshape(P, -1),
        "dt_bias": x["dt_bias"][0][:, None],
        "a_log": x["a_log"][0][:, None],
        "ident": np.eye(P, dtype=np.float32),
        "cmask": np.concatenate([tri, np.ones((P, P), np.float32), tri], axis=1),
        "rc": np.broadcast_to(counts.reshape(1, -1), (P, 64)),
        "state_conv": x["state_conv"][0],
        "state_pool": x["state_pool"][0],
        "state_ssd": x["state_ssd"][0].reshape(4, 2, GROUPS, XPG, P, D_STATE).transpose(2, 0, 4, 1, 3, 5)
                      .reshape(GROUPS * 4, P, UNIT),
        "state_T": x["state_ssd"][0].reshape(NSAMP, GROUPS, XPG * P, D_STATE).transpose(1, 0, 3, 2)
                    .reshape(GROUPS * NSAMP, D_STATE, XPG * P),
        "kc": x["cache_mem_k"][0].transpose(3, 2, 0, 1).reshape(P, -1),
        "vc": x["cache_mem_v"][0].reshape(NSAMP, 2, P, MH, MHD).transpose(2, 3, 0, 1, 4).reshape(P, -1),
    }
    arrays = {n: np.ascontiguousarray(v) for n, v in arrays.items()}
    assert arrays["wstream"].shape == (N_UNITS, P, UNIT), (arrays["wstream"].shape, N_UNITS)
    outs = {
        "yT": (P, KT * T), "new_ssd_p": (GROUPS, P, XPG * P), "tails": (P, CT * 11), "utail": (P, KT * 23),
        "mem_k": (P, MH * N_MEM), "mem_v": (P, 2 * MEM_DIM), "new_ssd_s": (GROUPS * 4, P, UNIT),
        "pass_conv": (NSAMP, CONV_W - 2, CONV_DIM), "pass_pool": (NSAMP, POOL_HIST - 1, D_MODEL),
    }
    nc = bacc.Bacc("TRN2", target_bir_lowering=False, num_devices=1, dynamic_dma_scratch_size=8192)
    ins = {n: nc.dram_tensor(f"in_{n}", v.shape, mybir.dt.from_np(v.dtype), kind="ExternalInput").ap() for n, v in arrays.items()}
    res = {n: nc.dram_tensor(f"out_{n}", v, F32, kind="ExternalOutput").ap() for n, v in outs.items()}
    build(nc, ins, res)
    r = run_bass_kernel_spmd(nc, [{f"in_{n}": v for n, v in arrays.items()}], core_ids=[0]).results[0]
    r = {n: np.asarray(r[f"out_{n}"]) for n in outs}

    y = r["yT"].reshape(P, KT, T).transpose(2, 1, 0).reshape(T, D_MODEL)
    back = np.argsort(tiles)
    tail = r["tails"].reshape(P, CT, 11)[:, back].transpose(2, 1, 0).reshape(11, CONV_DIM)
    utail = r["utail"].reshape(P, KT, 23).transpose(2, 1, 0).reshape(23, D_MODEL)
    new_conv_s = np.concatenate([r["pass_conv"], tail[3:, None]], axis=1)[None]
    new_pool_s = np.concatenate([r["pass_pool"], utail[15:, None]], axis=1)[None]
    new_ssd_p = r["new_ssd_p"].reshape(GROUPS, P, XPG, D_STATE).transpose(0, 2, 1, 3).reshape(1, 1, HEADS, 64, D_STATE)
    new_ssd_s = r["new_ssd_s"].reshape(GROUPS, 4, P, 2, XPG, D_STATE).transpose(1, 3, 0, 4, 2, 5)\
        .reshape(1, NSAMP, HEADS, 64, D_STATE)
    mem_k = r["mem_k"].reshape(P, MH, N_MEM).transpose(2, 1, 0)[None, None]
    mem_v = r["mem_v"].reshape(P, 2, MEM_DIM).transpose(1, 0, 2).reshape(1, 1, N_MEM, MH, MHD)
    return (y[None, :SEQ], y[SEQ:, None], new_ssd_p, tail[None, None, :3], utail[None, None, :15], mem_k, mem_v,
            new_ssd_s, new_conv_s, new_pool_s)
```
